# Optimizing a Trainium2 kernel written in Bass

```python
import math
import jax, jax.numpy as jnp
from jax import lax
import numpy as np
import jax
import jax.numpy as jnp

D_MODEL = 1024
BATCH = 1
SEQ = 512
DEPTH = 2

CHUNK = 64
Q_BLOCK = 128
PLE_DIM = 256
RMS_EPS = 1e-6

SB_HEADS = 8
SB_HEAD_DIM = 64
SB_WIDTH = SB_HEADS * SB_HEAD_DIM

DA_HEADS = 4
DA_HEAD_DIM = 64
DA_V_DIM = 2 * DA_HEAD_DIM
DA_QK_WIDTH = DA_HEADS * 2 * DA_HEAD_DIM
DA_WIDTH = DA_HEADS * DA_V_DIM

ROPE_THETA = 500000.0
ROPE_DIM = DA_HEAD_DIM // 4

N_GROUPS = 4
EXPERTS_PER_GROUP = 8
N_EXPERTS = N_GROUPS * EXPERTS_PER_GROUP
TOP_K = 2
EXPERT_HIDDEN = 256
MOE_BLOCK = 256

IN_SIZES = (SB_WIDTH, SB_WIDTH, SB_WIDTH, DA_QK_WIDTH, DA_QK_WIDTH, DA_WIDTH, D_MODEL, D_MODEL)
IN_WIDTH = sum(IN_SIZES)
IN_OFFSETS = tuple(int(o) for o in np.cumsum(IN_SIZES)[:-1])


def rmsnorm(x, g):
    xf = x.astype(jnp.float32)
    y = xf * lax.rsqrt(jnp.mean(xf * xf, axis=-1, keepdims=True) + RMS_EPS)
    return (y * g.astype(jnp.float32)).astype(x.dtype)

def apply_partial_rope(t, cos, sin):
    half = ROPE_DIM // 2
    r1 = t[..., :half]
    r2 = t[..., half:ROPE_DIM]
    rot = jnp.concatenate([r1 * cos - r2 * sin, r2 * cos + r1 * sin], axis=-1)
    return jnp.concatenate([rot, t[..., ROPE_DIM:]], axis=-1)

def stick_breaking_attention(q, k, v):
    B, H, S, d = q.shape
    scale = d ** -0.5
    key_idx = jnp.arange(S)

    def block(j):
        start = j * Q_BLOCK
        qb = lax.dynamic_slice_in_dim(q, start, Q_BLOCK, axis=2)
        z = jnp.einsum('bhqd,bhkd->bhqk', qb, k, preferred_element_type=jnp.float32) * scale
        q_idx = start + jnp.arange(Q_BLOCK)
        strict = key_idx[None, :] < q_idx[:, None]
        log_stay = jnp.where(strict, jax.nn.log_sigmoid(-z), 0.0)
        between = lax.cumsum(log_stay, axis=3, reverse=True) - log_stay
        w = jnp.where(strict, jnp.exp(jax.nn.log_sigmoid(z) + between), 0.0)
        return jnp.einsum('bhqk,bhkd->bhqd', w.astype(v.dtype), v)

    out = lax.map(block, jnp.arange(S // Q_BLOCK))
    return out.transpose(1, 0, 3, 2, 4).reshape(B, S, H, d)

def differential_attention(q, k, v, lam):
    B, H, _, S, d = q.shape
    dv = v.shape[-1]
    scale = d ** -0.5
    key_chunk = jnp.arange(S) // CHUNK
    neg = jnp.finfo(jnp.float32).min

    def block(j):
        start = j * Q_BLOCK
        qb = lax.dynamic_slice_in_dim(q, start, Q_BLOCK, axis=3)
        s = jnp.einsum('bhmqd,bhmkd->bhmqk', qb, k, preferred_element_type=jnp.float32) * scale
        q_chunk = (start + jnp.arange(Q_BLOCK)) // CHUNK
        allowed = key_chunk[None, :] <= q_chunk[:, None]
        a = jax.nn.softmax(jnp.where(allowed, s, neg), axis=-1)
        a = a[:, :, 0] - lam * a[:, :, 1]
        return jnp.einsum('bhqk,bhkd->bhqd', a.astype(v.dtype), v)

    out = lax.map(block, jnp.arange(S // Q_BLOCK))
    return out.transpose(1, 0, 3, 2, 4).reshape(B, S, H, dv)

def hierarchical_moe(h, w_rg, b_rg, w_re, b_re, w_gate, w_up, w_down):
    B, S, D = h.shape
    N = B * S
    t = h.reshape(N, D)
    rows = jnp.arange(N)
    g_logits = (t @ w_rg).astype(jnp.float32) + b_rg.astype(jnp.float32)
    g_prob = jax.nn.softmax(g_logits, axis=-1)
    g_sel = jnp.argmax(g_logits, axis=-1)
    g_p = g_prob[rows, g_sel]
    e_logits = ((t @ w_re).astype(jnp.float32) + b_re.astype(jnp.float32)).reshape(N, N_GROUPS, EXPERTS_PER_GROUP)
    e_prob = jax.nn.softmax(e_logits[rows, g_sel], axis=-1)
    top_p, top_i = lax.top_k(e_prob, TOP_K)
    gates = g_p[:, None] * top_p / jnp.sum(top_p, axis=-1, keepdims=True)

    expert_id = (g_sel[:, None] * EXPERTS_PER_GROUP + top_i).reshape(-1)
    token_id = jnp.repeat(rows, TOP_K)
    gate_flat = gates.reshape(-1)
    A = N * TOP_K

    order = jnp.argsort(expert_id)
    se, st, sg = expert_id[order], token_id[order], gate_flat[order]
    counts = jnp.zeros((N_EXPERTS,), jnp.int32).at[expert_id].add(1)
    pcounts = (counts + MOE_BLOCK - 1) // MOE_BLOCK * MOE_BLOCK
    starts = jnp.cumsum(counts) - counts
    pends = jnp.cumsum(pcounts)
    pstarts = pends - pcounts
    dest = pstarts[se] + jnp.arange(A) - starts[se]
    P = ((A + MOE_BLOCK - 1) // MOE_BLOCK) * MOE_BLOCK + N_EXPERTS * MOE_BLOCK
    n_blk = P // MOE_BLOCK
    slot_tok = jnp.full((P,), N, jnp.int32).at[dest].set(st)
    slot_gate = jnp.zeros((P,), jnp.float32).at[dest].set(sg)
    blk_e = jnp.minimum(jnp.searchsorted(pends, jnp.arange(n_blk) * MOE_BLOCK, side='right'), N_EXPERTS - 1)
    xs = jnp.concatenate([t, jnp.zeros((1, D), t.dtype)], axis=0)[slot_tok].reshape(n_blk, MOE_BLOCK, D)

    def expert_block(args):
        xb, e = args
        hid = jax.nn.silu(xb @ w_gate[e]) * (xb @ w_up[e])
        return hid @ w_down[e]

    ys = lax.map(expert_block, (xs, blk_e)).reshape(P, D)
    ys = ys * slot_gate[:, None].astype(ys.dtype)
    out = jax.ops.segment_sum(ys, slot_tok, num_segments=N + 1)[:N]
    return out.reshape(B, S, D)

def first_inputs(seed: int = 0) -> dict:
    key = jax.random.key(seed)
    ks = jax.random.split(key, 26)
    D = D_MODEL

    def nrm(k, shape, scale):
        return jax.random.normal(k, shape, jnp.float32) * scale

    def gain(k, shape):
        return 1.0 + 0.02 * jax.random.normal(k, shape, jnp.float32)

    offset = jax.random.randint(ks[2], (BATCH, 1), 0, 4096, dtype=jnp.int32)
    positions = (offset + jnp.arange(SEQ, dtype=jnp.int32)[None, :]).astype(jnp.int32)
    return {
        "x": nrm(ks[0], (BATCH, SEQ, D), 1.0),
        "p": nrm(ks[1], (DEPTH, BATCH, SEQ, PLE_DIM), 1.0),
        "positions": positions,
        "g_mix": gain(ks[3], (DEPTH, D)),
        "w_in": nrm(ks[4], (DEPTH, D, IN_WIDTH), D ** -0.5),
        "lam_q1": nrm(ks[5], (DEPTH, DA_HEAD_DIM), 0.1),
        "lam_k1": nrm(ks[6], (DEPTH, DA_HEAD_DIM), 0.1),
        "lam_q2": nrm(ks[7], (DEPTH, DA_HEAD_DIM), 0.1),
        "lam_k2": nrm(ks[8], (DEPTH, DA_HEAD_DIM), 0.1),
        "g_subln": gain(ks[9], (DEPTH, DA_V_DIM)),
        "w_br_a": nrm(ks[10], (DEPTH, SB_WIDTH, D), SB_WIDTH ** -0.5),
        "w_br_b": nrm(ks[11], (DEPTH, DA_WIDTH, D), DA_WIDTH ** -0.5),
        "w_o": nrm(ks[12], (DEPTH, D, D), D ** -0.5),
        "g_ffn": gain(ks[13], (DEPTH, D)),
        "w_router_group": nrm(ks[14], (DEPTH, D, N_GROUPS), D ** -0.5),
        "b_router_group": nrm(ks[15], (DEPTH, N_GROUPS), 0.01),
        "w_router_expert": nrm(ks[16], (DEPTH, D, N_EXPERTS), D ** -0.5),
        "b_router_expert": nrm(ks[17], (DEPTH, N_EXPERTS), 0.01),
        "w_exp_gate": nrm(ks[18], (DEPTH, N_EXPERTS, D, EXPERT_HIDDEN), D ** -0.5),
        "w_exp_up": nrm(ks[19], (DEPTH, N_EXPERTS, D, EXPERT_HIDDEN), D ** -0.5),
        "w_exp_down": nrm(ks[20], (DEPTH, N_EXPERTS, EXPERT_HIDDEN, D), EXPERT_HIDDEN ** -0.5),
        "g_ple": gain(ks[21], (DEPTH, D)),
        "w_ple": nrm(ks[22], (DEPTH, PLE_DIM, D), PLE_DIM ** -0.5),
        "w_ple_gate": nrm(ks[23], (DEPTH, D, D), D ** -0.5),
        "g_final": gain(ks[24], (D,)),
    }

def first_block(x, p, positions, g_mix, w_in, lam_q1, lam_k1, lam_q2, lam_k2, g_subln,
              w_br_a, w_br_b, w_o, g_ffn, w_router_group, b_router_group,
              w_router_expert, b_router_expert, w_exp_gate, w_exp_up, w_exp_down,
              g_ple, w_ple, w_ple_gate, g_final):
    B, S, D = x.shape
    inv_freq = ROPE_THETA ** (-jnp.arange(0, ROPE_DIM, 2, dtype=jnp.float32) / ROPE_DIM)
    ang = positions.astype(jnp.float32)[..., None] * inv_freq
    cos = jnp.cos(ang)[:, :, None, None, :].astype(x.dtype)
    sin = jnp.sin(ang)[:, :, None, None, :].astype(x.dtype)

    for i in range(DEPTH):
        lam_init = 0.8 - 0.6 * math.exp(-0.3 * i)
        h = rmsnorm(x, g_mix[i])
        u = h @ w_in[i]
        sb_q, sb_k, sb_v, da_q, da_k, da_v, gate_a, gate_b = jnp.split(u, IN_OFFSETS, axis=-1)

        to_heads = lambda t: t.reshape(B, S, SB_HEADS, SB_HEAD_DIM).transpose(0, 2, 1, 3)
        y_a = stick_breaking_attention(to_heads(sb_q), to_heads(sb_k), to_heads(sb_v))
        y_a = y_a.reshape(B, S, SB_WIDTH) @ w_br_a[i]

        dq = apply_partial_rope(da_q.reshape(B, S, DA_HEADS, 2, DA_HEAD_DIM), cos, sin)
        dk = apply_partial_rope(da_k.reshape(B, S, DA_HEADS, 2, DA_HEAD_DIM), cos, sin)
        dq = dq.transpose(0, 2, 3, 1, 4)
        dk = dk.transpose(0, 2, 3, 1, 4)
        dv = da_v.reshape(B, S, DA_HEADS, DA_V_DIM).transpose(0, 2, 1, 3)
        lam = (jnp.exp(jnp.sum(lam_q1[i].astype(jnp.float32) * lam_k1[i].astype(jnp.float32)))
               - jnp.exp(jnp.sum(lam_q2[i].astype(jnp.float32) * lam_k2[i].astype(jnp.float32)))
               + lam_init)
        y_b = differential_attention(dq, dk, dv, lam)
        y_b = rmsnorm(y_b, g_subln[i]) * (1.0 - lam_init)
        y_b = y_b.reshape(B, S, DA_WIDTH) @ w_br_b[i]

        merged = jax.nn.sigmoid(gate_a) * y_a + jax.nn.sigmoid(gate_b) * y_b
        x = x + merged @ w_o[i]

        x = x + hierarchical_moe(rmsnorm(x, g_ffn[i]), w_router_group[i], b_router_group[i],
                                 w_router_expert[i], b_router_expert[i],
                                 w_exp_gate[i], w_exp_up[i], w_exp_down[i])

        ple_gate = jax.nn.sigmoid(rmsnorm(x, g_ple[i]) @ w_ple_gate[i])
        x = x + (p[i] @ w_ple[i]) * ple_gate

    return rmsnorm(x, g_final)


DEPTH_2 = 1

HEAD_DIM = 64
SCALE = HEAD_DIM ** -0.5
NEG_INF = -1e30
EPS = 1e-6
A_GROUPS = ((128, 1), (512, 4), (2048, 16))
A_HEADS_PER_GROUP = 4
A_HEADS = A_HEADS_PER_GROUP * len(A_GROUPS)
A_WIDTH = A_HEADS * HEAD_DIM
A_OUT = A_HEADS_PER_GROUP * HEAD_DIM
A_BLOCK = max(w // d for w, d in A_GROUPS)
LRU_WIDTH = D_MODEL // 2
LRU_BLOCKS = 8
LRU_BLOCK_DIM = LRU_WIDTH // LRU_BLOCKS
CONV_WIDTH = 4
LRU_C = 8.0
C_HEADS = 8
C_WIDTH = C_HEADS * HEAD_DIM
MOBA_BLOCK = 256
MOBA_TOPK = 3
MOBA_Q_CHUNK = 32
REL_BUCKETS = 32
REL_MAX_DIST = 2048
REL_HEADS = A_HEADS + C_HEADS
FFN_HIDDEN = -(-8 * D_MODEL // (3 * 256)) * 256
IN_SIZES_2 = (A_WIDTH, A_WIDTH, A_WIDTH, LRU_WIDTH, LRU_WIDTH, C_WIDTH, C_WIDTH, C_WIDTH, 3 * D_MODEL)
IN_COLS = sum(IN_SIZES_2)


def rms_norm(x, g):
    xf = x.astype(jnp.float32)
    y = xf * lax.rsqrt(jnp.mean(xf * xf, axis=-1, keepdims=True) + EPS)
    return (y * g.astype(jnp.float32)).astype(x.dtype)

def rel_bucket(dist):
    max_exact = REL_BUCKETS // 2
    d = jnp.maximum(dist, 0)
    df = jnp.maximum(d, 1).astype(jnp.float32)
    large = max_exact + (jnp.log(df / max_exact) / math.log(REL_MAX_DIST / max_exact)
                         * (REL_BUCKETS - max_exact)).astype(jnp.int32)
    large = jnp.minimum(large, REL_BUCKETS - 1)
    return jnp.where(d < max_exact, d, large)

def dilated_window_attention(q, k, v, dilation, n_back, bias_tab):
    B, S, H, E = q.shape
    L = S // dilation
    nb = -(-L // A_BLOCK)
    Lp = nb * A_BLOCK

    def to_sub(t):
        t = t.reshape(B, L, dilation, H, E).transpose(0, 2, 3, 1, 4)
        t = jnp.pad(t, ((0, 0), (0, 0), (0, 0), (0, Lp - L), (0, 0)))
        return t.reshape(B, dilation, H, nb, A_BLOCK, E)

    qb, kb, vb = to_sub(q), to_sub(k), to_sub(v)

    def with_prev(t):
        prev = jnp.pad(t, ((0, 0), (0, 0), (0, 0), (1, 0), (0, 0), (0, 0)))[:, :, :, :nb]
        return jnp.concatenate([prev, t], axis=4)

    kk, vv = with_prev(kb), with_prev(vb)
    qi = jnp.arange(A_BLOCK)[:, None] + A_BLOCK
    kj = jnp.arange(2 * A_BLOCK)[None, :]
    delta = qi - kj
    band = (delta >= 0) & (delta <= n_back)
    has_prev = (jnp.arange(nb)[:, None, None] > 0) | (kj >= A_BLOCK)[None]
    valid = band[None] & has_prev
    bias = bias_tab.astype(jnp.float32)[rel_bucket(delta * dilation)]
    bias = jnp.transpose(bias, (2, 0, 1))
    logits = jnp.einsum('bdhnqe,bdhnke->bdhnqk', qb, kk).astype(jnp.float32) * SCALE
    logits = logits + bias[None, None, :, None]
    logits = jnp.where(valid[None, None, None], logits, NEG_INF)
    m = jnp.max(logits, axis=-1, keepdims=True)
    p = jnp.exp(logits - m)
    den = jnp.sum(p, axis=-1, keepdims=True)
    o = jnp.einsum('bdhnqk,bdhnke->bdhnqe', p, vv.astype(jnp.float32)) / den
    lse = (m + jnp.log(den))[..., 0]
    o = o.reshape(B, dilation, H, Lp, E)[:, :, :, :L].transpose(0, 3, 1, 2, 4).reshape(B, S, H, E)
    lse = lse.reshape(B, dilation, H, Lp)[:, :, :, :L].transpose(0, 3, 1, 2).reshape(B, S, H)
    return o, lse

def rg_lru_branch(xb, gb, conv_w, conv_b, w_a, b_a, w_x, b_x, lam):
    B, S, W = xb.shape
    xp = jnp.pad(xb, ((0, 0), (CONV_WIDTH - 1, 0), (0, 0)))
    xc = conv_b
    for i in range(CONV_WIDTH):
        xc = xc + xp[:, i:i + S] * conv_w[i]
    xr = xc.reshape(B, S, LRU_BLOCKS, LRU_BLOCK_DIM)
    r = jax.nn.sigmoid((jnp.einsum('bsnd,nde->bsne', xr, w_a).reshape(B, S, W) + b_a).astype(jnp.float32))
    ig = jax.nn.sigmoid((jnp.einsum('bsnd,nde->bsne', xr, w_x).reshape(B, S, W) + b_x).astype(jnp.float32))
    log_a = -LRU_C * r * jax.nn.softplus(-lam.astype(jnp.float32))
    a = jnp.exp(log_a)
    bterm = jnp.sqrt(-jnp.expm1(2.0 * log_a)) * (ig * xc.astype(jnp.float32))

    def combine(left, right):
        a1, b1 = left
        a2, b2 = right
        return a1 * a2, a2 * b1 + b2

    _, h = lax.associative_scan(combine, (a, bterm), axis=1)
    return (h * jax.nn.gelu(gb.astype(jnp.float32))).astype(xb.dtype)

def moba_attention(q, k, v, bias_tab):
    B, S, H, E = q.shape
    f32 = jnp.float32
    nblk = -(-S // MOBA_BLOCK)
    Sp = nblk * MOBA_BLOCK
    pad = ((0, 0), (0, 0), (0, Sp - S), (0, 0))
    qh = q.transpose(0, 2, 1, 3)
    qb = jnp.pad(qh, pad).reshape(B, H, nblk, MOBA_BLOCK, E)
    kb = jnp.pad(k.transpose(0, 2, 1, 3), pad).reshape(B, H, nblk, MOBA_BLOCK, E)
    vb = jnp.pad(v.transpose(0, 2, 1, 3), pad).reshape(B, H, nblk, MOBA_BLOCK, E)
    tab = bias_tab.astype(f32)
    off = jnp.arange(MOBA_BLOCK)
    delta = off[:, None] - off[None, :]
    bias_own = jnp.transpose(tab[rel_bucket(delta)], (2, 0, 1))
    lg = jnp.einsum('bhnqe,bhnke->bhnqk', qb, kb).astype(f32) * SCALE + bias_own[None, :, None]
    lg = jnp.where(delta >= 0, lg, NEG_INF)
    m_own = jnp.max(lg, axis=-1)
    p = jnp.exp(lg - m_own[..., None])
    den_own = jnp.sum(p, axis=-1).reshape(B, H, Sp)[:, :, :S]
    num_own = jnp.einsum('bhnqk,bhnke->bhnqe', p, vb.astype(f32)).reshape(B, H, Sp, E)[:, :, :S]
    m_own = m_own.reshape(B, H, Sp)[:, :, :S]
    n_sel = min(MOBA_TOPK, nblk - 1)
    if n_sel == 0:
        out = num_own / den_own[..., None]
    else:
        kmean = jnp.mean(kb.astype(f32), axis=3)
        qpos = jnp.arange(S)
        qblk = qpos // MOBA_BLOCK
        gate = jnp.einsum('bhse,bhne->bhsn', qh.astype(f32), kmean)
        gate = jnp.where(jnp.arange(nblk)[None, :] < qblk[:, None], gate, NEG_INF)
        _, idx = lax.top_k(gate, n_sel)
        base = (jnp.arange(B)[:, None] * H + jnp.arange(H)[None, :]) * nblk
        fidx = idx + base[:, :, None, None]
        kflat = kb.reshape(B * H * nblk, MOBA_BLOCK, E)
        vflat = vb.reshape(B * H * nblk, MOBA_BLOCK, E)
        head = jnp.arange(H)[None, :, None, None, None]
        tab_t = tab.T
        nq = S // MOBA_Q_CHUNK

        def chunks(t):
            return jnp.moveaxis(t.reshape(B, H, nq, MOBA_Q_CHUNK, *t.shape[3:]), 2, 0)

        def step(args):
            qc, fi, bi, qp, m_o, d_o, n_o = args
            ks = jnp.take(kflat, fi, axis=0)
            vs = jnp.take(vflat, fi, axis=0)
            lgs = jnp.einsum('bhqe,bhqnke->bhqnk', qc, ks).astype(f32) * SCALE
            kpos = bi[..., None] * MOBA_BLOCK + jnp.arange(MOBA_BLOCK)
            lgs = lgs + tab_t[head, rel_bucket(qp[:, None, None] - kpos)]
            ok = bi < (qp // MOBA_BLOCK)[:, None]
            lgs = jnp.where(ok[..., None], lgs, NEG_INF)
            mm = jnp.maximum(jnp.max(lgs, axis=(-2, -1)), m_o)
            ps = jnp.exp(lgs - mm[..., None, None])
            c_o = jnp.exp(m_o - mm)
            den = d_o * c_o + jnp.sum(ps, axis=(-2, -1))
            num = n_o * c_o[..., None] + jnp.einsum('bhqnk,bhqnke->bhqe', ps, vs.astype(f32))
            return num / den[..., None]

        out = lax.map(step, (chunks(qh), chunks(fidx), chunks(idx), qpos.reshape(nq, MOBA_Q_CHUNK),
                             chunks(m_own), chunks(den_own), chunks(num_own)))
        out = jnp.moveaxis(out, 0, 2).reshape(B, H, S, E)
    return out.transpose(0, 2, 1, 3)

def hybrid_layer(x, rel_bias, g_mix, w_in, conv_w, conv_b, lru_wa, lru_ba, lru_wx, lru_bx, lru_lam,
                 p_a, p_b, p_c, w_out, g_ffn, w_gu, w_down):
    B, S, D = x.shape
    h = rms_norm(x, g_mix)
    z = h @ w_in
    offs = np.cumsum(IN_SIZES_2)[:-1].tolist()
    qa, ka, va, xb, gb, qc, kc, vc, gates = jnp.split(z, offs, axis=-1)
    qa = qa.reshape(B, S, A_HEADS, HEAD_DIM)
    ka = ka.reshape(B, S, A_HEADS, HEAD_DIM)
    va = va.reshape(B, S, A_HEADS, HEAD_DIM)
    outs, lses = [], []
    for g, (window, dilation) in enumerate(A_GROUPS):
        sl = slice(g * A_HEADS_PER_GROUP, (g + 1) * A_HEADS_PER_GROUP)
        o, lse = dilated_window_attention(qa[:, :, sl], ka[:, :, sl], va[:, :, sl],
                                          dilation, window // dilation, rel_bias[:, sl])
        outs.append(o)
        lses.append(lse)
    wts = jax.nn.softmax(jnp.stack(lses, axis=0), axis=0)
    o_a = jnp.sum(wts[..., None] * jnp.stack(outs, axis=0), axis=0).reshape(B, S, A_OUT).astype(x.dtype)
    o_b = rg_lru_branch(xb, gb, conv_w, conv_b, lru_wa, lru_ba, lru_wx, lru_bx, lru_lam)
    o_c = moba_attention(qc.reshape(B, S, C_HEADS, HEAD_DIM), kc.reshape(B, S, C_HEADS, HEAD_DIM),
                         vc.reshape(B, S, C_HEADS, HEAD_DIM), rel_bias[:, A_HEADS:])
    o_c = o_c.reshape(B, S, C_WIDTH).astype(x.dtype)
    gt = jax.nn.sigmoid(gates.astype(jnp.float32)).astype(x.dtype).reshape(B, S, 3, D)
    merged = gt[:, :, 0] * (o_a @ p_a) + gt[:, :, 1] * (o_b @ p_b) + gt[:, :, 2] * (o_c @ p_c)
    x = x + merged @ w_out
    u = rms_norm(x, g_ffn) @ w_gu
    gate, up = jnp.split(u, 2, axis=-1)
    return x + (jax.nn.silu(gate) * up) @ w_down

def second_inputs(seed: int = 0) -> dict:
    key = jax.random.key(seed)
    ks = jax.random.split(key, 24)
    f32 = jnp.float32

    def nrm(k, shape, scale):
        return jax.random.normal(k, shape, f32) * scale

    u = jax.random.uniform(ks[11], (DEPTH_2, LRU_WIDTH), f32, 0.9, 0.999)
    a = u ** (1.0 / LRU_C)
    return {
        "x": nrm(ks[0], (BATCH, SEQ, D_MODEL), 1.0),
        "rel_bias": nrm(ks[1], (REL_BUCKETS, REL_HEADS), 0.5),
        "g_mix": 1.0 + nrm(ks[2], (DEPTH_2, D_MODEL), 0.05),
        "w_in": nrm(ks[3], (DEPTH_2, D_MODEL, IN_COLS), D_MODEL ** -0.5),
        "conv_w": nrm(ks[4], (DEPTH_2, CONV_WIDTH, LRU_WIDTH), CONV_WIDTH ** -0.5),
        "conv_b": nrm(ks[5], (DEPTH_2, LRU_WIDTH), 0.02),
        "lru_wa": nrm(ks[6], (DEPTH_2, LRU_BLOCKS, LRU_BLOCK_DIM, LRU_BLOCK_DIM), LRU_BLOCK_DIM ** -0.5),
        "lru_ba": nrm(ks[7], (DEPTH_2, LRU_WIDTH), 0.02),
        "lru_wx": nrm(ks[8], (DEPTH_2, LRU_BLOCKS, LRU_BLOCK_DIM, LRU_BLOCK_DIM), LRU_BLOCK_DIM ** -0.5),
        "lru_bx": nrm(ks[9], (DEPTH_2, LRU_WIDTH), 0.02),
        "lru_lam": jnp.log(a) - jnp.log1p(-a),
        "p_a": nrm(ks[12], (DEPTH_2, A_OUT, D_MODEL), A_OUT ** -0.5),
        "p_b": nrm(ks[13], (DEPTH_2, LRU_WIDTH, D_MODEL), LRU_WIDTH ** -0.5),
        "p_c": nrm(ks[14], (DEPTH_2, C_WIDTH, D_MODEL), C_WIDTH ** -0.5),
        "w_out": nrm(ks[15], (DEPTH_2, D_MODEL, D_MODEL), D_MODEL ** -0.5),
        "g_ffn": 1.0 + nrm(ks[16], (DEPTH_2, D_MODEL), 0.05),
        "w_gu": nrm(ks[17], (DEPTH_2, D_MODEL, 2 * FFN_HIDDEN), D_MODEL ** -0.5),
        "w_down": nrm(ks[18], (DEPTH_2, FFN_HIDDEN, D_MODEL), FFN_HIDDEN ** -0.5),
        "g_final": 1.0 + nrm(ks[19], (D_MODEL,), 0.05),
    }

def second_block(x, rel_bias, g_mix, w_in, conv_w, conv_b, lru_wa, lru_ba, lru_wx, lru_bx, lru_lam,
              p_a, p_b, p_c, w_out, g_ffn, w_gu, w_down, g_final):
    for l in range(DEPTH_2):
        x = hybrid_layer(x, rel_bias, g_mix[l], w_in[l], conv_w[l], conv_b[l], lru_wa[l], lru_ba[l],
                         lru_wx[l], lru_bx[l], lru_lam[l], p_a[l], p_b[l], p_c[l], w_out[l],
                         g_ffn[l], w_gu[l], w_down[l])
    return rms_norm(x, g_final)


def setup_inputs(seed=0):
    out = dict(first_inputs(seed))
    for name, value in second_inputs(seed + 1).items():
        if name != "x":
            out[name + "_2"] = value
    return out


def reference(
    x, p, positions, g_mix, w_in, lam_q1, lam_k1, lam_q2, lam_k2, g_subln, w_br_a, w_br_b, w_o,
    g_ffn, w_router_group, b_router_group, w_router_expert, b_router_expert, w_exp_gate,
    w_exp_up, w_exp_down, g_ple, w_ple, w_ple_gate, g_final, rel_bias_2, g_mix_2, w_in_2,
    conv_w_2, conv_b_2, lru_wa_2, lru_ba_2, lru_wx_2, lru_bx_2, lru_lam_2, p_a_2, p_b_2, p_c_2,
    w_out_2, g_ffn_2, w_gu_2, w_down_2, g_final_2,
):
    x = first_block(
        x, p, positions, g_mix, w_in, lam_q1, lam_k1, lam_q2, lam_k2, g_subln, w_br_a, w_br_b,
        w_o, g_ffn, w_router_group, b_router_group, w_router_expert, b_router_expert,
        w_exp_gate, w_exp_up, w_exp_down, g_ple, w_ple, w_ple_gate, g_final,
    )
    return second_block(
        x, rel_bias_2, g_mix_2, w_in_2, conv_w_2, conv_b_2, lru_wa_2, lru_ba_2, lru_wx_2,
        lru_bx_2, lru_lam_2, p_a_2, p_b_2, p_c_2, w_out_2, g_ffn_2, w_gu_2, w_down_2, g_final_2,
    )


_drawn_inputs = setup_inputs


def setup_inputs(seed=0):
    import zlib

    import numpy as np

    out = dict(_drawn_inputs(seed))
    spreads = {}
    factors = {'b_router_group': 3.354,
     'g_ple': 14.838,
     'lru_ba_2': 42.466,
     'lru_bx_2': 8.0,
     'b_router_expert': 2.726}
    for name, (base, spread) in spreads.items():
        noise = np.random.default_rng([zlib.crc32(name.encode()), seed]).standard_normal(out[name].shape)
        drawn = base * np.exp(spread * noise) if base else spread * noise
        out[name] = jnp.asarray(drawn.astype(out[name].dtype))
    for name, factor in factors.items():
        out[name] = (out[name] * factor).astype(out[name].dtype)
    return out
```

```python
from contextlib import ExitStack
import math

import numpy as np
import concourse.bass as bass
from concourse import mybir

F32 = mybir.dt.float32
I32 = mybir.dt.int32
U32 = mybir.dt.uint32
ALU = mybir.AluOpType
ACT = mybir.ActivationFunctionType
AX = mybir.AxisListType

P = 128
D = 1024
S = 512
NT = S // P
DC = D // P
DEPTH = 2
EPS = 1e-6
NEG = -1e30
HD = 64
SCALE = HD ** -0.5
RING = 18432


class Core:

    def __init__(self, nc, ctx):
        def sb(name, shape, dt=F32):
            return ctx.enter_context(nc.sbuf_tensor(name, shape, dt))

        self.nc = nc
        self.used_sems = set()
        self.ps = ctx.enter_context(nc.psum_tensor("banks", [P, 8, 512], F32))
        self.x = sb("x_tokens", [P, NT, D])
        self.hT = sb("h_transposed", [P, DC, S])
        self.ring = sb("weight_ring", [P, RING])
        self.ident = sb("identity", [P, P])
        self.neg_tri = sb("neg_tri", [P, P])
        self.neg_ones = sb("neg_ones", [P, P])
        self.strict_bias = sb("strict_bias", [P, P])
        self.chunk_bias = sb("chunk_bias", [P, P])
        self.rope_swap = sb("rope_swap", [P, P])

    def slot(self, offset, chunks, cols):
        return self.ring[:, offset:offset + chunks * cols].rearrange("p (c n) -> p c n", c=chunks)


def sems(k, ctx, names):
    found = [ctx.enter_context(k.nc.semaphore(n)) for n in names.split()]
    assert not k.used_sems & {x.num for x in found}
    k.used_sems |= {x.num for x in found}
    return found


def clear_sems(k):
    k.nc.gpsimd.dma_reset()
    for num in sorted(k.used_sems):
        k.nc.gpsimd.sem_clear(range(num, num + 1))
    k.used_sems = set()
    k.nc.all_engine_barrier()


def rows_pc(w):
    return w.rearrange("(p c) n -> p c n", c=DC)



def load_start(k, t):
    nc = k.nc
    with ExitStack() as ctx:
        (landed,) = sems(k, ctx, "start_landed")
        block = ctx.enter_context(nc.Block())

        @block.sync
        def _(sp):
            sp.dma_start(k.ident[:], t["c_ident"]).then_inc(landed, 16)
            sp.dma_start(k.neg_tri[:], t["c_neg_tri"]).then_inc(landed, 16)
            sp.dma_start(k.x[:], t["x"].rearrange("b (t p) d -> p (b t) d", p=P)).then_inc(landed, 16)
            sp.dma_start(k.strict_bias[:], t["c_strict_bias"]).then_inc(landed, 16)
            sp.dma_start(k.chunk_bias[:], t["c_chunk_bias"]).then_inc(landed, 16)
            sp.dma_start(k.rope_swap[:], t["c_rope_swap"]).then_inc(landed, 16)
            sp.wait_ge(landed, 96)

        @block.vector
        def _(dve):
            nc.vector.memset(k.neg_ones[:], -1.0)



def norm_transpose(k, tag, gain, rows=None):
    nc = k.nc
    with ExitStack() as ctx:
        xn = ctx.enter_context(nc.sbuf_tensor(tag + "_xn", [P, NT, D], F32))
        ss = ctx.enter_context(nc.sbuf_tensor(tag + "_ss", [P, NT], F32))
        g = ctx.enter_context(nc.sbuf_tensor(tag + "_g", [P, DC], F32))
        gain_landed, squares, mean_ready, root_ready, rstd_ready, xn_act, xn_dve, turned, stored = sems(k, ctx, " ".join(tag + s for s in
                              "_gain _squares _mean _root _rstd _xn_act _xn_dve _turned _stored".split()))
        block = ctx.enter_context(nc.Block())

        @block.sync
        def _(sp):
            sp.dma_start(g[:], gain.rearrange("(p c) -> p c", c=DC)).then_inc(gain_landed, 16)
            if rows is not None:
                sp.wait_ge(xn_act, 2)
                sp.wait_ge(xn_dve, 2)
                sp.dma_start(rows.rearrange("(t p) d -> p t d", p=P), xn[:]).then_inc(stored, 16)
                sp.wait_ge(stored, 16)

        @block.scalar
        def _(act):
            for t in range(NT):
                nc.scalar.activation(k.ps[:, 2 * t:2 * t + 2, :], k.x[:, t, :].rearrange("p (a n) -> p a n", a=2),
                                     ACT.Square, accum_out=ss[:, t:t + 1]).then_inc(squares, 1)
            act.wait_ge(mean_ready, 1)
            nc.scalar.activation(ss[:], ss[:], ACT.Sqrt).then_inc(root_ready, 1)
            act.wait_ge(rstd_ready, 1)
            for t in (0, 1):
                nc.scalar.activation(xn[:, t, :], k.x[:, t, :], ACT.Copy, scale=ss[:, t:t + 1]).then_inc(xn_act, 1)

        @block.vector
        def _(dve):
            dve.wait_ge(squares, NT)
            nc.vector.tensor_scalar(ss[:], ss[:], 1.0 / D, EPS, ALU.mult, ALU.add).then_inc(mean_ready, 1)
            dve.wait_ge(root_ready, 1)
            nc.vector.reciprocal(ss[:], ss[:]).then_inc(rstd_ready, 1)
            dve.wait_ge(rstd_ready, 1)
            for t in (2, 3):
                nc.vector.tensor_scalar(xn[:, t, :], k.x[:, t, :], ss[:, t:t + 1], None, ALU.mult).then_inc(xn_dve, 1)
            dve.wait_ge(gain_landed, 16)
            for c in range(DC):
                dve.wait_ge(turned, c + 1)
                nc.vector.tensor_scalar(k.hT[:, c, :], k.ps[:, c, :], g[:, c:c + 1], None, ALU.mult)

        @block.tensor
        def _(pe):
            pe.wait_ge(xn_act, 2)
            pe.wait_ge(xn_dve, 2)
            for c in range(DC):
                for t in range(NT):
                    last = nc.tensor.transpose(k.ps[:, c, t * P:(t + 1) * P], xn[:, t, c::DC], k.ident[:])
                last.then_inc(turned, 1)



def project_pair(nc, k, hT, wq, wk, wv, banks, done):
    for w, bank in ((wq, banks[0]), (wk, banks[1])):
        for c in range(DC):
            last = nc.tensor.matmul(k.ps[:, bank, :], w[:, c, :], hT[:, c, :], start=(c == 0), stop=(c == DC - 1))
        last.then_inc(done, 1)
    for t in range(NT):
        for c in range(DC):
            last = nc.tensor.matmul(k.ps[:, banks[2], t * P:(t + 1) * P], hT[:, c, t * P:(t + 1) * P], wv[:, c, :],
                                    start=(c == 0), stop=(c == DC - 1))
    last.then_inc(done, 1)


def stick_breaking(k, w_in, off_q, off_k, off_v, yT):
    nc = k.nc
    pairs = 4
    order = [(h, j) for h in (0, 1) for j in (3, 2, 1, 0)]
    bank = [0, 1, 2, 3, 4, 5, 6, 0]
    cols = [S - P * j for _, j in order]
    w = rows_pc(w_in)
    slots = [[k.slot((2 * s + b) * DC * P, DC, P) for s in range(3)] for b in range(1)]
    wq, wk, wv = slots[0]
    with ExitStack() as ctx:
        def sb(name, shape):
            return ctx.enter_context(nc.sbuf_tensor("sb_" + name, shape, F32))

        qT, kT, v = sb("qT", [P, S]), sb("kT", [P, S]), sb("v", [P, NT, P])
        mag = sb("mag", [P, 2, S])
        stay = sb("stay", [P, 8, S])
        prob = sb("prob", [P, 8, S])
        (q_landed, k_landed, v_landed, projected, q_ready, kv_ready, z_done, mag_done, exp_neg, ln_done,
         stay_done, logit_done, exp_done, pv_done, y_out) = sems(k, ctx, "sb_q_landed sb_k_landed sb_v_landed sb_projected sb_q_ready sb_kv_ready sb_z_done "
            "sb_mag_done sb_exp_neg sb_ln_done sb_stay_done sb_logit_done sb_exp_done "
            "sb_pv_done sb_y_out")
        block = ctx.enter_context(nc.Block())

        @block.sync
        def _(sp):
            loads = ((wq, off_q, q_landed), (wk, off_k, k_landed), (wv, off_v, v_landed))
            for dst, off, sem in loads:
                sp.dma_start(dst, w[:, :, off:off + P]).then_inc(sem, 16)
            with sp.Fori(1, pairs) as it:
                for n, (dst, off, sem) in enumerate(loads):
                    sp.wait_ge(projected, 3 * it + (n - 2))
                    sp.dma_start(dst, w[:, :, bass.ds(off + it * P, P)]).then_inc(sem, 16)

        @block.tensor
        def _(pe):
            def cumulate(n):
                h, j = order[n]
                for jj in range(j, NT):
                    tri = k.neg_tri if jj == j else k.neg_ones
                    last = nc.tensor.matmul(k.ps[:, bank[n], (jj - j) * P:cols[n]], tri[:],
                                            stay[:, 4 * h + 3 - jj, jj * P:S], start=False, stop=(jj == NT - 1),
                                            skip_group_check=True)
                last.then_inc(logit_done, 1)

            def scores(n):
                h, j = order[n]
                nc.tensor.matmul(k.ps[:, bank[n], 0:cols[n]], kT[64 * h:64 * h + 64, j * P:(j + 1) * P],
                                 qT[64 * h:64 * h + 64, j * P:S], start=True, stop=False,
                                 skip_group_check=True)
                nc.tensor.matmul(k.ps[:, bank[n], 0:P], k.ident[:], k.strict_bias[:], start=False, stop=False,
                                 skip_group_check=True).then_inc(z_done, 1)

            with pe.Fori(0, pairs) as it:
                pe.wait_ge(q_landed, it * 16 + 16)
                pe.wait_ge(k_landed, it * 16 + 16)
                pe.wait_ge(v_landed, it * 16 + 16)
                pe.wait_ge(exp_done, it * 8 + 1)
                project_pair(nc, k, k.hT, wq, wk, wv, (4, 5, 6), projected)
                pe.wait_ge(q_ready, it + 1)
                pe.wait_ge(kv_ready, it * 2 + 2)
                for n in range(7):
                    scores(n)
                for n in range(8):
                    pe.wait_ge(stay_done, it * 8 + (n + 1))
                    cumulate(n)
                    if n == 0:
                        pe.wait_ge(exp_done, it * 8 + 2)
                        scores(7)
                    if n % 4 == 3:
                        h = n // 4
                        if h == 0:
                            pe.wait_ge(y_out, it + 1)
                        pe.wait_ge(exp_done, it * 8 + (n + 2))
                        for j in range(NT):
                            last = nc.tensor.matmul(k.ps[64 * h:64 * h + 64, 7, j * P:S],
                                                    v[:, j, 64 * h:64 * h + 64],
                                                    prob[:, 4 * h + 3 - j, j * P:S],
                                                    start=(j == 0), stop=(j == NT - 1), skip_group_check=True)
                        last.then_inc(pv_done, 1)

        @block.scalar
        def _(act):
            act.preload_act_table_set("natural_log_exp_and_others")
            act.sem_inc(exp_done, 1)
            act.sem_inc(y_out, 1)

            def final(it, n):
                h, j = order[n]
                act.wait_ge(logit_done, it * 8 + (n + 1))
                nc.scalar.activation(prob[:, n, j * P:S], k.ps[:, bank[n], 0:cols[n]], ACT.Exp).then_inc(exp_done, 1)

            with act.Fori(0, pairs) as it:
                act.wait_ge(projected, it * 3 + 1)
                nc.scalar.activation(qT[:], k.ps[:, 4, :], ACT.Copy, scale=SCALE).then_inc(q_ready, 1)
                for n in range(8):
                    a = mag[:, n % 2, 0:cols[n]]
                    act.wait_ge(z_done, it * 8 + (n + 1))
                    if n >= 2:
                        act.wait_ge(stay_done, it * 8 + (n - 1))
                    nc.scalar.activation(a, k.ps[:, bank[n], 0:cols[n]], ACT.Abs).then_inc(mag_done, 1)
                    act.wait_ge(mag_done, it * 8 + (n + 1))
                    nc.scalar.activation(a, a, ACT.Exp, scale=-1.0).then_inc(exp_neg, 1)
                    act.wait_ge(exp_neg, it * 8 + (n + 1))
                    nc.scalar.activation(a, a, ACT.Ln, bias=1.0).then_inc(ln_done, 1)
                    if n:
                        final(it, n - 1)
                final(it, 7)
                act.wait_ge(pv_done, it * 2 + 2)
                nc.scalar.activation(yT[:, it, :], k.ps[:, 7, :], ACT.Copy).then_inc(y_out, 1)

        @block.vector
        def _(dve):
            with dve.Fori(0, pairs) as it:
                dve.wait_ge(projected, it * 3 + 2)
                nc.vector.tensor_copy(kT[:], k.ps[:, 5, :]).then_inc(kv_ready, 1)
                dve.wait_ge(projected, it * 3 + 3)
                nc.vector.tensor_copy(v[:], k.ps[:, 6, :].rearrange("p (t n) -> p t n", t=NT)).then_inc(kv_ready, 1)

                def combine(n):
                    h, j = order[n]
                    dve.wait_ge(ln_done, it * 8 + (n + 1))
                    nc.vector.scalar_tensor_tensor(out=stay[:, n, j * P:S], in0=k.ps[:, bank[n], 0:cols[n]],
                                                   scalar=0.0, in1=mag[:, n % 2, 0:cols[n]],
                                                   op0=ALU.max, op1=ALU.add).then_inc(stay_done, 1)

                for n in range(8):
                    combine(n)



def rotary_tables(k, t, cosT, sinT):
    nc = k.nc
    two_pi = (6.28125, 0.0019353071693331003, 1.0253131677018246e-11)
    magic = 12582912.0
    lim = 3.1415925
    with ExitStack() as ctx:
        def sb(name, shape, dt=F32):
            return ctx.enter_context(nc.sbuf_tensor("rot_" + name, shape, dt))

        pos_i, freq = sb("pos_i", [P, S], I32), sb("freq", [P, 1])
        ang, turn = sb("ang", [P, S]), sb("turn", [P, 2, S])
        landed, step, reduced = sems(k, ctx, "rot_landed rot_step rot_reduced")
        block = ctx.enter_context(nc.Block())

        @block.sync
        def _(sp):
            sp.dma_start(pos_i[:], t["positions"][0, :].partition_broadcast(P)).then_inc(landed, 16)
            sp.dma_start(freq[:], t["c_rope_freq"]).then_inc(landed, 16)

        @block.vector
        def _(dve):
            done = [0]

            def link(ins):
                ins.then_inc(step, 1)
                done[0] += 1
                dve.wait_ge(step, done[0])

            dve.wait_ge(landed, 32)
            link(nc.vector.tensor_copy(ang[:], pos_i[:]))
            link(nc.vector.tensor_scalar(ang[:], ang[:], freq[:], None, ALU.mult))
            for n, (quarter, dst) in enumerate(((0.0, sinT), (0.25, cosT))):
                u = turn[:, n, :]
                link(nc.vector.tensor_scalar(u, ang[:], 1.0 / (2 * math.pi), quarter, ALU.mult, ALU.add))
                link(nc.vector.tensor_scalar(u, u, magic, None, ALU.add))
                link(nc.vector.tensor_scalar(u, u, -magic, None, ALU.add))
                src = ang
                for part in two_pi:
                    link(nc.vector.scalar_tensor_tensor(out=dst[:], in0=u, scalar=-part, in1=src[:],
                                                        op0=ALU.mult, op1=ALU.add))
                    src = dst
                link(nc.vector.tensor_scalar(dst[:], dst[:], quarter * 2 * math.pi, None, ALU.add))
                nc.vector.tensor_scalar(dst[:], dst[:], lim, -lim, ALU.min, ALU.max).then_inc(reduced, 1)

        @block.scalar
        def _(act):
            for n, dst in enumerate((sinT, cosT)):
                act.wait_ge(reduced, n + 1)
                nc.scalar.activation(dst[:], dst[:], ACT.Sin)



def differential(k, w_in, off_q, off_k, off_v, lams, gain, lam_init, keep, cosT, sinT, yT):
    nc = k.nc
    heads = 4
    w = rows_pc(w_in)
    wq, wk, wv = [k.slot(n * DC * P, DC, P) for n in range(3)]
    with ExitStack() as ctx:
        def sb(name, shape):
            return ctx.enter_context(nc.sbuf_tensor("da_" + name, shape, F32))

        raw = sb("raw", [P, 2, S])
        turned_part = sb("turned_part", [P, 2, S])
        qT, kT, v = sb("qT", [P, S]), sb("kT", [P, S]), sb("v", [P, NT, P])
        probs = sb("probs", [P, 2, 2, S])
        diff = sb("diff", [P, 2, S])
        diffT = sb("diffT", [P, 2, S])
        neg_max, sums, coef = sb("neg_max", [P, 2 * NT]), sb("sums", [P, 2 * NT]), sb("coef", [P, NT])
        y, squares = sb("y", [P, NT, P]), sb("squares", [P, P])
        ss = sb("ss", [P, NT])
        lam_in, lam_dot, neg_lam = sb("lam_in", [P, 4, HD]), sb("lam_dot", [P, 4]), sb("neg_lam", [P, 1])
        lam_prod, scale_col, lam_const = sb("lam_prod", [P, HD]), sb("scale_col", [P, 1]), sb("lam_const", [P, 2])
        names = ("q_landed k_landed v_landed lam_landed lam_step lam_exp projected raw_ready v_ready swapped rope_step "
                 "qk_ready s_done max_done exp_done diff_step diff_done turned diffT_ready pv_done y_scaled "
                 "squared mean_ready log_ready rstd_ready normed yT_done y_out act_step")
        sem = dict(zip(names.split(), sems(k, ctx, " ".join("da_" + n for n in names.split()))))
        block = ctx.enter_context(nc.Block())

        @block.sync
        def _(sp):
            loads = ((wq, off_q, sem["q_landed"]), (wk, off_k, sem["k_landed"]), (wv, off_v, sem["v_landed"]))
            for dst, off, landed in loads:
                sp.dma_start(dst, w[:, :, off:off + P]).then_inc(landed, 16)
            for n, lam in enumerate(lams):
                sp.dma_start(lam_in[:, n, :], lam.partition_broadcast(P)).then_inc(sem["lam_landed"], 16)
            sp.dma_start(scale_col[:], gain.rearrange("(p a) -> p a", a=1)).then_inc(sem["lam_landed"], 16)
            sp.dma_start(lam_const[:, 0:1], lam_init.partition_broadcast(P)).then_inc(sem["lam_landed"], 16)
            sp.dma_start(lam_const[:, 1:2], keep.partition_broadcast(P)).then_inc(sem["lam_landed"], 16)
            with sp.Fori(1, heads) as it:
                for n, (dst, off, landed) in enumerate(loads):
                    sp.wait_ge(sem["projected"], 3 * it + (n - 2))
                    sp.dma_start(dst, w[:, :, bass.ds(off + it * P, P)]).then_inc(landed, 16)

        @block.tensor
        def _(pe):
            def scores(it, t):
                n = (t + 1) * P
                for m in (0, 1):
                    half = slice(64 * m, 64 * m + 64)
                    bank = 2 * (t % 2) + m
                    nc.tensor.matmul(k.ps[:, bank, 0:n], qT[half, t * P:n], kT[half, 0:n], start=True, stop=False)
                    last = nc.tensor.matmul(k.ps[:, bank, t * P:n], k.ident[:], k.chunk_bias[:], start=False, stop=True)
                last.then_inc(sem["s_done"], 1)

            with pe.Fori(0, heads) as it:
                for name in ("q_landed", "k_landed", "v_landed"):
                    pe.wait_ge(sem[name], it * 16 + 16)
                pe.wait_ge(sem["exp_done"], it * 8 + 1)
                pe.wait_ge(sem["diffT_ready"], it * 4 + 1)
                project_pair(nc, k, k.hT, wq, wk, wv, (0, 1, 2), sem["projected"])
                for n in (0, 1):
                    pe.wait_ge(sem["raw_ready"], it * 2 + (n + 1))
                    nc.tensor.matmul(k.ps[:, 3 + n, :], k.rope_swap[:], raw[:, n, :], start=True,
                                     stop=True).then_inc(sem["swapped"], 1)
                pe.wait_ge(sem["qk_ready"], it * 2 + 2)
                pe.wait_ge(sem["v_ready"], it + 1)
                scores(it, 0)
                for t in range(NT):
                    if t + 1 < NT:
                        if t >= 1:
                            pe.wait_ge(sem["exp_done"], it * 8 + (2 * t + 1))
                        scores(it, t + 1)
                    pe.wait_ge(sem["diff_done"], it * 4 + (t + 1))
                    if t >= 2:
                        pe.wait_ge(sem["diffT_ready"], it * 4 + t)
                    for b in range(t + 1):
                        last = nc.tensor.transpose(k.ps[:, 4 + t % 2, b * P:(b + 1) * P],
                                                   diff[:, t % 2, b * P:(b + 1) * P], k.ident[:])
                    last.then_inc(sem["turned"], 1)
                    pe.wait_ge(sem["diffT_ready"], it * 4 + (t + 2))
                    for b in range(t + 1):
                        last = nc.tensor.matmul(k.ps[:, 6, t * P:(t + 1) * P], diffT[:, t % 2, b * P:(b + 1) * P],
                                                v[:, b, :], start=(b == 0), stop=(b == t))
                    last.then_inc(sem["pv_done"], 1)
                for t in range(NT):
                    pe.wait_ge(sem["normed"], it * 4 + (t + 1))
                    last = nc.tensor.transpose(k.ps[:, 7, t * P:(t + 1) * P], y[:, t, :], k.ident[:])
                last.then_inc(sem["yT_done"], 1)
                pe.wait_ge(sem["y_out"], it + 1)

        @block.scalar
        def _(act):
            act.preload_act_table_set("natural_log_exp_and_others")
            act.wait_ge(sem["lam_step"], 2)
            nc.scalar.activation(lam_dot[:, 2:4], lam_dot[:, 0:2], ACT.Exp).then_inc(sem["lam_exp"], 1)
            act.sem_inc(sem["exp_done"], 1)
            act.sem_inc(sem["diffT_ready"], 1)
            with act.Fori(0, heads) as it:
                for n, scale in ((0, SCALE), (1, 1.0)):
                    act.wait_ge(sem["projected"], it * 3 + (n + 1))
                    nc.scalar.activation(raw[:, n, :], k.ps[:, n, :], ACT.Copy, scale=scale).then_inc(sem["raw_ready"], 1)

                def exps(t):
                    n = (t + 1) * P
                    act.wait_ge(sem["max_done"], it * 4 + (t + 1))
                    for m in (0, 1):
                        nc.scalar.activation(probs[:, t % 2, m, 0:n], k.ps[:, 2 * (t % 2) + m, 0:n], ACT.Exp,
                                             bias=neg_max[:, 2 * t + m:2 * t + m + 1],
                                             accum_out=sums[:, 2 * t + m:2 * t + m + 1]).then_inc(sem["exp_done"], 1)

                exps(0)
                for t in range(NT):
                    if t + 1 < NT:
                        if t >= 1:
                            act.wait_ge(sem["diff_done"], it * 4 + t)
                        exps(t + 1)
                    act.wait_ge(sem["turned"], it * 4 + (t + 1))
                    nc.scalar.activation(diffT[:, t % 2, 0:(t + 1) * P], k.ps[:, 4 + t % 2, 0:(t + 1) * P],
                                         ACT.Copy).then_inc(sem["diffT_ready"], 1)
                    act.wait_ge(sem["pv_done"], it * 4 + (t + 1))
                    nc.scalar.activation(y[:, t, :], k.ps[:, 6, t * P:(t + 1) * P], ACT.Copy,
                                         scale=sums[:, 2 * t:2 * t + 1]).then_inc(sem["y_scaled"], 1)
                    act.wait_ge(sem["y_scaled"], it * 4 + (t + 1))
                    nc.scalar.activation(squares[:], y[:, t, :], ACT.Square,
                                         accum_out=ss[:, t:t + 1]).then_inc(sem["squared"], 1)
                act.wait_ge(sem["mean_ready"], it + 1)
                nc.scalar.activation(ss[:], ss[:], ACT.Ln).then_inc(sem["log_ready"], 1)
                act.wait_ge(sem["log_ready"], it + 1)
                nc.scalar.activation(ss[:], ss[:], ACT.Exp, scale=-0.5).then_inc(sem["rstd_ready"], 1)
                act.wait_ge(sem["yT_done"], it + 1)
                nc.scalar.activation(yT[:, it, :], k.ps[:, 7, :], ACT.Copy, scale=scale_col[:]).then_inc(sem["y_out"], 1)

        @block.vector
        def _(dve):
            dve.wait_ge(sem["lam_landed"], 16 * 7)
            for n in (0, 1):
                nc.vector.tensor_tensor_reduce(out=lam_prod[:], in0=lam_in[:, 2 * n, :], in1=lam_in[:, 2 * n + 1, :],
                                               scale=1.0, scalar=0.0, op0=ALU.mult, op1=ALU.add,
                                               accum_out=lam_dot[:, n:n + 1]).then_inc(sem["lam_step"], 1)
                dve.wait_ge(sem["lam_step"], n + 1)
            dve.wait_ge(sem["lam_exp"], 1)
            nc.vector.tensor_tensor(neg_lam[:], lam_dot[:, 3:4], lam_dot[:, 2:3], ALU.subtract).then_inc(sem["lam_step"], 1)
            dve.wait_ge(sem["lam_step"], 3)
            nc.vector.tensor_tensor(neg_lam[:], neg_lam[:], lam_const[:, 0:1], ALU.subtract).then_inc(sem["lam_step"], 1)
            nc.vector.tensor_tensor(scale_col[:], scale_col[:], lam_const[:, 1:2], ALU.mult).then_inc(sem["lam_step"], 1)
            dve.wait_ge(sem["lam_step"], 5)
            with dve.Fori(0, heads) as it:
                dve.wait_ge(sem["projected"], it * 3 + 3)
                nc.vector.tensor_copy(v[:], k.ps[:, 2, :].rearrange("p (t n) -> p t n", t=NT)).then_inc(sem["v_ready"], 1)
                for n, dst in ((0, qT), (1, kT)):
                    dve.wait_ge(sem["raw_ready"], it * 2 + (n + 1))
                    nc.vector.tensor_tensor(turned_part[:, n, :], raw[:, n, :], cosT[:], ALU.mult)\
                        .then_inc(sem["rope_step"], 1)
                    dve.wait_ge(sem["swapped"], it * 2 + (n + 1))
                    nc.vector.tensor_tensor(dst[:], k.ps[:, 3 + n, :], sinT[:], ALU.mult).then_inc(sem["rope_step"], 1)
                    dve.wait_ge(sem["rope_step"], it * 4 + (2 * n + 2))
                    nc.vector.tensor_tensor(dst[:], dst[:], turned_part[:, n, :], ALU.add).then_inc(sem["qk_ready"], 1)

                def maxima(t):
                    dve.wait_ge(sem["s_done"], it * 4 + (t + 1))
                    b = 2 * (t % 2)
                    nc.vector.tensor_reduce(out=neg_max[:, 2 * t:2 * t + 2], in_=k.ps[:, b:b + 2, 0:(t + 1) * P],
                                            axis=AX.X, op=ALU.max, negate=True).then_inc(sem["max_done"], 1)

                maxima(0)
                for t in range(NT):
                    if t + 1 < NT:
                        maxima(t + 1)
                    n = (t + 1) * P
                    dve.wait_ge(sem["exp_done"], it * 8 + (2 * t + 3))
                    base = it * 12 + 3 * t
                    nc.vector.reciprocal(coef[:, t:t + 1], sums[:, 2 * t + 1:2 * t + 2]).then_inc(sem["diff_step"], 1)
                    dve.wait_ge(sem["diff_step"], base + 1)
                    nc.vector.scalar_tensor_tensor(out=coef[:, t:t + 1], in0=coef[:, t:t + 1], scalar=neg_lam[:],
                                                   in1=sums[:, 2 * t:2 * t + 1], op0=ALU.mult,
                                                   op1=ALU.mult).then_inc(sem["diff_step"], 1)
                    dve.wait_ge(sem["diff_step"], base + 2)
                    nc.vector.reciprocal(sums[:, 2 * t:2 * t + 1], sums[:, 2 * t:2 * t + 1]).then_inc(sem["diff_step"], 1)
                    nc.vector.scalar_tensor_tensor(out=diff[:, t % 2, 0:n], in0=probs[:, t % 2, 1, 0:n],
                                                   scalar=coef[:, t:t + 1], in1=probs[:, t % 2, 0, 0:n],
                                                   op0=ALU.mult, op1=ALU.add).then_inc(sem["diff_done"], 1)
                dve.wait_ge(sem["squared"], it * 4 + 4)
                nc.vector.tensor_scalar(ss[:], ss[:], 1.0 / P, EPS, ALU.mult, ALU.add).then_inc(sem["mean_ready"], 1)
                dve.wait_ge(sem["rstd_ready"], it + 1)
                for t in range(NT):
                    nc.vector.tensor_scalar(y[:, t, :], y[:, t, :], ss[:, t:t + 1], None,
                                            ALU.mult).then_inc(sem["normed"], 1)



def every(eng, blocks, per_round, step):
    rounds = -(-blocks // per_round)
    for u in range(min(per_round, blocks)):
        step(0, u)
    if rounds > 3:
        with eng.Fori(1, rounds - 2) as it:
            for u in range(per_round):
                step(it, u)
    for it in range(max(1, rounds - 2), rounds):
        for u in range(min(per_round, blocks - it * per_round)):
            step(it, u)


def wait(eng, sem, value):
    if not isinstance(value, int) or value > 0:
        eng.wait_ge(sem, value)


def merge(k, tag, w_in, gates, branches, mergedT):
    nc = k.nc
    cols, nb = 256, len(gates)
    w = rows_pc(w_in)
    words = nb * DC * cols + sum(n for _, _, n in branches) * cols
    assert 2 * words <= RING

    def places(u):
        at, g, b = u * words, [], []
        for _ in gates:
            g.append(k.slot(at, DC, cols))
            at += DC * cols
        for _, _, n in branches:
            b.append(k.slot(at, n, cols))
            at += n * cols
        return g, b

    halves = [places(0), places(1)]
    per_body = 2 * 2 * nb
    with ExitStack() as ctx:
        def sb(name, shape):
            return ctx.enter_context(nc.sbuf_tensor(tag + "_" + name, shape, F32))

        sig, part = sb("sig", [P, 4, S]), sb("part", [P, 4, S])
        landed0, landed1, multiplied, sig_done, bank_free, summed = sems(k, ctx, " ".join(tag + n for n in "_landed0 _landed1 _multiplied _sig_done _bank_free _summed".split()))
        landed = (landed0, landed1)
        block = ctx.enter_context(nc.Block())

        @block.sync
        def _(sp):
            def load(u, col):
                for dst, off in zip(halves[u][0], gates):
                    sp.dma_start(dst, w[:, :, bass.ds(off + col, cols)]).then_inc(landed[u], 16)
                for dst, (wb, _, n) in zip(halves[u][1], branches):
                    sp.dma_start(dst, wb.rearrange("(c p) n -> p c n", p=P)[:, :, bass.ds(col, cols)])\
                        .then_inc(landed[u], 16)

            load(0, 0)
            load(1, cols)
            for u in (0, 1):
                sp.wait_ge(multiplied, 2 * nb * (u + 1))
                load(u, (2 + u) * cols)

        @block.tensor
        def _(pe):
            with pe.Fori(0, 2) as it:
                for u in (0, 1):
                    pe.wait_ge(landed[u], it * (32 * nb) + 32 * nb)
                    for m in (0, 1):
                        for b, (_, yT, n) in enumerate(branches):
                            i = (2 * u + m) * nb + b
                            r = i % 4
                            pe.wait_ge(bank_free, it * per_body + (i + 1))
                            for c in range(DC):
                                nc.tensor.matmul(k.ps[:, 2 * r, :], halves[u][0][b][:, c, m * P:(m + 1) * P],
                                                 k.hT[:, c, :], start=(c == 0), stop=(c == DC - 1))
                            for c in range(n):
                                last = nc.tensor.matmul(k.ps[:, 2 * r + 1, :], halves[u][1][b][:, c, m * P:(m + 1) * P],
                                                        yT[:, c, :], start=(c == 0), stop=(c == n - 1))
                            last.then_inc(multiplied, 1)

        @block.scalar
        def _(act):
            with act.Fori(0, 2) as it:
                for i in range(per_body):
                    act.wait_ge(multiplied, it * per_body + (i + 1))
                    nc.scalar.activation(sig[:, i % 4, :], k.ps[:, 2 * (i % 4), :], ACT.Sigmoid).then_inc(sig_done, 1)

        @block.vector
        def _(dve):
            dve.sem_inc(bank_free, 4)
            with dve.Fori(0, 2) as it:
                for i in range(per_body):
                    chunk, b, r = i // nb, i % nb, i % 4
                    out = mergedT[:, it * 4 + chunk, :]
                    dve.wait_ge(sig_done, it * per_body + (i + 1))
                    dst = out if b == 0 else part[:, r, :]
                    nc.vector.tensor_tensor(dst, sig[:, r, :], k.ps[:, 2 * r + 1, :], ALU.mult).then_inc(bank_free, 1)
                    if b:
                        dve.wait_ge(bank_free, it * per_body + (i + 5))
                        if b > 1:
                            dve.wait_ge(summed, it * (4 * (nb - 1)) + (chunk * (nb - 1) + b - 1))
                        nc.vector.tensor_tensor(out, out, part[:, r, :], ALU.add).then_inc(summed, 1)


def project_and_add(k, tag, w_out, srcT):
    nc = k.nc
    w = [k.slot(n * DC * 512, DC, 512) for n in (0, 1)]
    rows = w_out.rearrange("(c p) n -> p c n", p=P)
    with ExitStack() as ctx:
        landed0, landed1, multiplied = sems(k, ctx, f"{tag}_landed0 {tag}_landed1 {tag}_multiplied")
        block = ctx.enter_context(nc.Block())

        @block.sync
        def _(sp):
            for n, landed in enumerate((landed0, landed1)):
                sp.dma_start(w[n], rows[:, :, n * 512:(n + 1) * 512]).then_inc(landed, 16)

        @block.tensor
        def _(pe):
            for n, landed in enumerate((landed0, landed1)):
                pe.wait_ge(landed, 16)
                for t in range(NT):
                    for c in range(DC):
                        last = nc.tensor.matmul(k.ps[:, n * NT + t, :], srcT[:, c, t * P:(t + 1) * P], w[n][:, c, :],
                                                start=(c == 0), stop=(c == DC - 1))
                    last.then_inc(multiplied, 1)

        @block.vector
        def _(dve):
            for n in (0, 1):
                for t in range(NT):
                    dve.wait_ge(multiplied, n * NT + t + 1)
                    part = k.x[:, t, n * 512:(n + 1) * 512]
                    nc.vector.tensor_tensor(part, part, k.ps[:, n * NT + t, :], ALU.add)



GROUPS, PER_GROUP = 4, 8
EXPERTS = GROUPS * PER_GROUP
HID = 256
SPILL = 2 * S // P
BLOCKS = EXPERTS + SPILL
SKIP = 65536.0


class Routing:

    def __init__(self, nc, ctx):
        def sb(name, shape, dt=F32):
            return ctx.enter_context(nc.sbuf_tensor("route_" + name, shape, dt))

        self.gate = sb("gate", [P, 2, NT])
        self.token = sb("token", [P, BLOCKS], I32)
        self.row = sb("row", [P, BLOCKS], I32)
        self.spill_expert = sb("spill_expert", [1, SPILL + 1], I32)
        self.gain = sb("gain", [P, DC])


def route(k, tag, r, w_group, b_group, w_expert, b_expert, gain):
    nc = k.nc
    NE, NL = EXPERTS, GROUPS + EXPERTS
    magic = 12582912.0
    with ExitStack() as ctx:
        def sb(name, shape, dt=F32):
            return ctx.enter_context(nc.sbuf_tensor(tag + "_" + name, shape, dt))

        w = sb("w", [P, DC, NL])
        bias = sb("bias", [P, NL])
        iota = sb("iota", [P, P])
        block_base = sb("block_base", [P, NE])
        lg = sb("lg", [P, NT, NL])
        gpad = sb("gpad", [P, NT, 8])
        gtop, gidx = sb("gtop", [P, NT, 8]), sb("gidx", [P, NT, 8], U32)
        gsel, gneg, gsum = sb("gsel", [P, NT]), sb("gneg", [P, NT]), sb("gsum", [P, NT])
        gexp = sb("gexp", [P, NT, GROUPS])
        chosen = sb("chosen", [P, NT, GROUPS])
        em = sb("em", [P, NT, NE])
        pen = sb("pen", [P, NT, GROUPS])
        etop, eidx = sb("etop", [P, NT, 8]), sb("eidx", [P, NT, 8], U32)
        esel = sb("esel", [P, 2, NT])
        gap, den = sb("gap", [P, NT]), sb("den", [P, NT])
        onehot = sb("onehot", [P, 2, NT, NE])
        member = sb("member", [P, NT, NE])
        counts, spills, ends, delta = sb("counts", [P, NE]), sb("spills", [P, NE]), sb("ends", [P, NE]), sb("delta", [P, NE])
        ones_row = sb("ones_row", [P, NE])
        over = sb("over", [P, NT, NE])
        slotv = sb("slotv", [P, NT, NE])
        junk = sb("junk", [P, NE])
        dest, blk, lane = sb("dest", [P, 8]), sb("blk", [P, 8]), sb("lane", [P, 8])
        values = sb("values", [P, 8, 2])
        lane_hot = sb("lane_hot", [P, 8, P])
        block_hot = sb("block_hot", [P, 8, 2, BLOCKS])
        table = sb("table", [P, 2, BLOCKS])
        spill_f = sb("spill_f", [P, SPILL + 1])
        ones, before = sb("ones", [P, P]), sb("before", [P, P])
        landed, link_sem, logits_done, gneg_ready, gexp_done, gap_ready, ratio_done, member_ready, ranked, hot_ready, tabled = sems(k, ctx, " ".join(tag + n for n in ("_landed _link _logits_done _gneg_ready _gexp_done _gap_ready _ratio_done "
                                                "_member_ready _ranked _hot_ready _tabled").split()))
        block = ctx.enter_context(nc.Block())

        @block.sync
        def _(sp):
            sp.dma_start(w[:, :, 0:GROUPS], rows_pc(w_group)).then_inc(landed, 16)
            sp.dma_start(w[:, :, GROUPS:NL], rows_pc(w_expert)).then_inc(landed, 16)
            sp.dma_start(bias[:, 0:GROUPS], b_group.partition_broadcast(P)).then_inc(landed, 16)
            sp.dma_start(bias[:, GROUPS:NL], b_expert.partition_broadcast(P)).then_inc(landed, 16)
            sp.dma_start(r.gain[:], gain.rearrange("(p c) -> p c", c=DC)).then_inc(landed, 16)
            sp.dma_start(iota[:], k.t["c_iota"].partition_broadcast(P)).then_inc(landed, 16)
            sp.dma_start(before[:], k.t["c_before"]).then_inc(landed, 16)
            sp.dma_start(values[:], k.t["c_slot_values"]).then_inc(landed, 16)

        @block.tensor
        def _(pe):
            pe.wait_ge(landed, 16 * 8)
            for t in range(NT):
                for c in range(DC):
                    last = nc.tensor.matmul(k.ps[:, 0, t * NL:(t + 1) * NL], k.hT[:, c, t * P:(t + 1) * P], w[:, c, :],
                                            start=(c == 0), stop=(c == DC - 1))
            last.then_inc(logits_done, 1)
            pe.wait_ge(member_ready, 1)
            for t in range(NT):
                for b in range(t + 1):
                    nc.tensor.matmul(k.ps[:, 1, t * NE:(t + 1) * NE], (before if b == t else ones)[:], member[:, b, :],
                                     start=(b == 0), stop=(b == t))
            for b in range(NT):
                last = nc.tensor.matmul(k.ps[:, 2, 0:NE], ones[:], member[:, b, :], start=(b == 0), stop=(b == NT - 1))
            last.then_inc(ranked, 1)
            pe.wait_ge(hot_ready, 8)
            for i in range(8):
                last = nc.tensor.matmul(k.ps[:, 3, 0:2 * BLOCKS], lane_hot[:, i, :],
                                        block_hot[:, i, :, :].rearrange("p a b -> p (a b)"), start=(i == 0), stop=(i == 7))
            last.then_inc(tabled, 1)

        @block.scalar
        def _(act):
            act.wait_ge(gneg_ready, 1)
            for t in range(NT):
                nc.scalar.activation(gexp[:, t, :], lg[:, t, 0:GROUPS], ACT.Exp, bias=gneg[:, t:t + 1],
                                     accum_out=gsum[:, t:t + 1]).then_inc(gexp_done, 1)
            act.wait_ge(gap_ready, 1)
            nc.scalar.activation(gap[:], gap[:], ACT.Exp).then_inc(ratio_done, 1)

        @block.vector
        def _(dve):
            V = nc.vector
            done = [0]

            def link(*instructions):
                for ins in instructions:
                    ins.then_inc(link_sem, 1)
                    done[0] += 1
                dve.wait_ge(link_sem, done[0])

            link(V.memset(gpad[:], NEG), V.memset(ones[:], 1.0), V.memset(ones_row[:], 1.0))
            dve.wait_ge(landed, 16 * 8)
            dve.wait_ge(logits_done, 1)
            link(*[V.tensor_tensor(lg[:, t, :], k.ps[:, 0, t * NL:(t + 1) * NL], bias[:], ALU.add) for t in range(NT)])
            link(V.tensor_copy(gpad[:, :, 0:GROUPS], lg[:, :, 0:GROUPS]),
                 V.tensor_scalar(block_base[:], iota[:, 0:NE], float(P), None, ALU.mult))
            link(*[V.max(gtop[:, t, :], gpad[:, t, :]) for t in range(NT)])
            link(V.tensor_scalar(gneg[:], gtop[:, :, 0], -1.0, None, ALU.mult))
            dve.sem_inc(gneg_ready, 1)
            link(*[V.max_index(gidx[:, t, :], gtop[:, t, :], gpad[:, t, :]) for t in range(NT)])
            link(V.tensor_copy(gsel[:], gidx[:, :, 0]))
            link(*[V.tensor_scalar(chosen[:, t, :], iota[:, 0:GROUPS], gsel[:, t:t + 1], None, ALU.is_equal)
                   for t in range(NT)])
            link(V.tensor_scalar(pen[:], chosen[:], -NEG, NEG, ALU.mult, ALU.add))

            def per_group(a):
                return a.rearrange("p (g e) -> p g e", g=GROUPS)

            def spread(a):
                return a.unsqueeze(2).to_broadcast([P, GROUPS, PER_GROUP])

            link(*[V.tensor_tensor(per_group(em[:, t, :]), per_group(lg[:, t, GROUPS:NL]), spread(chosen[:, t, :]), ALU.mult)
                   for t in range(NT)])
            link(*[V.tensor_tensor(per_group(em[:, t, :]), per_group(em[:, t, :]), spread(pen[:, t, :]), ALU.add)
                   for t in range(NT)])
            link(*[V.max(etop[:, t, :], em[:, t, :]) for t in range(NT)])
            link(*[V.max_index(eidx[:, t, :], etop[:, t, :], em[:, t, :]) for t in range(NT)])
            link(V.tensor_copy(esel[:, 0, :], eidx[:, :, 0]), V.tensor_copy(esel[:, 1, :], eidx[:, :, 1]),
                 V.tensor_tensor(gap[:], etop[:, :, 1], etop[:, :, 0], ALU.subtract))
            dve.sem_inc(gap_ready, 1)
            link(*[V.tensor_scalar(onehot[:, c, t, :], iota[:, 0:NE], esel[:, c, t:t + 1], None, ALU.is_equal)
                   for t in range(NT) for c in (0, 1)])
            link(V.tensor_tensor(member[:], onehot[:, 0, :, :], onehot[:, 1, :, :], ALU.add))
            dve.sem_inc(member_ready, 1)
            dve.wait_ge(gexp_done, NT)
            dve.wait_ge(ratio_done, 1)
            link(V.tensor_scalar(den[:], gap[:], 1.0, None, ALU.add))
            link(V.tensor_tensor(den[:], den[:], gsum[:], ALU.mult))
            link(V.reciprocal(r.gate[:, 0, :], den[:]))
            link(V.tensor_tensor(r.gate[:, 1, :], r.gate[:, 0, :], gap[:], ALU.mult))
            dve.wait_ge(ranked, 1)
            link(V.tensor_copy(counts[:], k.ps[:, 2, 0:NE]))
            link(V.tensor_scalar(spills[:], counts[:], 1.0 * P, None, ALU.is_gt))
            for full in (2, 3):
                link(V.scalar_tensor_tensor(out=spills[:], in0=counts[:], scalar=full * P + 0.0, in1=spills[:],
                                            op0=ALU.is_gt, op1=ALU.add))
            link(V.tensor_tensor_scan(ends[:], ones_row[:], spills[:], 0.0, ALU.mult, ALU.add))
            link(V.tensor_tensor(delta[:], ends[:], spills[:], ALU.subtract))
            link(V.tensor_scalar(delta[:], delta[:], float(P), float((NE - 1) * P), ALU.mult, ALU.add))
            link(V.tensor_tensor(delta[:], delta[:], block_base[:], ALU.subtract))
            for t in range(NT):
                rank = k.ps[:, 1, t * NE:(t + 1) * NE]
                link(V.tensor_scalar(over[:, t, :], rank, P - 0.5, None, ALU.is_gt))
                link(V.tensor_tensor(over[:, t, :], over[:, t, :], delta[:], ALU.mult))
                link(V.tensor_tensor(slotv[:, t, :], rank, block_base[:], ALU.add))
                link(V.tensor_tensor(slotv[:, t, :], slotv[:, t, :], over[:, t, :], ALU.add))
                for c in (0, 1):
                    link(V.tensor_tensor_reduce(out=junk[:], in0=onehot[:, c, t, :], in1=slotv[:, t, :], scale=1.0,
                                                scalar=0.0, op0=ALU.mult, op1=ALU.add,
                                                accum_out=dest[:, 2 * t + c:2 * t + c + 1]))
            link(V.tensor_scalar(blk[:], dest[:], -(P / 2 - 0.5), 1.0 / P, ALU.add, ALU.mult))
            link(V.tensor_scalar(blk[:], blk[:], magic, None, ALU.add))
            link(V.tensor_scalar(blk[:], blk[:], -magic, None, ALU.add))
            link(V.scalar_tensor_tensor(out=lane[:], in0=blk[:], scalar=-float(P), in1=dest[:], op0=ALU.mult, op1=ALU.add))
            for i in range(8):
                V.tensor_scalar(lane_hot[:, i, :], iota[:], lane[:, i:i + 1], None, ALU.is_equal)
                for a in (0, 1):
                    last = V.tensor_scalar(block_hot[:, i, a, :], iota[:, 0:BLOCKS], blk[:, i:i + 1], values[:, i, a:a + 1],
                                           ALU.is_equal, ALU.mult)
                last.then_inc(hot_ready, 1)
            for b in range(SPILL):
                link(V.tensor_scalar(junk[:], ends[:], b + 0.5, None, ALU.is_lt, ALU.add, accum_out=spill_f[:, b:b + 1]))
            link(V.tensor_scalar(spill_f[:, 0:SPILL], spill_f[:, 0:SPILL], float(NE - 1), None, ALU.min),
                 V.tensor_copy(spill_f[:, SPILL:SPILL + 1], ends[:, NE - 1:NE]))
            link(V.tensor_copy(r.spill_expert[:], spill_f[0:1, :]))
            dve.wait_ge(tabled, 1)
            link(V.tensor_scalar(table[:].rearrange("p a b -> p (a b)"), k.ps[:, 3, 0:2 * BLOCKS], 0.0, SKIP,
                                 ALU.is_equal, ALU.mult))
            link(V.tensor_tensor(table[:].rearrange("p a b -> p (a b)"), table[:].rearrange("p a b -> p (a b)"),
                                 k.ps[:, 3, 0:2 * BLOCKS], ALU.add))
            link(V.tensor_scalar(r.token[:], table[:, 0, :], -1.0, None, ALU.add),
                 V.tensor_scalar(r.row[:], table[:, 1, :], -1.0, None, ALU.add))


def experts(k, tag, r, layer, blocks, spill, xn_rows, y_rows, w_gate, w_up, w_down):
    nc = k.nc
    first = EXPERTS if spill else 0
    words = DC * 2 * HID + 2 * D
    assert 3 * words <= RING
    U = 3
    slots = [(k.slot(u * words, DC, 2 * HID), k.slot(u * words + DC * 2 * HID, 2, D)) for u in range(3)]
    with ExitStack() as ctx:
        def sb(name, shape, dt=F32):
            return ctx.enter_context(nc.sbuf_tensor(tag + "_" + name, shape, dt))

        idx = sb("idx", [P, U, 2], I32)
        xs = sb("xs", [P, U, D])
        xsT = sb("xsT", [P, U, DC, P])
        silu = sb("silu", [P, HID])
        hid = sb("hid", [P, U, HID])
        hidT = sb("hidT", [P, U, 2, P])
        y = sb("y", [P, U, D])
        names = ("w_landed0 w_landed1 w_landed2 cleared wait_kept token_ready row_ready gathered0 gathered1 gathered2 turned xsT_ready gu_done silu_done hid_ready "
                 "hid_turned hidT_ready down_done y_act y_dve scattered0 scattered1 scattered2")
        sem = dict(zip(names.split(), sems(k, ctx, " ".join(tag + "_" + n for n in names.split()))))
        w_landed, gathered, scattered = [[sem[f"{n}{u}"] for u in range(U)] for n in ("w_landed", "gathered", "scattered")]
        block = ctx.enter_context(nc.Block())

        def before(it, u):
            return (it, u - 1) if u else (it - 1, U - 1)

        def after(it, u):
            return (it, u + 1) if u + 1 < U else (it + 1, 0)

        def first_block(it, u):
            return isinstance(it, int) and it == 0 and u == 0

        def last_block(it, u):
            return isinstance(it, int) and it * U + u == blocks - 1

        @block.sync
        def _(sp):
            def step(it, u):
                wait(sp, sem["down_done"], it * U + (u - U + 1))
                n = it * U + u
                e = sp.value_load(r.spill_expert[0:1, bass.ds(n, 1)], min_val=0, max_val=EXPERTS - 1) if spill else n
                gu, down = slots[u]
                sp.dma_start(gu[:, :, 0:HID], rows_pc(w_gate[layer, e])).then_inc(w_landed[u], 16)
                sp.dma_start(gu[:, :, HID:2 * HID], rows_pc(w_up[layer, e])).then_inc(w_landed[u], 16)
                sp.dma_start(down, w_down[layer, e].rearrange("(f p) n -> p f n", p=P)).then_inc(w_landed[u], 16)

            every(sp, blocks, U, step)

        @block.gpsimd
        def _(pool):
            def gather(it, u):
                n = it * U + u
                wait(pool, sem["turned"], it * U + (u - U + 1))
                nc.gpsimd.tensor_copy(idx[:, u, 0:1], r.token[:, bass.ds(n + first, 1)]).then_inc(sem["token_ready"], 1)
                pool.wait_ge(sem["token_ready"], it * U + (u + 1))
                pool.sem_inc(sem["wait_kept"], 1)
                nc.gpsimd.indirect_dma_start(out=xs[:, u, :], out_offset=None, in_=xn_rows[:, :],
                                             in_offset=bass.IndirectOffsetOnAxis(ap=idx[:, u, 0:1], axis=0),
                                             bounds_check=last_token, oob_is_err=False).then_inc(gathered[u], 16)

            def scatter(it, u):
                n = it * U + u
                wait(pool, scattered[u], it * 16)
                nc.gpsimd.tensor_copy(idx[:, u, 1:2], r.row[:, bass.ds(n + first, 1)]).then_inc(sem["row_ready"], 1)
                pool.wait_ge(sem["row_ready"], it * U + (u + 1))
                pool.wait_ge(sem["y_act"], it * U + (u + 1))
                pool.wait_ge(sem["y_dve"], it * U + (u + 1))
                pool.sem_inc(sem["wait_kept"], 1)
                nc.gpsimd.indirect_dma_start(out=y_rows[:, :], in_=y[:, u, :], in_offset=None,
                                             out_offset=bass.IndirectOffsetOnAxis(ap=idx[:, u, 1:2], axis=0),
                                             bounds_check=last_row, oob_is_err=False).then_inc(scattered[u], 16)

            last_token, last_row = pool.to_reg(S - 1), pool.to_reg(2 * S - 1)
            nc.gpsimd.memset(xs[:], 0.0).then_inc(sem["cleared"], 1)
            pool.wait_ge(sem["cleared"], 1)
            for u in range(U):
                gather(0, u)

            def step(it, u):
                if not isinstance(it, int) or (it + 1) * U + u < blocks:
                    gather(it + 1, u)
                scatter(it, u)

            every(pool, blocks, U, step)
            for u in range(U):
                pool.wait_ge(scattered[u], 16 * len(range(u, blocks, U)))

        @block.tensor
        def _(pe):
            def turn(it, u):
                pe.wait_ge(gathered[u], it * 16 + 16)
                wait(pe, sem["xsT_ready"], it * U + u)
                for c in range(DC):
                    last = nc.tensor.transpose(k.ps[:, c // 4, (c % 4) * P:(c % 4 + 1) * P], xs[:, u, c::DC], k.ident[:])
                last.then_inc(sem["turned"], 1)

            def down(it, u):
                pe.wait_ge(sem["hidT_ready"], it * U + (u + 1))
                wait(pe, sem["y_act"], it * U + u)
                wait(pe, sem["y_dve"], it * U + u)
                for half in (0, 1):
                    for f in (0, 1):
                        last = nc.tensor.matmul(k.ps[:, 4 + half, :], hidT[:, u, f, :],
                                                slots[u][1][:, f, half * 512:(half + 1) * 512], start=(f == 0), stop=(f == 1))
                last.then_inc(sem["down_done"], 1)

            def step(it, u):
                pe.wait_ge(w_landed[u], it * 48 + 48)
                pe.wait_ge(sem["xsT_ready"], it * U + (u + 1))
                wait(pe, sem["hid_ready"], it * U + u)
                for c in range(DC):
                    last = nc.tensor.matmul(k.ps[:, 2, :], xsT[:, u, c, :], slots[u][0][:, c, :],
                                            start=(c == 0), stop=(c == DC - 1))
                last.then_inc(sem["gu_done"], 1)
                if not first_block(it, u):
                    down(*before(it, u))
                if not last_block(it, u):
                    turn(*after(it, u))
                pe.wait_ge(sem["hid_ready"], it * U + (u + 1))
                for f in (0, 1):
                    last = nc.tensor.transpose(k.ps[:, 3, f * P:(f + 1) * P], hid[:, u, f * P:(f + 1) * P], k.ident[:])
                last.then_inc(sem["hid_turned"], 1)

            turn(0, 0)
            every(pe, blocks, U, step)
            down(*divmod(blocks - 1, U))

        @block.scalar
        def _(act):
            def y_half(it, u):
                act.wait_ge(sem["down_done"], it * U + (u + 1))
                wait(act, scattered[u], it * 16)
                nc.scalar.activation(y[:, u, 0:512], k.ps[:, 4, :], ACT.Copy).then_inc(sem["y_act"], 1)

            def step(it, u):
                act.wait_ge(sem["gu_done"], it * U + (u + 1))
                nc.scalar.activation(silu[:], k.ps[:, 2, 0:HID], ACT.Silu).then_inc(sem["silu_done"], 1)
                if not first_block(it, u):
                    y_half(*before(it, u))
                act.wait_ge(sem["hid_turned"], it * U + (u + 1))
                nc.scalar.activation(hidT[:, u, :, :].rearrange("p f n -> p (f n)"), k.ps[:, 3, 0:HID],
                                     ACT.Copy).then_inc(sem["hidT_ready"], 1)

            every(act, blocks, U, step)
            y_half(*divmod(blocks - 1, U))

        @block.vector
        def _(dve):
            def gained(it, u):
                dve.wait_ge(sem["turned"], it * U + (u + 1))
                for b in (0, 1):
                    last = nc.vector.tensor_tensor(xsT[:, u, 4 * b:4 * b + 4, :],
                                                   k.ps[:, b, :].rearrange("p (c n) -> p c n", c=4),
                                                   r.gain[:, 4 * b:4 * b + 4].unsqueeze(2).to_broadcast([P, 4, P]), ALU.mult)
                last.then_inc(sem["xsT_ready"], 1)

            def y_half(it, u):
                dve.wait_ge(sem["down_done"], it * U + (u + 1))
                wait(dve, scattered[u], it * 16)
                nc.vector.tensor_copy(y[:, u, 512:D], k.ps[:, 5, :]).then_inc(sem["y_dve"], 1)

            def step(it, u):
                dve.wait_ge(sem["silu_done"], it * U + (u + 1))
                nc.vector.tensor_tensor(hid[:, u, :], silu[:], k.ps[:, 2, HID:2 * HID], ALU.mult).then_inc(sem["hid_ready"], 1)
                if not first_block(it, u):
                    y_half(*before(it, u))
                if not last_block(it, u):
                    gained(*after(it, u))

            gained(0, 0)
            every(dve, blocks, U, step)
            y_half(*divmod(blocks - 1, U))


def combine_experts(k, tag, r, y_rows):
    nc = k.nc
    rows = y_rows.rearrange("(t p c) d -> p t (c d)", p=P, c=2)
    y = k.ring[:, 0:NT * 2 * D].rearrange("p (t c d) -> p t c d", t=NT, c=2)
    with ExitStack() as ctx:
        (*landed, added) = sems(k, ctx, " ".join(f"{tag}_landed{t}" for t in range(NT)) + f" {tag}_added")
        block = ctx.enter_context(nc.Block())

        @block.sync
        def _(sp):
            for t in range(NT):
                sp.dma_start(y[:, t, :, :].rearrange("p c d -> p (c d)"), rows[:, t, :]).then_inc(landed[t], 16)

        @block.vector
        def _(dve):
            for t in range(NT):
                dve.wait_ge(landed[t], 16)
                for c in (0, 1):
                    nc.vector.scalar_tensor_tensor(out=k.x[:, t, :], in0=y[:, t, c, :], scalar=r.gate[:, c, t:t + 1],
                                                   in1=k.x[:, t, :], op0=ALU.mult, op1=ALU.add).then_inc(added, 1)
                    dve.wait_ge(added, 2 * t + c + 1)


def embed_per_layer(k, tag, p_rows, w_ple, w_gate):
    nc = k.nc
    PC = 2
    wg = k.slot(0, DC, D)
    wp = k.slot(DC * D, PC, D)
    with ExitStack() as ctx:
        def sb(name, shape):
            return ctx.enter_context(nc.sbuf_tensor(tag + "_" + name, shape, F32))

        rows, pT = sb("rows", [P, NT, PC * P]), sb("pT", [P, PC, S])
        sig, part = sb("sig", [P, 3, 512]), sb("part", [P, 3, 512])
        p_landed, wp_landed, wg0, wg1, turned, pT_ready, multiplied, sig_done, part_done = sems(k, ctx, " ".join(tag + n for n in
                              "_p_landed _wp_landed _wg0 _wg1 _turned _pT_ready _multiplied _sig_done _part_done".split()))
        block = ctx.enter_context(nc.Block())

        @block.sync
        def _(sp):
            sp.dma_start(rows[:], p_rows.rearrange("(t p) d -> p t d", p=P)).then_inc(p_landed, 16)
            sp.dma_start(wp, w_ple.rearrange("(c p) n -> p c n", p=P)).then_inc(wp_landed, 16)
            for n, sem in enumerate((wg0, wg1)):
                sp.dma_start(wg[:, :, n * 512:(n + 1) * 512], rows_pc(w_gate)[:, :, n * 512:(n + 1) * 512]).then_inc(sem, 16)

        @block.tensor
        def _(pe):
            pe.wait_ge(p_landed, 16)
            for c in range(PC):
                for t in range(NT):
                    last = nc.tensor.transpose(k.ps[:, 6 + c, t * P:(t + 1) * P], rows[:, t, c * P:(c + 1) * P], k.ident[:])
            last.then_inc(turned, 1)
            pe.wait_ge(pT_ready, 1)
            pe.wait_ge(wp_landed, 16)
            for n, sem in enumerate((wg0, wg1)):
                pe.wait_ge(sem, 16)
                half = slice(n * 512, (n + 1) * 512)
                for t in range(NT):
                    i = n * NT + t
                    wait(pe, part_done, i - 2)
                    g = 2 * (i % 3)
                    for c in range(PC):
                        nc.tensor.matmul(k.ps[:, g + 1, :], pT[:, c, t * P:(t + 1) * P], wp[:, c, half],
                                         start=(c == 0), stop=(c == PC - 1))
                    for c in range(DC):
                        last = nc.tensor.matmul(k.ps[:, g, :], k.hT[:, c, t * P:(t + 1) * P], wg[:, c, half],
                                                start=(c == 0), stop=(c == DC - 1))
                    last.then_inc(multiplied, 1)

        @block.scalar
        def _(act):
            for i in range(2 * NT):
                act.wait_ge(multiplied, i + 1)
                nc.scalar.activation(sig[:, i % 3, :], k.ps[:, 2 * (i % 3), :], ACT.Sigmoid).then_inc(sig_done, 1)

        @block.vector
        def _(dve):
            dve.wait_ge(turned, 1)
            nc.vector.tensor_copy(pT[:], k.ps[:, 6:8, :]).then_inc(pT_ready, 1)
            for n in (0, 1):
                for t in range(NT):
                    i = n * NT + t
                    dve.wait_ge(sig_done, i + 1)
                    nc.vector.tensor_tensor(part[:, i % 3, :], sig[:, i % 3, :], k.ps[:, 2 * (i % 3) + 1, :],
                                            ALU.mult).then_inc(part_done, 1)
                    dve.wait_ge(part_done, i + 1)
                    xs = k.x[:, t, n * 512:(n + 1) * 512]
                    nc.vector.tensor_tensor(xs, xs, part[:, i % 3, :], ALU.add)



WINDOW_HEADS, WINDOW_GROUPS = 4, ((128, 1), (512, 4), (2048, 16))
BLOCK_HEADS = 8
BIAS_HEADS = WINDOW_HEADS * len(WINDOW_GROUPS) + BLOCK_HEADS
BUCKETS = 32
LINE = S + P


def bias_lines(k, rel_bias, lines):
    nc = k.nc
    with ExitStack() as ctx:
        def sb(name, shape):
            return ctx.enter_context(nc.sbuf_tensor("bl_" + name, shape, F32))

        table, hot, hidden = sb("table", [BUCKETS, BIAS_HEADS]), sb("hot", [BUCKETS, LINE]), sb("hidden", [BIAS_HEADS, LINE])
        line = sb("line", [BIAS_HEADS, LINE])
        landed, multiplied, line_ready, stored = sems(k, ctx, "bl_landed bl_multiplied bl_line_ready bl_stored")
        block = ctx.enter_context(nc.Block())
        half = LINE // 2

        @block.sync
        def _(sp):
            sp.dma_start(table[:], rel_bias).then_inc(landed, 16)
            sp.dma_start(hot[:], k.t["c_bucket_hot"]).then_inc(landed, 16)
            sp.dma_start(hidden[:], k.t["c_hidden"]).then_inc(landed, 16)
            sp.wait_ge(line_ready, 2)
            sp.dma_start(lines, line[:].unsqueeze(1).to_broadcast([BIAS_HEADS, P, LINE])).then_inc(stored, 16)
            sp.wait_ge(stored, 16)

        @block.tensor
        def _(pe):
            pe.wait_ge(landed, 48)
            for n in (0, 1):
                nc.tensor.matmul(k.ps[0:BIAS_HEADS, n, 0:half], table[:], hot[:, n * half:(n + 1) * half], start=True,
                                 stop=True).then_inc(multiplied, 1)

        @block.vector
        def _(dve):
            for n in (0, 1):
                dve.wait_ge(multiplied, n + 1)
                part = slice(n * half, (n + 1) * half)
                nc.vector.tensor_tensor(line[:, part], k.ps[0:BIAS_HEADS, n, 0:half], hidden[:, part],
                                        ALU.add).then_inc(line_ready, 1)


def load_bias_tables(k, tag, lines, first, count, tables):
    nc = k.nc
    with ExitStack() as ctx:
        (landed,) = sems(k, ctx, tag + "_landed")
        block = ctx.enter_context(nc.Block())

        @block.sync
        def _(sp):
            with nc.allow_non_contiguous_dma(reason="rows overlap"):
                for h in range(count):
                    src = bass.AP(lines.tensor, (first + h) * P * LINE + P - 1, [[LINE - 1, P], [1, S]])
                    sp.dma_start(tables[:, h, :], src).then_inc(landed, 16)
            sp.wait_ge(landed, 16 * count)



def biased_attention(k, tag, w_in, groups, banded, pairs, tables, yT):
    nc = k.nc
    ng = len(groups)
    w = rows_pc(w_in)
    slots = [[k.slot((3 * g + n) * DC * P, DC, P) for n in range(3)] for g in range(ng)]

    def span(g, t):
        return max(0, t - 1) if banded and g == 0 else 0

    steps = [(h, t) for h in (0, 1) for t in range(NT)]
    widths = [sum((t + 1 - span(g, t)) * P for g in range(ng)) for _, t in steps]
    widest = max(widths)
    s_base = (lambda n: 0) if ng > 1 else (lambda n: n % 2)
    t_base = (lambda n: 3) if ng > 1 else (lambda n: 3 + n % 2)
    with ExitStack() as ctx:
        def sb(name, shape):
            return ctx.enter_context(nc.sbuf_tensor(tag + "_" + name, shape, F32))

        qT, kT, v = sb("qT", [P, ng, S]), sb("kT", [P, ng, S]), sb("v", [P, ng, NT, P])
        bias = sb("bias", [P, ng, 2, S])
        probs, probsT = sb("probs", [P, 2, widest]), sb("probsT", [P, 2, widest])
        maxima, neg_max, sums = sb("maxima", [P, 8, ng]), sb("neg_max", [P, 8]), sb("sums", [P, 8])
        names = ("w_landed bias_landed projected q_ready k_ready v_ready s_done biased max_ready exp_done inverted "
                 "normed turned probsT_ready pv_done y_out wait_kept")
        sem = dict(zip(names.split(), sems(k, ctx, " ".join(tag + "_" + n for n in names.split()))))
        block = ctx.enter_context(nc.Block())

        @block.sync
        def _(sp):
            def load_weights(col):
                for g, (oq, ok, ov, _) in enumerate(groups):
                    for dst, off in zip(slots[g], (oq, ok, ov)):
                        sp.dma_start(dst, w[:, :, bass.ds(off + col, P)]).then_inc(sem["w_landed"], 16)

            def load_bias(it):
                for g, (_, _, _, first) in enumerate(groups):
                    sp.dma_start(bias[:, g, :, :], tables[:, bass.ds(first + 2 * it, 2), :]).then_inc(sem["bias_landed"], 16)

            load_weights(0)
            load_bias(0)
            with sp.Fori(1, pairs) as it:
                sp.wait_ge(sem["projected"], it * (3 * ng))
                load_weights(it * P)
                sp.wait_ge(sem["biased"], it * (8 * ng))
                load_bias(it)

        @block.tensor
        def _(pe):
            def scores(it, n):
                h, t = steps[n]
                half = slice(64 * h, 64 * h + 64)
                for g in range(ng):
                    k0 = span(g, t) * P
                    last = nc.tensor.matmul(k.ps[:, s_base(n) + g, 0:(t + 1) * P - k0], qT[half, g, t * P:(t + 1) * P],
                                            kT[half, g, k0:(t + 1) * P], start=True, stop=True)
                last.then_inc(sem["s_done"], 1)

            with pe.Fori(0, pairs) as it:
                pe.wait_ge(sem["w_landed"], it * (48 * ng) + 48 * ng)
                for g in range(ng):
                    b = 3 * (g % 2)
                    if g >= 2:
                        pe.wait_ge(sem["q_ready"], it * ng + (g - 1))
                        pe.wait_ge(sem["k_ready"], it * ng + (g - 1))
                        pe.wait_ge(sem["v_ready"], it * ng + (g - 1))
                    project_pair(nc, k, k.hT, *slots[g], (b, b + 1, b + 2), sem["projected"])
                for name in ("q_ready", "k_ready", "v_ready"):
                    pe.wait_ge(sem[name], it * ng + ng)
                scores(it, 0)
                for n in range(8):
                    h, t = steps[n]
                    if n < 7:
                        if ng > 1 or n >= 1:
                            pe.wait_ge(sem["biased"], it * (8 * ng) + ng * (n + 1 if ng > 1 else n))
                        scores(it, n + 1)
                    pe.wait_ge(sem["normed"], it * 8 + (n + 1))
                    for b in range(widths[n] // P):
                        last = nc.tensor.transpose(k.ps[:, t_base(n) + b // 4, (b % 4) * P:(b % 4 + 1) * P],
                                                   probs[:, n % 2, b * P:(b + 1) * P], k.ident[:])
                    last.then_inc(sem["turned"], 1)
                    if n == 0:
                        pe.wait_ge(sem["y_out"], it + 1)
                    pe.wait_ge(sem["probsT_ready"], it * 8 + (n + 1))
                    keys = [(g, kt) for g in range(ng) for kt in range(span(g, t), t + 1)]
                    for b, (g, kt) in enumerate(keys):
                        last = nc.tensor.matmul(k.ps[64 * h:64 * h + 64, 6, t * P:(t + 1) * P],
                                                v[:, g, kt, 64 * h:64 * h + 64], probsT[:, n % 2, b * P:(b + 1) * P],
                                                start=(b == 0), stop=(b == len(keys) - 1))
                last.then_inc(sem["pv_done"], 1)

        @block.scalar
        def _(act):
            act.sem_inc(sem["y_out"], 1)
            with act.Fori(0, pairs) as it:
                for g in range(ng):
                    act.wait_ge(sem["projected"], it * (3 * ng) + (3 * g + 1))
                    nc.scalar.activation(qT[:, g, :], k.ps[:, 3 * (g % 2), :], ACT.Copy, scale=SCALE)\
                        .then_inc(sem["q_ready"], 1)
                    act.wait_ge(sem["projected"], it * (3 * ng) + (3 * g + 2))
                    nc.scalar.activation(kT[:, g, :], k.ps[:, 3 * (g % 2) + 1, :], ACT.Copy).then_inc(sem["k_ready"], 1)

                def exponential(n):
                    act.wait_ge(sem["max_ready"], it * 8 + (n + 1))
                    a = probs[:, n % 2, 0:widths[n]]
                    nc.scalar.activation(a, a, ACT.Exp, bias=neg_max[:, n:n + 1],
                                         accum_out=sums[:, n:n + 1]).then_inc(sem["exp_done"], 1)

                exponential(0)
                for n in range(8):
                    if n < 7:
                        exponential(n + 1)
                    act.wait_ge(sem["turned"], it * 8 + (n + 1))
                    for b in range(0, widths[n], 512):
                        m = min(512, widths[n] - b)
                        last = nc.scalar.activation(probsT[:, n % 2, b:b + m], k.ps[:, t_base(n) + b // 512, 0:m], ACT.Copy)
                    last.then_inc(sem["probsT_ready"], 1)
                act.wait_ge(sem["pv_done"], it + 1)
                nc.scalar.activation(yT[:, it, :], k.ps[:, 6, :], ACT.Copy).then_inc(sem["y_out"], 1)

        @block.vector
        def _(dve):
            with dve.Fori(0, pairs) as it:
                for g in range(ng):
                    dve.wait_ge(sem["projected"], it * (3 * ng) + (3 * g + 3))
                    nc.vector.tensor_copy(v[:, g, :, :], k.ps[:, 3 * (g % 2) + 2, :].rearrange("p (t n) -> p t n", t=NT))\
                        .then_inc(sem["v_ready"], 1)
                dve.wait_ge(sem["bias_landed"], it * (16 * ng) + 16 * ng)

                def biased(n):
                    h, t = steps[n]
                    dve.wait_ge(sem["s_done"], it * 8 + (n + 1))
                    dve.sem_inc(sem["wait_kept"], 1)
                    at = 0
                    for g in range(ng):
                        k0 = span(g, t) * P
                        m = (t + 1) * P - k0
                        nc.vector.tensor_tensor_reduce(out=probs[:, n % 2, at:at + m], in0=k.ps[:, s_base(n) + g, 0:m],
                                                       in1=bias[:, g, h, S - m:S], scale=1.0, scalar=NEG,
                                                       op0=ALU.add, op1=ALU.max,
                                                       accum_out=maxima[:, n, g:g + 1]).then_inc(sem["biased"], 1)
                        at += m
                    dve.wait_ge(sem["biased"], it * (8 * ng) + ng * (n + 1))
                    nc.vector.tensor_reduce(out=neg_max[:, n:n + 1], in_=maxima[:, n, :], axis=AX.X, op=ALU.max,
                                            negate=True).then_inc(sem["max_ready"], 1)

                biased(0)
                for n in range(8):
                    if n < 7:
                        biased(n + 1)
                    dve.wait_ge(sem["exp_done"], it * 8 + (n + 1))
                    nc.vector.reciprocal(sums[:, n:n + 1], sums[:, n:n + 1]).then_inc(sem["inverted"], 1)
                    dve.wait_ge(sem["inverted"], it * 8 + (n + 1))
                    a = probs[:, n % 2, 0:widths[n]]
                    nc.vector.tensor_scalar(a, a, sums[:, n:n + 1], None, ALU.mult).then_inc(sem["normed"], 1)



TAPS = 4
LRU_C = 8.0


def recurrence(k, w_in, off_x, off_g, conv_w, conv_b, w_a, b_a, w_x, b_x, lam, yT):
    nc = k.nc
    C = 4
    w = rows_pc(w_in)
    with ExitStack() as ctx:
        def sb(name, shape):
            return ctx.enter_context(nc.sbuf_tensor("rg_" + name, shape, F32))

        wx, wg = k.slot(0, DC, C * P), k.slot(DC * C * P, DC, C * P)
        diag_a, diag_x = sb("diag_a", [P, C, P]), sb("diag_x", [P, C, P])
        taps, bias = sb("taps", [P, TAPS, C]), sb("bias", [P, 4, C])
        sp_t = sb("sp_t", [P, 6, C])
        xp, xc = sb("xp", [P, C, S + TAPS - 1]), sb("xc", [P, C, S])
        mag, inp, tanh_t, recip, gate = (sb(n, [P, C, S]) for n in ("mag", "inp", "tanh_t", "recip", "gate"))
        names = ("wx wg small blocks zeroed x_done g_done xp_ready conv gates_done r_ready i_ready softplus lam_exp link "
                 "mag_ready tanh_done log_done recip_done a_ready ratio_ready root_done gelu_done")
        sem = dict(zip(names.split(), sems(k, ctx, " ".join("rg_" + n for n in names.split()))))
        block = ctx.enter_context(nc.Block())

        @block.sync
        def _(sp):
            sp.dma_start(wx, w[:, :, off_x:off_x + C * P]).then_inc(sem["wx"], 16)
            sp.dma_start(wg, w[:, :, off_g:off_g + C * P]).then_inc(sem["wg"], 16)
            with nc.allow_non_contiguous_dma(reason="one word per channel"):
                for tap in range(TAPS):
                    sp.dma_start(taps[:, tap, :], conv_w[tap].rearrange("(c p) -> p c", p=P)).then_inc(sem["small"], 16)
                for n, b in enumerate((conv_b, b_a, b_x, lam)):
                    sp.dma_start(bias[:, n, :], b.rearrange("(c p) -> p c", p=P)).then_inc(sem["small"], 16)
            sp.wait_ge(sem["zeroed"], 1)
            for dst, src in ((diag_a, w_a), (diag_x, w_x)):
                for h in (0, 1):
                    half = slice(64 * h, 64 * h + 64)
                    sp.dma_start(dst[half, :, half], src[h::2].rearrange("n d e -> d n e")).then_inc(sem["blocks"], 16)

        @block.tensor
        def _(pe):
            for name, wt, base, done in (("wx", wx, 0, "x_done"), ("wg", wg, C, "g_done")):
                pe.wait_ge(sem[name], 16)
                for c in range(C):
                    for d in range(DC):
                        last = nc.tensor.matmul(k.ps[:, base + c, :], wt[:, d, c * P:(c + 1) * P], k.hT[:, d, :],
                                                start=(d == 0), stop=(d == DC - 1))
                    last.then_inc(sem[done], 1)
            pe.wait_ge(sem["blocks"], 64)
            pe.wait_ge(sem["conv"], C * TAPS)
            pe.wait_ge(sem["gelu_done"], C)
            for c in range(C):
                nc.tensor.matmul(k.ps[:, c, :], diag_a[:, c, :], xc[:, c, :], start=True, stop=True)
                nc.tensor.matmul(k.ps[:, C + c, :], diag_x[:, c, :], xc[:, c, :], start=True,
                                 stop=True).then_inc(sem["gates_done"], 1)

        @block.scalar
        def _(act):
            A = nc.scalar.activation
            act.wait_ge(sem["small"], 16 * 8)
            act.wait_ge(sem["link"], 1)
            A(sp_t[:, 1, :], sp_t[:, 0, :], ACT.Exp, scale=-1.0).then_inc(sem["lam_exp"], 1)
            for c in range(C):
                act.wait_ge(sem["x_done"], c + 1)
                A(xp[:, c, TAPS - 1:], k.ps[:, c, :], ACT.Copy).then_inc(sem["xp_ready"], 1)
            for c in range(C):
                act.wait_ge(sem["g_done"], c + 1)
                A(gate[:, c, :], k.ps[:, C + c, :], ACT.Gelu_apprx_tanh).then_inc(sem["gelu_done"], 1)
            for c in range(C):
                act.wait_ge(sem["gates_done"], c + 1)
                A(mag[:, c, :], k.ps[:, c, :], ACT.Sigmoid, bias=bias[:, 1, c:c + 1]).then_inc(sem["r_ready"], 1)
                A(inp[:, c, :], k.ps[:, C + c, :], ACT.Sigmoid, bias=bias[:, 2, c:c + 1]).then_inc(sem["i_ready"], 1)
            for c in range(C):
                act.wait_ge(sem["mag_ready"], c + 1)
                A(tanh_t[:, c, :], mag[:, c, :], ACT.Tanh).then_inc(sem["tanh_done"], 1)
            act.preload_act_table_set("natural_log_exp_and_others")
            for c in range(C):
                act.wait_ge(sem["tanh_done"], c + 1)
                A(recip[:, c, :], tanh_t[:, c, :], ACT.Ln, bias=1.0).then_inc(sem["log_done"], 1)
            for c in range(C):
                act.wait_ge(sem["log_done"], c + 1)
                A(recip[:, c, :], recip[:, c, :], ACT.Exp, scale=-1.0).then_inc(sem["recip_done"], 1)
                A(mag[:, c, :], mag[:, c, :], ACT.Exp, scale=-1.0).then_inc(sem["a_ready"], 1)
            for c in range(C):
                act.wait_ge(sem["ratio_ready"], c + 1)
                A(recip[:, c, :], recip[:, c, :], ACT.Sqrt, scale=2.0).then_inc(sem["root_done"], 1)

        @block.vector
        def _(dve):
            V = nc.vector
            done = [0]

            def link(*instructions):
                for ins in instructions:
                    ins.then_inc(sem["link"], 1)
                    done[0] += 1
                dve.wait_ge(sem["link"], done[0])

            dve.wait_ge(sem["small"], 16 * 8)
            link(V.scalar_tensor_tensor(out=sp_t[:, 0, :], in0=bias[:, 3, :], scalar=-1.0, in1=bias[:, 3, :],
                                        op0=ALU.mult, op1=ALU.max))
            dve.wait_ge(sem["lam_exp"], 1)
            link(V.tensor_scalar(sp_t[:, 2, :], sp_t[:, 1, :], 2.0, None, ALU.add))
            link(V.reciprocal(sp_t[:, 2, :], sp_t[:, 2, :]))
            link(V.tensor_tensor(sp_t[:, 2, :], sp_t[:, 2, :], sp_t[:, 1, :], ALU.mult))
            link(V.tensor_tensor(sp_t[:, 3, :], sp_t[:, 2, :], sp_t[:, 2, :], ALU.mult),
                 V.memset(sp_t[:, 4, :], 1.0 / 17))
            for odd in (15, 13, 11, 9, 7, 5, 3, 1):
                link(V.tensor_tensor(sp_t[:, 4, :], sp_t[:, 4, :], sp_t[:, 3, :], ALU.mult))
                link(V.tensor_scalar(sp_t[:, 4, :], sp_t[:, 4, :], 1.0 / odd, None, ALU.add))
            link(V.tensor_tensor(sp_t[:, 4, :], sp_t[:, 4, :], sp_t[:, 2, :], ALU.mult),
                 V.tensor_scalar(sp_t[:, 5, :], bias[:, 3, :], -1.0, 0.0, ALU.mult, ALU.max))
            link(V.scalar_tensor_tensor(out=sp_t[:, 5, :], in0=sp_t[:, 4, :], scalar=2.0, in1=sp_t[:, 5, :],
                                        op0=ALU.mult, op1=ALU.add))
            link(V.tensor_scalar(sp_t[:, 5, :], sp_t[:, 5, :], LRU_C, None, ALU.mult))
            dve.sem_inc(sem["softplus"], 1)
            dve.wait_ge(sem["zeroed"], 1)
            for c in range(C):
                dve.wait_ge(sem["xp_ready"], c + 1)
                V.tensor_scalar(xc[:, c, :], xp[:, c, 0:S], taps[:, 0, c:c + 1], bias[:, 0, c:c + 1], ALU.mult,
                                ALU.add).then_inc(sem["conv"], 1)
                for tap in range(1, TAPS):
                    dve.wait_ge(sem["conv"], TAPS * c + tap)
                    V.scalar_tensor_tensor(out=xc[:, c, :], in0=xp[:, c, tap:tap + S], scalar=taps[:, tap, c:c + 1],
                                           in1=xc[:, c, :], op0=ALU.mult, op1=ALU.add).then_inc(sem["conv"], 1)
            for c in range(C):
                dve.wait_ge(sem["r_ready"], c + 1)
                V.tensor_scalar(mag[:, c, :], mag[:, c, :], sp_t[:, 5, c:c + 1], None, ALU.mult).then_inc(sem["mag_ready"], 1)
                dve.wait_ge(sem["i_ready"], c + 1)
                link(V.tensor_tensor(inp[:, c, :], inp[:, c, :], xc[:, c, :], ALU.mult))
            for c in range(C):
                dve.wait_ge(sem["recip_done"], c + 1)
                V.tensor_tensor(recip[:, c, :], recip[:, c, :], tanh_t[:, c, :], ALU.mult).then_inc(sem["ratio_ready"], 1)
            for c in range(C):
                dve.wait_ge(sem["root_done"], c + 1)
                dve.wait_ge(sem["a_ready"], c + 1)
                link(V.tensor_tensor(inp[:, c, :], inp[:, c, :], recip[:, c, :], ALU.mult))
                link(V.tensor_tensor_scan(xc[:, c, :], mag[:, c, :], inp[:, c, :], 0.0, ALU.mult, ALU.add))
                V.tensor_tensor(yT[:, c, :], xc[:, c, :], gate[:, c, :], ALU.mult)

        @block.gpsimd
        def _(pool):
            nc.gpsimd.memset(xp[:, :, 0:TAPS - 1], 0.0)
            nc.gpsimd.memset(diag_a[:], 0.0)
            nc.gpsimd.memset(diag_x[:], 0.0)
            pool.drain().then_inc(sem["zeroed"], 1)



FFN = -(-8 * D // (3 * 256)) * 256
FC = FFN // P


def feed_forward(k, w_gu, w_down):
    nc = k.nc
    cols, U = 256, 2
    blocks = FFN // cols
    w = rows_pc(w_gu)
    slots = [(k.slot(u * 2 * DC * cols, DC, cols), k.slot((2 * u + 1) * DC * cols, DC, cols)) for u in range(U)]
    R = 8
    down_at = [k.slot(n * D, 1, D) for n in range(R)]
    with ExitStack() as ctx:
        hiddenT = ctx.enter_context(nc.sbuf_tensor("ff_hiddenT", [P, FC, S], F32))
        silu = ctx.enter_context(nc.sbuf_tensor("ff_silu", [P, 4, S], F32))
        with ExitStack() as up:
            landed0, landed1, multiplied, silu_done, hidden_ready = sems(
                k, up, "ff_landed0 ff_landed1 ff_multiplied ff_silu_done ff_hidden_ready")
            landed = (landed0, landed1)
            block = up.enter_context(nc.Block())

            @block.sync
            def _(sp):
                def step(it, u):
                    wait(sp, multiplied, it * (2 * U) + 2 * (u - 1))
                    col = (it * U + u) * cols
                    sp.dma_start(slots[u][0], w[:, :, bass.ds(col, cols)]).then_inc(landed[u], 16)
                    sp.dma_start(slots[u][1], w[:, :, bass.ds(col + FFN, cols)]).then_inc(landed[u], 16)

                every(sp, blocks, U, step)

            @block.tensor
            def _(pe):
                def step(it, u):
                    pe.wait_ge(landed[u], it * 32 + 32)
                    for m in (0, 1):
                        i = 2 * u + m
                        wait(pe, hidden_ready, it * 4 + (i - 3))
                        for part in (0, 1):
                            for c in range(DC):
                                last = nc.tensor.matmul(k.ps[:, 2 * i + part, :], slots[u][part][:, c, m * P:(m + 1) * P],
                                                        k.hT[:, c, :], start=(c == 0), stop=(c == DC - 1))
                        last.then_inc(multiplied, 1)

                every(pe, blocks, U, step)

            @block.scalar
            def _(act):
                def step(it, u):
                    for m in (0, 1):
                        i = 2 * u + m
                        act.wait_ge(multiplied, it * 4 + (i + 1))
                        nc.scalar.activation(silu[:, i, :], k.ps[:, 2 * i, :], ACT.Silu).then_inc(silu_done, 1)

                every(act, blocks, U, step)

            @block.vector
            def _(dve):
                def step(it, u):
                    for m in (0, 1):
                        i = 2 * u + m
                        dve.wait_ge(silu_done, it * 4 + (i + 1))
                        nc.vector.tensor_tensor(hiddenT[:, bass.ds(it * 4 + i, 1), :].rearrange("p a n -> p (a n)"),
                                                silu[:, i, :], k.ps[:, 2 * i + 1, :], ALU.mult).then_inc(hidden_ready, 1)

                every(dve, blocks, U, step)

        with ExitStack() as down:
            landed = sems(k, down, " ".join(f"fd_landed{n}" for n in range(R)))
            used, added = sems(k, down, "fd_used fd_added")
            block = down.enter_context(nc.Block())

            @block.sync
            def _(sp):
                for c in range(FC):
                    wait(sp, used, c - R + 1)
                    sp.dma_start(down_at[c % R][:, 0, :], w_down[c * P:(c + 1) * P, :]).then_inc(landed[c % R], 16)

            @block.tensor
            def _(pe):
                for c in range(FC):
                    pe.wait_ge(landed[c % R], 16 * (c // R + 1))
                    for t in range(NT):
                        for n in (0, 1):
                            last = nc.tensor.matmul(k.ps[:, 2 * t + n, :], hiddenT[:, c, t * P:(t + 1) * P],
                                                    down_at[c % R][:, 0, n * 512:(n + 1) * 512],
                                                    start=(c == 0), stop=(c == FC - 1))
                    last.then_inc(used, 1)

            @block.vector
            def _(dve):
                dve.wait_ge(used, FC)
                for t in range(NT):
                    nc.vector.tensor_tensor(k.x[:, t, :], k.x[:, t, :], k.ps[:, 2 * t:2 * t + 2, :].rearrange("p a n -> p (a n)"),
                                            ALU.add).then_inc(added, 1)


def final_norm(k, tag, gain, out=None):
    nc = k.nc
    with ExitStack() as ctx:
        g = ctx.enter_context(nc.sbuf_tensor(tag + "_g", [P, D], F32))
        ss = ctx.enter_context(nc.sbuf_tensor(tag + "_ss", [P, NT], F32))
        landed, squares, mean_ready, root_ready, rstd_ready, normed, stored = sems(
            k, ctx, " ".join(tag + n for n in "_landed _squares _mean _root _rstd _normed _stored".split()))
        block = ctx.enter_context(nc.Block())

        @block.sync
        def _(sp):
            sp.dma_start(g[:], gain.partition_broadcast(P)).then_inc(landed, 16)
            if out is not None:
                for t in range(NT):
                    sp.wait_ge(normed, t + 1)
                    sp.dma_start(out[0, t * P:(t + 1) * P, :], k.x[:, t, :]).then_inc(stored, 16)
                sp.wait_ge(stored, 16 * NT)

        @block.scalar
        def _(act):
            for t in range(NT):
                nc.scalar.activation(k.ps[:, 2 * t:2 * t + 2, :], k.x[:, t, :].rearrange("p (a n) -> p a n", a=2),
                                     ACT.Square, accum_out=ss[:, t:t + 1]).then_inc(squares, 1)
            act.wait_ge(mean_ready, 1)
            nc.scalar.activation(ss[:], ss[:], ACT.Sqrt).then_inc(root_ready, 1)

        @block.vector
        def _(dve):
            dve.wait_ge(squares, NT)
            nc.vector.tensor_scalar(ss[:], ss[:], 1.0 / D, EPS, ALU.mult, ALU.add).then_inc(mean_ready, 1)
            dve.wait_ge(root_ready, 1)
            nc.vector.reciprocal(ss[:], ss[:]).then_inc(rstd_ready, 1)
            dve.wait_ge(rstd_ready, 1)
            dve.wait_ge(landed, 16)
            for t in range(NT):
                nc.vector.scalar_tensor_tensor(out=k.x[:, t, :], in0=k.x[:, t, :], scalar=ss[:, t:t + 1], in1=g[:],
                                               op0=ALU.mult, op1=ALU.mult).then_inc(normed, 1)


def second_layer(k, t, lines):
    nc = k.nc
    w_in = t["w_in_2"][0]
    with ExitStack() as mix:
        yaT = mix.enter_context(nc.sbuf_tensor("ya2_transposed", [P, 2, S], F32))
        ybT = mix.enter_context(nc.sbuf_tensor("yb2_transposed", [P, 4, S], F32))
        ycT = mix.enter_context(nc.sbuf_tensor("yc2_transposed", [P, 4, S], F32))
        bias_lines(k, t["rel_bias_2"], lines)
        norm_transpose(k, "mix2", t["g_mix_2"][0])
        width = WINDOW_HEADS * HD
        window = len(WINDOW_GROUPS) * width
        groups = tuple((g * width, window + g * width, 2 * window + g * width, g * WINDOW_HEADS)
                       for g in range(len(WINDOW_GROUPS)))
        with ExitStack() as stage:
            tables = stage.enter_context(nc.sbuf_tensor("window_bias", [P, BIAS_HEADS - BLOCK_HEADS, S], F32))
            load_bias_tables(k, "wt", lines, 0, BIAS_HEADS - BLOCK_HEADS, tables)
            biased_attention(k, "wa", w_in, groups, True, WINDOW_HEADS // 2, tables, yaT)
        at = 3 * window
        recurrence(k, w_in, at, at + 512, t["conv_w_2"][0], t["conv_b_2"][0], t["lru_wa_2"][0], t["lru_ba_2"][0],
                   t["lru_wx_2"][0], t["lru_bx_2"][0], t["lru_lam_2"][0], ybT)
        at += 1024
        assert S // 256 - 1 <= 3
        with ExitStack() as stage:
            tables = stage.enter_context(nc.sbuf_tensor("block_bias", [P, BLOCK_HEADS, S], F32))
            load_bias_tables(k, "bt", lines, BIAS_HEADS - BLOCK_HEADS, BLOCK_HEADS, tables)
            biased_attention(k, "ba", w_in, ((at, at + 512, at + 1024, 0),), False, BLOCK_HEADS // 2, tables, ycT)
        at += 1536
        mergedT = mix.enter_context(nc.sbuf_tensor("merged2_transposed", [P, DC, S], F32))
        merge(k, "mg2", w_in, (at, at + D, at + 2 * D),
              ((t["p_a_2"][0], yaT, 2), (t["p_b_2"][0], ybT, 4), (t["p_c_2"][0], ycT, 4)), mergedT)
        project_and_add(k, "op2", t["w_out_2"][0], mergedT)
    norm_transpose(k, "ffn2", t["g_ffn_2"][0])
    feed_forward(k, t["w_gu_2"][0], t["w_down_2"][0])



IN = {}


def first_layer(k, t, i, scratch):
    nc = k.nc
    xn_rows, y_rows = scratch
    with ExitStack() as ctx:
        with ExitStack() as mix:
            mergedT = mix.enter_context(nc.sbuf_tensor("merged_transposed", [P, DC, S], F32))
            yaT = mix.enter_context(nc.sbuf_tensor("ya_transposed", [P, 4, S], F32))
            ybT = mix.enter_context(nc.sbuf_tensor("yb_transposed", [P, 4, S], F32))
            norm_transpose(k, "mix", t["g_mix"][i])
            w_in = t["w_in"][i]
            stick_breaking(k, w_in, 0, 512, 1024, yaT)
            differential(k, w_in, 1536, 2048, 2560, [t[n][i] for n in ("lam_q1", "lam_k1", "lam_q2", "lam_k2")],
                         t["g_subln"][i], t["c_lam_init"][i], t["c_keep"][i], k.cosT, k.sinT, ybT)
            merge(k, "mg", w_in, (3072, 4096), ((t["w_br_a"][i], yaT, 4), (t["w_br_b"][i], ybT, 4)), mergedT)
            project_and_add(k, "op", t["w_o"][i], mergedT)
        with ExitStack() as moe:
            r = Routing(nc, moe)
            norm_transpose(k, "ffn", t["g_ffn"][i], xn_rows)
            route(k, "rt", r, t["w_router_group"][i], t["b_router_group"][i], t["w_router_expert"][i],
                  t["b_router_expert"][i], t["g_ffn"][i])
            weights = (t["w_exp_gate"], t["w_exp_up"], t["w_exp_down"])
            experts(k, "ex", r, i, EXPERTS, False, xn_rows, y_rows, *weights)
            spilled = nc.values_load(r.spill_expert[0:1, SPILL:SPILL + 1], min_val=0, max_val=SPILL)
            with nc.If(spilled > 0):
                experts(k, "sp", r, i, SPILL, True, xn_rows, y_rows, *weights)
            combine_experts(k, "cb", r, y_rows)
        norm_transpose(k, "ple", t["g_ple"][i])
        embed_per_layer(k, "pe", t["p"][i, 0], t["w_ple"][i], t["w_ple_gate"][i])


def program(nc, t, out, stop=None):
    with ExitStack() as ctx:
        k = Core(nc, ctx)
        k.t = t
        load_start(k, t)
        k.cosT = ctx.enter_context(nc.sbuf_tensor("cos_t", [P, S], F32))
        k.sinT = ctx.enter_context(nc.sbuf_tensor("sin_t", [P, S], F32))
        rotary_tables(k, t, k.cosT, k.sinT)
        xn_rows = nc.dram_tensor("xn_rows", [S, D], F32)
        y_rows = nc.dram_tensor("y_rows", [2 * S, D], F32)
        clear_sems(k)
        with nc.Fori(0, DEPTH) as i:
            first_layer(k, t, i, (xn_rows.ap(), y_rows.ap()))
            clear_sems(k)
        if stop == 1:
            return
        final_norm(k, "fn", t["g_final"])
        second_layer(k, t, nc.dram_tensor("bias_lines", [BIAS_HEADS, P, LINE], F32).ap())
        final_norm(k, "fn2", t["g_final_2"], out)


def constants():
    f = np.float32
    r = np.arange(P)
    half = 8
    swap = np.zeros((P, P), f)
    freq = np.zeros((P, 1), f)
    inv = (f(500000.0) ** (-np.arange(0, 16, 2, dtype=f) / f(16))).astype(f)
    for head in (0, 64):
        for i in range(half):
            swap[head + half + i, head + i] = -1
            swap[head + i, head + half + i] = 1
            freq[head + i] = freq[head + half + i] = inv[i]
    lam_init = np.array([[0.8 - 0.6 * math.exp(-0.3 * i)] for i in range(DEPTH)], f)
    dist = S - 1 - np.arange(LINE)
    far = np.maximum(dist, 1).astype(f)
    exact = BUCKETS // 2
    large = exact + (np.log(far / exact).astype(f) / f(math.log(2048 / exact)) * f(BUCKETS - exact)).astype(np.int32)
    bucket = np.where(dist < exact, np.maximum(dist, 0), np.minimum(large, BUCKETS - 1))
    hot = (np.arange(BUCKETS)[:, None] == bucket[None, :]).astype(f)
    hidden = np.zeros((BIAS_HEADS, LINE), f)
    for g, (window, dilation) in enumerate(WINDOW_GROUPS):
        seen = (dist >= 0) & (dist <= window) & (dist % dilation == 0)
        hidden[g * WINDOW_HEADS:(g + 1) * WINDOW_HEADS] = np.where(seen, f(0), f(NEG))
    hidden[BIAS_HEADS - BLOCK_HEADS:] = np.where(dist >= 0, f(0), f(NEG))
    token = np.arange(S).reshape(NT, P)
    values = np.zeros((P, 8, 2), f)
    for tile in range(NT):
        for c in (0, 1):
            values[:, 2 * tile + c, 0] = token[tile] + 1
            values[:, 2 * tile + c, 1] = 2 * token[tile] + c + 1
    return {
        "c_iota": r.astype(f),
        "c_bucket_hot": hot,
        "c_hidden": hidden,
        "c_before": (r[:, None] < r[None, :]).astype(f),
        "c_slot_values": values,
        "c_ident": np.eye(P, dtype=f),
        "c_neg_tri": -(r[:, None] >= r[None, :]).astype(f),
        "c_chunk_bias": np.where((r[:, None] < 64) & (r[None, :] >= 64), f(NEG), f(0)),
        "c_rope_swap": swap,
        "c_rope_freq": freq,
        "c_lam_init": lam_init,
        "c_keep": (1.0 - lam_init.astype(np.float64)).astype(f),
        "c_strict_bias": np.where(r[:, None] < r[None, :], f(0), f(NEG)),
    }



_INPUTS = (
    "x p positions g_mix w_in lam_q1 lam_k1 lam_q2 lam_k2 g_subln w_br_a w_br_b w_o g_ffn w_router_group b_router_group "
    "w_router_expert b_router_expert w_exp_gate w_exp_up w_exp_down g_ple w_ple w_ple_gate g_final rel_bias_2 g_mix_2 "
    "w_in_2 conv_w_2 conv_b_2 lru_wa_2 lru_ba_2 lru_wx_2 lru_bx_2 lru_lam_2 p_a_2 p_b_2 p_c_2 w_out_2 g_ffn_2 w_gu_2 "
    "w_down_2 g_final_2").split()


def kernel(**inputs):
    import concourse.bacc as bacc
    from concourse.bass_utils import run_bass_kernel_spmd

    nc = bacc.Bacc("TRN2", target_bir_lowering=False, num_devices=1)
    arrays, t = {}, {}
    given = {name: np.ascontiguousarray(inputs[name]) for name in _INPUTS}
    for name, a in {**given, **constants()}.items():
        arrays["in_" + name] = a
        t[name] = nc.dram_tensor("in_" + name, a.shape, mybir.dt.from_np(a.dtype), kind="ExternalInput").ap()
    out = nc.dram_tensor("out_0", (1, S, D), F32, kind="ExternalOutput").ap()
    program(nc, t, out)
    r = run_bass_kernel_spmd(nc, [arrays], core_ids=[0])
    return r.results[0]["out_0"]
```

```python
from contextlib import ExitStack
import math

import numpy as np
import concourse.bass as bass
from concourse import mybir

F32 = mybir.dt.float32
I32 = mybir.dt.int32
U32 = mybir.dt.uint32
ALU = mybir.AluOpType
F32R = mybir.dt.float32r
ACT = mybir.ActivationFunctionType
AX = mybir.AxisListType

P = 128
D = 1024
S = 512
NT = S // P
DC = D // P
DEPTH = 2
EPS = 1e-6
NEG = -1e30
HD = 64
SCALE = HD ** -0.5
RING = 18432


class Core:

    def __init__(self, nc, ctx):
        def sb(name, shape, dt=F32):
            return ctx.enter_context(nc.sbuf_tensor(name, shape, dt))

        self.nc = nc
        self.used_sems = set()
        self.ps = ctx.enter_context(nc.psum_tensor("banks", [P, 8, 512], F32))
        self.x = sb("x_tokens", [P, NT, D])
        self.hT = sb("h_transposed", [P, DC, S])
        self.ident = sb("identity", [P, P])
        self.neg_tri = sb("neg_tri", [P, P])
        self.neg_ones = sb("neg_ones", [P, P])
        self.strict_bias = sb("strict_bias", [P, P])
        self.chunk_bias = sb("chunk_bias", [P, P])
        self.rope_swap = sb("rope_swap", [P, P])
        self.ring_scope = ctx.enter_context(ExitStack())
        self.ring = self.ring_scope.enter_context(nc.sbuf_tensor("weight_ring", [P, RING], F32))

    def slot(self, offset, chunks, cols):
        return self.ring[:, offset:offset + chunks * cols].rearrange("p (c n) -> p c n", c=chunks)


def sems(k, ctx, names):
    found = [ctx.enter_context(k.nc.semaphore(n)) for n in names.split()]
    assert not k.used_sems & {x.num for x in found}
    k.used_sems |= {x.num for x in found}
    return found


def clear_sems(k):
    k.nc.gpsimd.dma_reset()
    for num in sorted(k.used_sems):
        k.nc.gpsimd.sem_clear(range(num, num + 1))
    k.used_sems = set()
    k.nc.all_engine_barrier()


class Loads:

    def __init__(self, k, ctx, *groups):
        self.landed = sems(k, ctx, " ".join(name for name, _ in groups))
        self.groups = [pairs for _, pairs in groups]

    def issue(self, sp):
        for landed, pairs in zip(self.landed, self.groups):
            for dst, src in pairs:
                sp.dma_start(dst, src).then_inc(landed, 16)


def rows_pc(w):
    return w.rearrange("(p c) n -> p c n", c=DC)



def mask_low_bits(nc, dst, src):
    return nc.vector.tensor_scalar(dst.bitcast(I32), src.bitcast(I32), -4096, None, ALU.bitwise_and)


def split_product(nc, out, a, b, start, stop):
    for n, (left, right) in enumerate(((a[0], b[0]), (a[0], b[1]), (a[1], b[0]))):
        last = nc.tensor.matmul(out, left, right, start=(start and n == 0), stop=(stop and n == 2))
    return last



def load_start(k, t):
    nc = k.nc
    with ExitStack() as ctx:
        (landed,) = sems(k, ctx, "start_landed")
        block = ctx.enter_context(nc.Block())

        @block.sync
        def _(sp):
            sp.dma_start(k.ident[:], t["c_ident"]).then_inc(landed, 16)
            sp.dma_start(k.neg_tri[:], t["c_neg_tri"]).then_inc(landed, 16)
            sp.dma_start(k.x[:], t["x"].rearrange("b (t p) d -> p (b t) d", p=P)).then_inc(landed, 16)
            sp.dma_start(k.strict_bias[:], t["c_strict_bias"]).then_inc(landed, 16)
            sp.dma_start(k.chunk_bias[:], t["c_chunk_bias"]).then_inc(landed, 16)
            sp.dma_start(k.rope_swap[:], t["c_rope_swap"]).then_inc(landed, 16)
            sp.wait_ge(landed, 96)

        @block.vector
        def _(dve):
            nc.vector.memset(k.neg_ones[:], -1.0)



def norm_transpose(k, tag, gain, ahead=(), rows=None):
    nc = k.nc
    with ExitStack() as ctx:
        xn = ctx.enter_context(nc.sbuf_tensor(tag + "_xn", [P, NT, D], F32))
        ss = ctx.enter_context(nc.sbuf_tensor(tag + "_ss", [P, NT], F32))
        g = ctx.enter_context(nc.sbuf_tensor(tag + "_g", [P, DC], F32))
        gain_landed, squares, mean_ready, root_ready, rstd_ready, xn_ready, turned, stored = sems(k, ctx, " ".join(tag + s for s in
                              "_gain _squares _mean _root _rstd _xn_ready _turned _stored".split()))
        block = ctx.enter_context(nc.Block())

        @block.sync
        def _(sp):
            if rows is not None:
                sp.wait_ge(xn_ready, NT)
                sp.dma_start(rows.rearrange("(t p) d -> p t d", p=P), xn[:]).then_inc(stored, 16)
            for loads in ahead:
                loads.issue(sp)
            if rows is not None:
                sp.wait_ge(stored, 16)

        @block.scalar
        def _(act):
            nc.scalar.dma_start(g[:], gain.rearrange("(p c) -> p c", c=DC)).then_inc(gain_landed, 16)
            for t in range(NT):
                nc.scalar.activation(k.ps[:, 2 * t:2 * t + 2, :], k.x[:, t, :].rearrange("p (a n) -> p a n", a=2),
                                     ACT.Square, accum_out=ss[:, t:t + 1]).then_inc(squares, 1)
            act.wait_ge(mean_ready, 1)
            nc.scalar.activation(ss[:], ss[:], ACT.Sqrt).then_inc(root_ready, 1)
            act.wait_ge(rstd_ready, 1)
            for t in (0, 1):
                nc.scalar.activation(xn[:, t, :], k.x[:, t, :], ACT.Copy, scale=ss[:, t:t + 1]).then_inc(xn_ready, 1)

        @block.vector
        def _(dve):
            dve.wait_ge(squares, NT)
            nc.vector.tensor_scalar(ss[:], ss[:], 1.0 / D, EPS, ALU.mult, ALU.add).then_inc(mean_ready, 1)
            dve.wait_ge(root_ready, 1)
            nc.vector.reciprocal(ss[:], ss[:]).then_inc(rstd_ready, 1)
            dve.wait_ge(rstd_ready, 1)
            for t in (2, 3):
                nc.vector.tensor_scalar(xn[:, t, :], k.x[:, t, :], ss[:, t:t + 1], None, ALU.mult).then_inc(xn_ready, 1)
            dve.wait_ge(gain_landed, 16)
            for c in range(DC):
                dve.wait_ge(turned, c + 1)
                nc.vector.tensor_scalar(k.hT[:, c, :], k.ps[:, c, :], g[:, c:c + 1], None, ALU.mult)

        @block.tensor
        def _(pe):
            pe.wait_ge(xn_ready, NT)
            for c in range(DC):
                for t in range(NT):
                    last = nc.tensor.transpose(k.ps[:, c, t * P:(t + 1) * P], xn[:, t, c::DC], k.ident[:])
                last.then_inc(turned, 1)



def projection(nc, k, bank, kind, w, quantum):
    if kind < 2:
        last = nc.tensor.matmul(k.ps[:, bank, :], w[:, quantum, :], k.hT[:, quantum, :], start=(quantum == 0),
                                stop=(quantum == DC - 1))
    else:
        t, half = divmod(quantum, 2)
        for c in range(half * 4, half * 4 + 4):
            last = nc.tensor.matmul(k.ps[:, bank, t * P:(t + 1) * P], k.hT[:, c, t * P:(t + 1) * P], w[:, c, :],
                                    start=(c == 0), stop=(c == DC - 1))
    return last


def qkv_loads(k, ctx, tag, base, w_in, offs):
    slots = [k.slot(base + n * DC * P, DC, P) for n in range(len(offs))]
    loads = Loads(k, ctx, *((f"{tag}_landed{n}", [(dst, rows_pc(w_in)[:, :, off:off + P])])
                            for n, (dst, off) in enumerate(zip(slots, offs))))
    loads.slots = slots
    return loads


def spread_eighths():
    eighths = [(m, c) for m in range(3) for c in range(8)]
    return [eighths[3 * n:3 * n + 2] for n in range(8)], [eighths[3 * n + 2:3 * n + 3] for n in range(8)]


def stick_breaking(k, w_in, off_q, off_k, off_v, yT, first, ahead):
    nc = k.nc
    pairs = 4
    steps = 8 * pairs
    w = rows_pc(w_in)
    before, after = spread_eighths()
    banks = (4, 5, 6)
    with ExitStack() as ctx:
        def sb(name, shape):
            return ctx.enter_context(nc.sbuf_tensor("sb_" + name, shape, F32))

        qT, kT, v = sb("qT", [P, 2, S]), sb("kT", [P, 2, S]), sb("v", [P, 2, NT, P])
        mag = sb("mag", [P, 2, S])
        stay = sb("stay", [P, 8, S])
        prob = sb("prob", [P, 8, S])
        projected, q_ready, k_ready, v_ready, z_done, act_step, stay_done, logit_done, exp_done, \
            pv_done, y_out = sems(k, ctx, " ".join("sb_" + n for n in (
                "projected q_ready k_ready v_ready z_done act_step stay_done logit_done exp_done "
                "pv_done y_out").split()))
        block = ctx.enter_context(nc.Block())

        def place(s):
            j = 3 - s % 4
            return s % 8 // 4, j, S - P * j

        @block.sync
        def _(sp):
            ahead.issue(sp)
            with sp.Fori(1, pairs) as it:
                for n, off in enumerate((off_q, off_k, off_v)):
                    sp.wait_ge(projected, 3 * it + (n - 2))
                    sp.dma_start(first.slots[n], w[:, :, bass.ds(off + it * P, P)]).then_inc(first.landed[n], 16)

        @block.tensor
        def _(pe):
            def project(pair, part):
                for m, c in part:
                    if c == 0:
                        pe.wait_ge(first.landed[m], 16 * (pair + 1))
                        wait(pe, (q_ready, k_ready, v_ready)[m], pair)
                    last = projection(nc, k, banks[m], m, first.slots[m], c)
                    if c == 7:
                        last.then_inc(projected, 1)

            def scores(s):
                h, j, cols = place(s)
                pair = s // 8
                if s % 8 == 0:
                    pe.wait_ge(q_ready, pair + 1)
                    pe.wait_ge(k_ready, pair + 1)
                wait(pe, exp_done, s - 3)
                nc.tensor.matmul(k.ps[:, s % 4, 0:cols], kT[64 * h:64 * h + 64, pair % 2, j * P:(j + 1) * P],
                                 qT[64 * h:64 * h + 64, pair % 2, j * P:S], start=True, stop=False,
                                 skip_group_check=True)
                nc.tensor.matmul(k.ps[:, s % 4, 0:P], k.ident[:], k.strict_bias[:], start=False, stop=False,
                                 skip_group_check=True).then_inc(z_done, 1)

            def cumulate(s):
                h, j, cols = place(s)
                pe.wait_ge(stay_done, s + 1)
                for jj in range(j, NT):
                    tri = k.neg_tri if jj == j else k.neg_ones
                    last = nc.tensor.matmul(k.ps[:, s % 4, (jj - j) * P:cols], tri[:],
                                            stay[:, 4 * h + 3 - jj, jj * P:S], start=False, stop=(jj == NT - 1),
                                            skip_group_check=True)
                last.then_inc(logit_done, 1)

            def weigh(head):
                pair, h = divmod(head, 2)
                if h == 0:
                    wait(pe, y_out, pair)
                    pe.wait_ge(v_ready, pair + 1)
                pe.wait_ge(exp_done, 4 * head + 4)
                for j in range(NT):
                    last = nc.tensor.matmul(k.ps[64 * h:64 * h + 64, 7, j * P:S], v[:, pair % 2, j, 64 * h:64 * h + 64],
                                            prob[:, 4 * h + 3 - j, j * P:S], start=(j == 0), stop=(j == NT - 1),
                                            skip_group_check=True)
                last.then_inc(pv_done, 1)

            for m in range(3):
                project(0, [(m, c) for c in range(8)])
            scores(0)
            scores(1)
            for s in range(steps):
                if s + 2 < steps:
                    scores(s + 2)
                more = s // 8 + 1 < pairs
                if more:
                    project(s // 8 + 1, before[s % 8])
                cumulate(s)
                if more:
                    project(s // 8 + 1, after[s % 8])
                if s and s % 4 == 0:
                    weigh(s // 4 - 1)
            weigh(2 * pairs - 1)

        @block.scalar
        def _(act):
            def take_q(pair):
                act.wait_ge(projected, 3 * pair + 1)
                nc.scalar.activation(qT[:, pair % 2, :], k.ps[:, banks[0], :], ACT.Copy, scale=SCALE).then_inc(q_ready, 1)

            def take_result(pair):
                act.wait_ge(pv_done, 2 * pair + 2)
                nc.scalar.activation(yT[:, pair, :], k.ps[:, 7, :], ACT.Copy).then_inc(y_out, 1)

            def final(s):
                _, j, cols = place(s)
                act.wait_ge(logit_done, s + 1)
                nc.scalar.activation(prob[:, s % 8, j * P:S], k.ps[:, s % 4, 0:cols], ACT.Exp).then_inc(exp_done, 1)

            act.preload_act_table_set("natural_log_exp_and_others")
            take_q(0)
            for s in range(steps):
                _, j, cols = place(s)
                a = mag[:, s % 2, 0:cols]
                act.wait_ge(z_done, s + 1)
                wait(act, stay_done, s - 1)
                nc.scalar.activation(a, k.ps[:, s % 4, 0:cols], ACT.Abs).then_inc(act_step, 1)
                act.wait_ge(act_step, 3 * s + 1)
                nc.scalar.activation(a, a, ACT.Exp, scale=-1.0).then_inc(act_step, 1)
                act.wait_ge(act_step, 3 * s + 2)
                nc.scalar.activation(a, a, ACT.Ln, bias=1.0).then_inc(act_step, 1)
                if s:
                    final(s - 1)
                if s % 8 == 2 and s // 8 + 1 < pairs:
                    take_q(s // 8 + 1)
                if s % 8 == 1 and s > 8:
                    take_result(s // 8 - 1)
            final(steps - 1)
            take_result(pairs - 1)

        @block.vector
        def _(dve):
            def take(pair, m):
                dve.wait_ge(projected, 3 * pair + m + 1)
                if m == 1:
                    nc.vector.tensor_copy(kT[:, pair % 2, :], k.ps[:, banks[1], :]).then_inc(k_ready, 1)
                else:
                    nc.vector.tensor_copy(v[:, pair % 2, :, :], k.ps[:, banks[2], :].rearrange("p (t n) -> p t n", t=NT))\
                        .then_inc(v_ready, 1)

            take(0, 1)
            take(0, 2)
            for s in range(steps):
                _, j, cols = place(s)
                dve.wait_ge(act_step, 3 * s + 3)
                nc.vector.scalar_tensor_tensor(out=stay[:, s % 8, j * P:S], in0=k.ps[:, s % 4, 0:cols],
                                               scalar=0.0, in1=mag[:, s % 2, 0:cols],
                                               op0=ALU.max, op1=ALU.add).then_inc(stay_done, 1)
                if s // 8 + 1 < pairs and s % 8 in (5, 7):
                    take(s // 8 + 1, 1 if s % 8 == 5 else 2)



def rotary_tables(k, t, cosT, sinT):
    nc = k.nc
    two_pi = (6.28125, 0.0019353071693331003, 1.0253131677018246e-11)
    magic = 12582912.0
    lim = 3.1415925
    with ExitStack() as ctx:
        def sb(name, shape, dt=F32):
            return ctx.enter_context(nc.sbuf_tensor("rot_" + name, shape, dt))

        pos_i, freq = sb("pos_i", [P, S], I32), sb("freq", [P, 1])
        ang, turn = sb("ang", [P, S]), sb("turn", [P, 2, S])
        landed, step, reduced = sems(k, ctx, "rot_landed rot_step rot_reduced")
        block = ctx.enter_context(nc.Block())

        @block.sync
        def _(sp):
            sp.dma_start(pos_i[:], t["positions"][0, :].partition_broadcast(P)).then_inc(landed, 16)
            sp.dma_start(freq[:], t["c_rope_freq"]).then_inc(landed, 16)

        @block.vector
        def _(dve):
            done = [0]

            def link(ins):
                ins.then_inc(step, 1)
                done[0] += 1
                dve.wait_ge(step, done[0])

            dve.wait_ge(landed, 32)
            link(nc.vector.tensor_copy(ang[:], pos_i[:]))
            link(nc.vector.tensor_scalar(ang[:], ang[:], freq[:], None, ALU.mult))
            for n, (quarter, dst) in enumerate(((0.0, sinT), (0.25, cosT))):
                u = turn[:, n, :]
                link(nc.vector.tensor_scalar(u, ang[:], 1.0 / (2 * math.pi), quarter, ALU.mult, ALU.add))
                link(nc.vector.tensor_scalar(u, u, magic, None, ALU.add))
                link(nc.vector.tensor_scalar(u, u, -magic, None, ALU.add))
                src = ang
                for part in two_pi:
                    link(nc.vector.scalar_tensor_tensor(out=dst[:], in0=u, scalar=-part, in1=src[:],
                                                        op0=ALU.mult, op1=ALU.add))
                    src = dst
                link(nc.vector.tensor_scalar(dst[:], dst[:], quarter * 2 * math.pi, None, ALU.add))
                nc.vector.tensor_scalar(dst[:], dst[:], lim, -lim, ALU.min, ALU.max).then_inc(reduced, 1)

        @block.scalar
        def _(act):
            for n, dst in enumerate((sinT, cosT)):
                act.wait_ge(reduced, n + 1)
                nc.scalar.activation(dst[:], dst[:], ACT.Sin)



def differential(k, w_in, off_q, off_k, off_v, lams, gain, lam_init, keep, cosT, sinT, yT, first, ahead):
    nc = k.nc
    heads = 4
    steps = heads * NT
    w = rows_pc(w_in)
    matrices = first.slots
    before = [[(0, c) for c in range(5)], [(1, c) for c in range(4)], [], [(2, c) for c in range(4, 8)]]
    after = [[(0, c) for c in range(5, 8)], [(1, c) for c in range(4, 8)], [(2, c) for c in range(4)], []]
    with ExitStack() as ctx:
        def sb(name, shape):
            return ctx.enter_context(nc.sbuf_tensor("da_" + name, shape, F32))

        raw = sb("raw", [P, 2, S])
        turned_part = sb("turned_part", [P, 2, S])
        qT, kT, v = sb("qT", [P, 2, S]), sb("kT", [P, 2, S]), sb("v", [P, 2, NT, P])
        probs = sb("probs", [P, 2, 2, S])
        diff = sb("diff", [P, 2, S])
        diffT = sb("diffT", [P, 2, S])
        neg_max, sums, coef = sb("neg_max", [P, 2 * NT]), sb("sums", [P, 2 * NT]), sb("coef", [P, NT])
        y, squares = sb("y", [P, 2, NT, P]), sb("squares", [P, P])
        ss = sb("ss", [P, 2, NT])
        lam_in, lam_dot, neg_lam = sb("lam_in", [P, 4, HD]), sb("lam_dot", [P, 4]), sb("neg_lam", [P, 1])
        lam_prod, scale_col, lam_const = sb("lam_prod", [P, HD]), sb("scale_col", [P, 1]), sb("lam_const", [P, 2])
        names = ("lam_landed lam_step lam_exp projected raw_ready v_ready swapped rope_step "
                 "qk_ready s_done max_done exp_done diff_step diff_done turned diffT_ready pv_done y_scaled "
                 "squared mean_ready log_ready rstd_ready normed yT_done y_out")
        sem = dict(zip(names.split(), sems(k, ctx, " ".join("da_" + n for n in names.split()))))
        block = ctx.enter_context(nc.Block())

        @block.sync
        def _(sp):
            for n, lam in enumerate(lams):
                sp.dma_start(lam_in[:, n, :], lam.partition_broadcast(P)).then_inc(sem["lam_landed"], 16)
            sp.dma_start(scale_col[:], gain.rearrange("(p a) -> p a", a=1)).then_inc(sem["lam_landed"], 16)
            sp.dma_start(lam_const[:, 0:1], lam_init.partition_broadcast(P)).then_inc(sem["lam_landed"], 16)
            sp.dma_start(lam_const[:, 1:2], keep.partition_broadcast(P)).then_inc(sem["lam_landed"], 16)
            ahead.issue(sp)
            with sp.Fori(1, heads) as it:
                for n, off in enumerate((off_q, off_k, off_v)):
                    sp.wait_ge(sem["projected"], 3 * it + (n - 2))
                    sp.dma_start(matrices[n], w[:, :, bass.ds(off + it * P, P)]).then_inc(first.landed[n], 16)

        @block.tensor
        def _(pe):
            def project(head, part, bank):
                for n, c in part:
                    if c == 0:
                        pe.wait_ge(first.landed[n], 16 * (head + 1))
                        if head and n == 0:
                            pe.wait_ge(sem["v_ready"], head)
                        if head and n == 2:
                            pe.wait_ge(sem["rope_step"], 4 * head + 3)
                    last = projection(nc, k, bank, n, matrices[n], c)
                    if c == 7:
                        last.then_inc(sem["projected"], 1)

            def swap(head, n, bank):
                pe.wait_ge(sem["raw_ready"], 2 * head + n + 1)
                nc.tensor.matmul(k.ps[:, bank, :], k.rope_swap[:], raw[:, n, :], start=True,
                                 stop=True).then_inc(sem["swapped"], 1)

            def scores(s):
                head, t = divmod(s, NT)
                n = (t + 1) * P
                if t == 0:
                    pe.wait_ge(sem["qk_ready"], 2 * head + 2)
                wait(pe, sem["exp_done"], 2 * (s - 1))
                for m in (0, 1):
                    half = slice(64 * m, 64 * m + 64)
                    bank = 2 * (s % 2) + m
                    nc.tensor.matmul(k.ps[:, bank, 0:n], qT[half, head % 2, t * P:n], kT[half, head % 2, 0:n],
                                     start=True, stop=False)
                    last = nc.tensor.matmul(k.ps[:, bank, t * P:n], k.ident[:], k.chunk_bias[:], start=False, stop=True)
                last.then_inc(sem["s_done"], 1)

            def turn_result(head):
                pe.wait_ge(sem["normed"], NT * (head + 1))
                for t in range(NT):
                    last = nc.tensor.transpose(k.ps[:, 5, t * P:(t + 1) * P], y[:, head % 2, t, :], k.ident[:])
                last.then_inc(sem["yT_done"], 1)

            for n, bank in ((0, 0), (1, 1)):
                project(0, [(n, c) for c in range(8)], bank)
            swap(0, 0, 5)
            swap(0, 1, 7)
            project(0, [(2, c) for c in range(8)], 4)
            scores(0)
            for s in range(steps):
                head, t = divmod(s, NT)
                more = head + 1 < heads
                if s + 1 < steps:
                    scores(s + 1)
                if t == 1 and head:
                    if more:
                        pe.wait_ge(sem["raw_ready"], 2 * head + 3)
                    turn_result(head - 1)
                if more:
                    project(head + 1, before[t], (5, 7, 5, 5)[t])
                    if t == 2:
                        wait(pe, sem["y_out"], head)
                        swap(head + 1, 0, 5)
                        swap(head + 1, 1, 7)
                if t == 0:
                    pe.wait_ge(sem["v_ready"], head + 1)
                pe.wait_ge(sem["diff_done"], s + 1)
                for b in range(t + 1):
                    last = nc.tensor.transpose(k.ps[:, 4, b * P:(b + 1) * P], diff[:, s % 2, b * P:(b + 1) * P], k.ident[:])
                last.then_inc(sem["turned"], 1)
                if more:
                    project(head + 1, after[t], (5, 7, 5, 5)[t])
                pe.wait_ge(sem["diffT_ready"], s + 1)
                wait(pe, sem["y_scaled"], s - 1)
                for b in range(t + 1):
                    last = nc.tensor.matmul(k.ps[:, 6, s % 2 * P:(s % 2 + 1) * P], diffT[:, s % 2, b * P:(b + 1) * P],
                                            v[:, head % 2, b, :], start=(b == 0), stop=(b == t))
                last.then_inc(sem["pv_done"], 1)
            turn_result(heads - 1)

        @block.scalar
        def _(act):
            def take_raw(head, n, bank):
                act.wait_ge(sem["projected"], 3 * head + n + 1)
                nc.scalar.activation(raw[:, n, :], k.ps[:, bank, :], ACT.Copy,
                                     scale=1.0 if n else SCALE).then_inc(sem["raw_ready"], 1)

            def exps(s):
                t = s % NT
                n = (t + 1) * P
                act.wait_ge(sem["max_done"], s + 1)
                wait(act, sem["diff_done"], s - 1)
                for m in (0, 1):
                    nc.scalar.activation(probs[:, s % 2, m, 0:n], k.ps[:, 2 * (s % 2) + m, 0:n], ACT.Exp,
                                         bias=neg_max[:, 2 * t + m:2 * t + m + 1],
                                         accum_out=sums[:, 2 * t + m:2 * t + m + 1]).then_inc(sem["exp_done"], 1)

            def scale_result(s):
                head, t = divmod(s, NT)
                act.wait_ge(sem["pv_done"], s + 1)
                nc.scalar.activation(y[:, head % 2, t, :], k.ps[:, 6, s % 2 * P:(s % 2 + 1) * P], ACT.Copy,
                                     scale=sums[:, 2 * t:2 * t + 1]).then_inc(sem["y_scaled"], 1)
                act.wait_ge(sem["y_scaled"], s + 1)
                nc.scalar.activation(squares[:], y[:, head % 2, t, :], ACT.Square,
                                     accum_out=ss[:, head % 2, t:t + 1]).then_inc(sem["squared"], 1)

            def inverse_root(head):
                one = ss[:, head % 2, :]
                act.wait_ge(sem["mean_ready"], head + 1)
                nc.scalar.activation(one, one, ACT.Ln).then_inc(sem["log_ready"], 1)
                act.wait_ge(sem["log_ready"], head + 1)
                nc.scalar.activation(one, one, ACT.Exp, scale=-0.5).then_inc(sem["rstd_ready"], 1)

            def take_result(head):
                act.wait_ge(sem["yT_done"], head + 1)
                nc.scalar.activation(yT[:, head, :], k.ps[:, 5, :], ACT.Copy, scale=scale_col[:]).then_inc(sem["y_out"], 1)

            act.preload_act_table_set("natural_log_exp_and_others")
            act.wait_ge(sem["lam_step"], 2)
            nc.scalar.activation(lam_dot[:, 2:4], lam_dot[:, 0:2], ACT.Exp).then_inc(sem["lam_exp"], 1)
            take_raw(0, 0, 0)
            take_raw(0, 1, 1)
            exps(0)
            for s in range(steps):
                head, t = divmod(s, NT)
                if s + 1 < steps:
                    exps(s + 1)
                if s:
                    scale_result(s - 1)
                act.wait_ge(sem["turned"], s + 1)
                nc.scalar.activation(diffT[:, s % 2, 0:(t + 1) * P], k.ps[:, 4, 0:(t + 1) * P],
                                     ACT.Copy).then_inc(sem["diffT_ready"], 1)
                if t == 0:
                    if head + 1 < heads:
                        take_raw(head + 1, 0, 5)
                    if head:
                        inverse_root(head - 1)
                if t == 1:
                    if head:
                        take_result(head - 1)
                    if head + 1 < heads:
                        take_raw(head + 1, 1, 7)
            scale_result(steps - 1)
            inverse_root(heads - 1)
            take_result(heads - 1)

        @block.vector
        def _(dve):
            dve.wait_ge(sem["lam_landed"], 16 * 7)
            for n in (0, 1):
                nc.vector.tensor_tensor_reduce(out=lam_prod[:], in0=lam_in[:, 2 * n, :], in1=lam_in[:, 2 * n + 1, :],
                                               scale=1.0, scalar=0.0, op0=ALU.mult, op1=ALU.add,
                                               accum_out=lam_dot[:, n:n + 1]).then_inc(sem["lam_step"], 1)
                dve.wait_ge(sem["lam_step"], n + 1)
            dve.wait_ge(sem["lam_exp"], 1)
            nc.vector.tensor_tensor(neg_lam[:], lam_dot[:, 3:4], lam_dot[:, 2:3], ALU.subtract).then_inc(sem["lam_step"], 1)
            dve.wait_ge(sem["lam_step"], 3)
            nc.vector.tensor_tensor(neg_lam[:], neg_lam[:], lam_const[:, 0:1], ALU.subtract).then_inc(sem["lam_step"], 1)
            nc.vector.tensor_tensor(scale_col[:], scale_col[:], lam_const[:, 1:2], ALU.mult).then_inc(sem["lam_step"], 1)
            dve.wait_ge(sem["lam_step"], 5)

            def cos_part(head, n):
                dve.wait_ge(sem["raw_ready"], 2 * head + n + 1)
                nc.vector.tensor_tensor(turned_part[:, n, :], raw[:, n, :], cosT[:], ALU.mult)\
                    .then_inc(sem["rope_step"], 1)

            def sin_part(head, n, bank):
                dst = (qT, kT)[n][:, head % 2, :]
                dve.wait_ge(sem["swapped"], 2 * head + n + 1)
                nc.vector.tensor_tensor(dst, k.ps[:, bank, :], sinT[:], ALU.mult).then_inc(sem["rope_step"], 1)
                dve.wait_ge(sem["rope_step"], 4 * head + 3 + n)
                nc.vector.tensor_tensor(dst, dst, turned_part[:, n, :], ALU.add).then_inc(sem["qk_ready"], 1)

            def take_v(head, bank):
                dve.wait_ge(sem["projected"], 3 * head + 3)
                nc.vector.tensor_copy(v[:, head % 2, :, :], k.ps[:, bank, :].rearrange("p (t n) -> p t n", t=NT))\
                    .then_inc(sem["v_ready"], 1)

            def maxima(s):
                t, b = s % NT, 2 * (s % 2)
                dve.wait_ge(sem["s_done"], s + 1)
                nc.vector.tensor_reduce(out=neg_max[:, 2 * t:2 * t + 2], in_=k.ps[:, b:b + 2, 0:(t + 1) * P],
                                        axis=AX.X, op=ALU.max, negate=True).then_inc(sem["max_done"], 1)

            def difference(s):
                t = s % NT
                n = (t + 1) * P
                dve.wait_ge(sem["exp_done"], 2 * s + 2)
                nc.vector.reciprocal(coef[:, t:t + 1], sums[:, 2 * t + 1:2 * t + 2]).then_inc(sem["diff_step"], 1)
                dve.wait_ge(sem["diff_step"], 3 * s + 1)
                nc.vector.scalar_tensor_tensor(out=coef[:, t:t + 1], in0=coef[:, t:t + 1], scalar=neg_lam[:],
                                               in1=sums[:, 2 * t:2 * t + 1], op0=ALU.mult,
                                               op1=ALU.mult).then_inc(sem["diff_step"], 1)
                dve.wait_ge(sem["diff_step"], 3 * s + 2)
                nc.vector.reciprocal(sums[:, 2 * t:2 * t + 1], sums[:, 2 * t:2 * t + 1]).then_inc(sem["diff_step"], 1)
                nc.vector.scalar_tensor_tensor(out=diff[:, s % 2, 0:n], in0=probs[:, s % 2, 1, 0:n],
                                               scalar=coef[:, t:t + 1], in1=probs[:, s % 2, 0, 0:n],
                                               op0=ALU.mult, op1=ALU.add).then_inc(sem["diff_done"], 1)

            def norm(head):
                one = ss[:, head % 2, :]
                dve.wait_ge(sem["squared"], NT * (head + 1))
                nc.vector.tensor_scalar(one, one, 1.0 / P, EPS, ALU.mult, ALU.add).then_inc(sem["mean_ready"], 1)
                dve.wait_ge(sem["rstd_ready"], head + 1)
                for t in range(NT):
                    nc.vector.tensor_scalar(y[:, head % 2, t, :], y[:, head % 2, t, :], ss[:, head % 2, t:t + 1], None,
                                            ALU.mult).then_inc(sem["normed"], 1)

            for n, bank in ((0, 5), (1, 7)):
                cos_part(0, n)
            for n, bank in ((0, 5), (1, 7)):
                sin_part(0, n, bank)
            take_v(0, 4)
            maxima(0)
            for s in range(steps):
                head, t = divmod(s, NT)
                if s + 1 < steps:
                    maxima(s + 1)
                difference(s)
                if t == 0 and head:
                    norm(head - 1)
                if head + 1 < heads:
                    if t == 2:
                        cos_part(head + 1, 0)
                        cos_part(head + 1, 1)
                        sin_part(head + 1, 0, 5)
                        sin_part(head + 1, 1, 7)
                    if t == 3:
                        take_v(head + 1, 5)
            norm(heads - 1)



def every(eng, blocks, per_round, step):
    rounds = -(-blocks // per_round)
    for u in range(min(per_round, blocks)):
        step(0, u)
    if rounds > 3:
        with eng.Fori(1, rounds - 2) as it:
            for u in range(per_round):
                step(it, u)
    for it in range(max(1, rounds - 2), rounds):
        for u in range(min(per_round, blocks - it * per_round)):
            step(it, u)


def wait(eng, sem, value):
    if not isinstance(value, int) or value > 0:
        eng.wait_ge(sem, value)


class MergePlan:

    COLS = 256

    def __init__(self, k, ctx, tag, w_in, gates, branches, bases, early):
        self.w, self.gates, self.branches = rows_pc(w_in), gates, branches
        self.halves = [self.places(k, base) for base in bases]
        self.first = Loads(k, ctx, *((f"{tag}_landed{u}", self.pairs(u, u * self.COLS) if u < early else [])
                                     for u in (0, 1)))
        self.early = early

    @staticmethod
    def words(gates, branches):
        return (len(gates) * DC + sum(n for _, _, n in branches)) * MergePlan.COLS

    def places(self, k, at):
        found = []
        for n in [DC] * len(self.gates) + [n for _, _, n in self.branches]:
            found.append(k.slot(at, n, self.COLS))
            at += n * self.COLS
        assert at <= RING
        return found[:len(self.gates)], found[len(self.gates):]

    def pairs(self, u, col):
        gate_at, branch_at = self.halves[u]
        return ([(dst, self.w[:, :, bass.ds(off + col, self.COLS)]) for dst, off in zip(gate_at, self.gates)]
                + [(dst, wb.rearrange("(c p) n -> p c n", p=P)[:, :, bass.ds(col, self.COLS)])
                   for dst, (wb, _, _) in zip(branch_at, self.branches)])


def merge(k, tag, plan, mergedT, ahead):
    nc = k.nc
    halves, branches, cols, nb = plan.halves, plan.branches, plan.COLS, len(plan.gates)
    landed = plan.first.landed
    per_body = 2 * 2 * nb
    with ExitStack() as ctx:
        def sb(name, shape):
            return ctx.enter_context(nc.sbuf_tensor(tag + "_" + name, shape, F32))

        sig, part = sb("sig", [P, 4, S]), sb("part", [P, 4, S])
        multiplied, sig_done, bank_free, summed = sems(
            k, ctx, " ".join(tag + n for n in "_multiplied _sig_done _bank_free _summed".split()))
        block = ctx.enter_context(nc.Block())

        @block.sync
        def _(sp):
            def load(u, col):
                for dst, src in plan.pairs(u, col):
                    sp.dma_start(dst, src).then_inc(landed[u], 16)

            for u in range(plan.early, 2):
                load(u, u * cols)
            for u in (0, 1):
                sp.wait_ge(multiplied, 2 * nb * (u + 1))
                load(u, (2 + u) * cols)
            sp.wait_ge(multiplied, 2 * nb * 3)
            ahead.issue(sp)

        @block.tensor
        def _(pe):
            with pe.Fori(0, 2) as it:
                for u in (0, 1):
                    pe.wait_ge(landed[u], it * (32 * nb) + 32 * nb)
                    for m in (0, 1):
                        for b, (_, yT, n) in enumerate(branches):
                            i = (2 * u + m) * nb + b
                            r = i % 4
                            pe.wait_ge(bank_free, it * per_body + (i + 1))
                            for c in range(DC):
                                nc.tensor.matmul(k.ps[:, 2 * r, :], halves[u][0][b][:, c, m * P:(m + 1) * P],
                                                 k.hT[:, c, :], start=(c == 0), stop=(c == DC - 1))
                            for c in range(n):
                                last = nc.tensor.matmul(k.ps[:, 2 * r + 1, :], halves[u][1][b][:, c, m * P:(m + 1) * P],
                                                        yT[:, c, :], start=(c == 0), stop=(c == n - 1))
                            last.then_inc(multiplied, 1)

        @block.scalar
        def _(act):
            with act.Fori(0, 2) as it:
                for i in range(per_body):
                    act.wait_ge(multiplied, it * per_body + (i + 1))
                    nc.scalar.activation(sig[:, i % 4, :], k.ps[:, 2 * (i % 4), :], ACT.Sigmoid).then_inc(sig_done, 1)

        @block.vector
        def _(dve):
            dve.sem_inc(bank_free, 4)
            with dve.Fori(0, 2) as it:
                for i in range(per_body):
                    chunk, b, r = i // nb, i % nb, i % 4
                    out = mergedT[:, it * 4 + chunk, :]
                    dve.wait_ge(sig_done, it * per_body + (i + 1))
                    dst = out if b == 0 else part[:, r, :]
                    nc.vector.tensor_tensor(dst, sig[:, r, :], k.ps[:, 2 * r + 1, :], ALU.mult).then_inc(bank_free, 1)
                    if b:
                        dve.wait_ge(bank_free, it * per_body + (i + 5))
                        if b > 1:
                            dve.wait_ge(summed, it * (4 * (nb - 1)) + (chunk * (nb - 1) + b - 1))
                        nc.vector.tensor_tensor(out, out, part[:, r, :], ALU.add).then_inc(summed, 1)


def output_loads(k, ctx, tag, base, w_out):
    rows = w_out.rearrange("(c p) n -> p c n", p=P)
    loads = Loads(k, ctx, (tag + "_landed0", [(k.slot(base, DC, 512), rows[:, :, 0:512])]))
    loads.slots = [k.slot(base, DC, 512), k.slot(0 if base >= DC * 512 else base + DC * 512, DC, 512)]
    return loads


def project_and_add(k, tag, w_out, srcT, first, ahead=()):
    nc = k.nc
    w = first.slots
    rows = w_out.rearrange("(c p) n -> p c n", p=P)
    with ExitStack() as ctx:
        (landed0,) = first.landed
        landed1, multiplied = sems(k, ctx, f"{tag}_landed1 {tag}_multiplied")
        block = ctx.enter_context(nc.Block())

        @block.sync
        def _(sp):
            sp.dma_start(w[1], rows[:, :, 512:D]).then_inc(landed1, 16)
            for loads in ahead:
                loads.issue(sp)

        @block.tensor
        def _(pe):
            for n, landed in enumerate((landed0, landed1)):
                pe.wait_ge(landed, 16)
                for t in range(NT):
                    for c in range(DC):
                        last = nc.tensor.matmul(k.ps[:, n * NT + t, :], srcT[:, c, t * P:(t + 1) * P], w[n][:, c, :],
                                                start=(c == 0), stop=(c == DC - 1))
                    last.then_inc(multiplied, 1)

        @block.vector
        def _(dve):
            for n in (0, 1):
                for t in range(NT):
                    dve.wait_ge(multiplied, n * NT + t + 1)
                    part = k.x[:, t, n * 512:(n + 1) * 512]
                    nc.vector.tensor_tensor(part, part, k.ps[:, n * NT + t, :], ALU.add)



GROUPS, PER_GROUP = 4, 8
EXPERTS = GROUPS * PER_GROUP
HID = 256
SPILL = 2 * S // P
BLOCKS = EXPERTS + SPILL
SKIP = 65536.0


class Routing:

    def __init__(self, nc, ctx):
        def sb(name, shape, dt=F32):
            return ctx.enter_context(nc.sbuf_tensor("route_" + name, shape, dt))

        self.gate = sb("gate", [P, 2, NT])
        self.token = sb("token", [P, BLOCKS], I32)
        self.row = sb("row", [P, BLOCKS], I32)
        self.spill_expert = sb("spill_expert", [1, SPILL + 1], I32)
        self.gain = sb("gain", [P, DC])
        self.w = sb("w", [P, DC, GROUPS + EXPERTS])
        self.bias = sb("bias", [P, GROUPS + EXPERTS])
        self.iota = sb("iota", [P, P])
        self.before = sb("before", [P, P])
        self.values = sb("values", [P, 8, 2])

    def loads(self, k, ctx, w_group, b_group, w_expert, b_expert, gain):
        return Loads(k, ctx, ("rt_landed", [
            (self.w[:, :, 0:GROUPS], rows_pc(w_group)), (self.w[:, :, GROUPS:], rows_pc(w_expert)),
            (self.bias[:, 0:GROUPS], b_group.partition_broadcast(P)),
            (self.bias[:, GROUPS:], b_expert.partition_broadcast(P)),
            (self.gain[:], gain.rearrange("(p c) -> p c", c=DC)), (self.iota[:], k.t["c_iota"].partition_broadcast(P)),
            (self.before[:], k.t["c_before"]), (self.values[:], k.t["c_slot_values"])]))


def route(k, tag, r, first):
    nc = k.nc
    NE, NL = EXPERTS, GROUPS + EXPERTS
    magic = 12582912.0
    with ExitStack() as ctx:
        def sb(name, shape, dt=F32):
            return ctx.enter_context(nc.sbuf_tensor(tag + "_" + name, shape, dt))

        w, bias, iota, before, values = r.w, r.bias, r.iota, r.before, r.values
        block_base = sb("block_base", [P, NE])
        lg = sb("lg", [P, NT, NL])
        gpad = sb("gpad", [P, NT, 8])
        gtop, gidx = sb("gtop", [P, NT, 8]), sb("gidx", [P, NT, 8], U32)
        gsel, gneg, gsum = sb("gsel", [P, NT]), sb("gneg", [P, NT]), sb("gsum", [P, NT])
        gexp = sb("gexp", [P, NT, GROUPS])
        chosen = sb("chosen", [P, NT, GROUPS])
        em = sb("em", [P, NT, NE])
        pen = sb("pen", [P, NT, GROUPS])
        etop, eidx = sb("etop", [P, NT, 8]), sb("eidx", [P, NT, 8], U32)
        esel = sb("esel", [P, 2, NT])
        gap, den = sb("gap", [P, NT]), sb("den", [P, NT])
        onehot = sb("onehot", [P, 2, NT, NE])
        member = sb("member", [P, NT, NE])
        counts, spills, ends, delta = sb("counts", [P, NE]), sb("spills", [P, NE]), sb("ends", [P, NE]), sb("delta", [P, NE])
        ones_row = sb("ones_row", [P, NE])
        over = sb("over", [P, NT, NE])
        slotv = sb("slotv", [P, NT, NE])
        junk = sb("junk", [P, NE])
        dest, blk, lane = sb("dest", [P, 8]), sb("blk", [P, 8]), sb("lane", [P, 8])
        lane_hot = sb("lane_hot", [P, 8, P])
        block_hot = sb("block_hot", [P, 8, 2, BLOCKS])
        table = sb("table", [P, 2, BLOCKS])
        spill_f = sb("spill_f", [P, SPILL + 1])
        ones = sb("ones", [P, P])
        (landed,) = first.landed
        link_sem, logits_done, gneg_ready, gexp_done, gap_ready, ratio_done, member_ready, ranked, hot_ready, tabled = sems(k, ctx, " ".join(tag + n for n in ("_link _logits_done _gneg_ready _gexp_done _gap_ready _ratio_done "
                                                "_member_ready _ranked _hot_ready _tabled").split()))
        block = ctx.enter_context(nc.Block())

        @block.tensor
        def _(pe):
            pe.wait_ge(landed, 16 * 8)
            for t in range(NT):
                for c in range(DC):
                    last = nc.tensor.matmul(k.ps[:, 0, t * NL:(t + 1) * NL], k.hT[:, c, t * P:(t + 1) * P], w[:, c, :],
                                            start=(c == 0), stop=(c == DC - 1))
            last.then_inc(logits_done, 1)
            pe.wait_ge(member_ready, 1)
            for t in range(NT):
                for b in range(t + 1):
                    nc.tensor.matmul(k.ps[:, 1, t * NE:(t + 1) * NE], (before if b == t else ones)[:], member[:, b, :],
                                     start=(b == 0), stop=(b == t))
            for b in range(NT):
                last = nc.tensor.matmul(k.ps[:, 2, 0:NE], ones[:], member[:, b, :], start=(b == 0), stop=(b == NT - 1))
            last.then_inc(ranked, 1)
            pe.wait_ge(hot_ready, 8)
            for i in range(8):
                last = nc.tensor.matmul(k.ps[:, 3, 0:2 * BLOCKS], lane_hot[:, i, :],
                                        block_hot[:, i, :, :].rearrange("p a b -> p (a b)"), start=(i == 0), stop=(i == 7))
            last.then_inc(tabled, 1)

        @block.scalar
        def _(act):
            act.wait_ge(gneg_ready, 1)
            for t in range(NT):
                nc.scalar.activation(gexp[:, t, :], lg[:, t, 0:GROUPS], ACT.Exp, bias=gneg[:, t:t + 1],
                                     accum_out=gsum[:, t:t + 1]).then_inc(gexp_done, 1)
            act.wait_ge(gap_ready, 1)
            nc.scalar.activation(gap[:], gap[:], ACT.Exp).then_inc(ratio_done, 1)

        @block.vector
        def _(dve):
            V = nc.vector
            done = [0]

            def link(*instructions):
                for ins in instructions:
                    ins.then_inc(link_sem, 1)
                    done[0] += 1
                dve.wait_ge(link_sem, done[0])

            link(V.memset(gpad[:], NEG), V.memset(ones[:], 1.0), V.memset(ones_row[:], 1.0))
            dve.wait_ge(landed, 16 * 8)
            dve.wait_ge(logits_done, 1)
            link(*[V.tensor_tensor(lg[:, t, :], k.ps[:, 0, t * NL:(t + 1) * NL], bias[:], ALU.add) for t in range(NT)])
            link(V.tensor_copy(gpad[:, :, 0:GROUPS], lg[:, :, 0:GROUPS]),
                 V.tensor_scalar(block_base[:], iota[:, 0:NE], float(P), None, ALU.mult))
            link(*[V.max(gtop[:, t, :], gpad[:, t, :]) for t in range(NT)])
            link(V.tensor_scalar(gneg[:], gtop[:, :, 0], -1.0, None, ALU.mult))
            dve.sem_inc(gneg_ready, 1)
            link(*[V.max_index(gidx[:, t, :], gtop[:, t, :], gpad[:, t, :]) for t in range(NT)])
            link(V.tensor_copy(gsel[:], gidx[:, :, 0]))
            link(*[V.tensor_scalar(chosen[:, t, :], iota[:, 0:GROUPS], gsel[:, t:t + 1], None, ALU.is_equal)
                   for t in range(NT)])
            link(V.tensor_scalar(pen[:], chosen[:], -NEG, NEG, ALU.mult, ALU.add))

            def per_group(a):
                return a.rearrange("p (g e) -> p g e", g=GROUPS)

            def spread(a):
                return a.unsqueeze(2).to_broadcast([P, GROUPS, PER_GROUP])

            link(*[V.tensor_tensor(per_group(em[:, t, :]), per_group(lg[:, t, GROUPS:NL]), spread(chosen[:, t, :]), ALU.mult)
                   for t in range(NT)])
            link(*[V.tensor_tensor(per_group(em[:, t, :]), per_group(em[:, t, :]), spread(pen[:, t, :]), ALU.add)
                   for t in range(NT)])
            link(*[V.max(etop[:, t, :], em[:, t, :]) for t in range(NT)])
            link(*[V.max_index(eidx[:, t, :], etop[:, t, :], em[:, t, :]) for t in range(NT)])
            link(V.tensor_copy(esel[:, 0, :], eidx[:, :, 0]), V.tensor_copy(esel[:, 1, :], eidx[:, :, 1]),
                 V.tensor_tensor(gap[:], etop[:, :, 1], etop[:, :, 0], ALU.subtract))
            dve.sem_inc(gap_ready, 1)
            link(*[V.tensor_scalar(onehot[:, c, t, :], iota[:, 0:NE], esel[:, c, t:t + 1], None, ALU.is_equal)
                   for t in range(NT) for c in (0, 1)])
            link(V.tensor_tensor(member[:], onehot[:, 0, :, :], onehot[:, 1, :, :], ALU.add))
            dve.sem_inc(member_ready, 1)
            dve.wait_ge(gexp_done, NT)
            dve.wait_ge(ratio_done, 1)
            link(V.tensor_scalar(den[:], gap[:], 1.0, None, ALU.add))
            link(V.tensor_tensor(den[:], den[:], gsum[:], ALU.mult))
            link(V.reciprocal(r.gate[:, 0, :], den[:]))
            link(V.tensor_tensor(r.gate[:, 1, :], r.gate[:, 0, :], gap[:], ALU.mult))
            dve.wait_ge(ranked, 1)
            link(V.tensor_copy(counts[:], k.ps[:, 2, 0:NE]))
            link(V.tensor_scalar(spills[:], counts[:], 1.0 * P, None, ALU.is_gt))
            for full in (2, 3):
                link(V.scalar_tensor_tensor(out=spills[:], in0=counts[:], scalar=full * P + 0.0, in1=spills[:],
                                            op0=ALU.is_gt, op1=ALU.add))
            link(V.tensor_tensor_scan(ends[:], ones_row[:], spills[:], 0.0, ALU.mult, ALU.add))
            link(V.tensor_tensor(delta[:], ends[:], spills[:], ALU.subtract))
            link(V.tensor_scalar(delta[:], delta[:], float(P), float((NE - 1) * P), ALU.mult, ALU.add))
            link(V.tensor_tensor(delta[:], delta[:], block_base[:], ALU.subtract))
            for t in range(NT):
                rank = k.ps[:, 1, t * NE:(t + 1) * NE]
                link(V.tensor_scalar(over[:, t, :], rank, P - 0.5, None, ALU.is_gt))
                link(V.tensor_tensor(over[:, t, :], over[:, t, :], delta[:], ALU.mult))
                link(V.tensor_tensor(slotv[:, t, :], rank, block_base[:], ALU.add))
                link(V.tensor_tensor(slotv[:, t, :], slotv[:, t, :], over[:, t, :], ALU.add))
                for c in (0, 1):
                    link(V.tensor_tensor_reduce(out=junk[:], in0=onehot[:, c, t, :], in1=slotv[:, t, :], scale=1.0,
                                                scalar=0.0, op0=ALU.mult, op1=ALU.add,
                                                accum_out=dest[:, 2 * t + c:2 * t + c + 1]))
            link(V.tensor_scalar(blk[:], dest[:], -(P / 2 - 0.5), 1.0 / P, ALU.add, ALU.mult))
            link(V.tensor_scalar(blk[:], blk[:], magic, None, ALU.add))
            link(V.tensor_scalar(blk[:], blk[:], -magic, None, ALU.add))
            link(V.scalar_tensor_tensor(out=lane[:], in0=blk[:], scalar=-float(P), in1=dest[:], op0=ALU.mult, op1=ALU.add))
            for i in range(8):
                V.tensor_scalar(lane_hot[:, i, :], iota[:], lane[:, i:i + 1], None, ALU.is_equal)
                for a in (0, 1):
                    last = V.tensor_scalar(block_hot[:, i, a, :], iota[:, 0:BLOCKS], blk[:, i:i + 1], values[:, i, a:a + 1],
                                           ALU.is_equal, ALU.mult)
                last.then_inc(hot_ready, 1)
            for b in range(SPILL):
                link(V.tensor_scalar(junk[:], ends[:], b + 0.5, None, ALU.is_lt, ALU.add, accum_out=spill_f[:, b:b + 1]))
            link(V.tensor_scalar(spill_f[:, 0:SPILL], spill_f[:, 0:SPILL], float(NE - 1), None, ALU.min),
                 V.tensor_copy(spill_f[:, SPILL:SPILL + 1], ends[:, NE - 1:NE]))
            link(V.tensor_copy(r.spill_expert[:], spill_f[0:1, :]))
            dve.wait_ge(tabled, 1)
            link(V.tensor_scalar(table[:].rearrange("p a b -> p (a b)"), k.ps[:, 3, 0:2 * BLOCKS], 0.0, SKIP,
                                 ALU.is_equal, ALU.mult))
            link(V.tensor_tensor(table[:].rearrange("p a b -> p (a b)"), table[:].rearrange("p a b -> p (a b)"),
                                 k.ps[:, 3, 0:2 * BLOCKS], ALU.add))
            link(V.tensor_scalar(r.token[:], table[:, 0, :], -1.0, None, ALU.add),
                 V.tensor_scalar(r.row[:], table[:, 1, :], -1.0, None, ALU.add))


EXPERT_WORDS = DC * 2 * HID + 2 * D


def expert_slots(k, u):
    return k.slot(u * EXPERT_WORDS, DC, 2 * HID), k.slot(u * EXPERT_WORDS + DC * 2 * HID, 2, D)


def expert_pairs(k, u, w_gate, w_up, w_down):
    gu, down = expert_slots(k, u)
    return [(gu[:, :, 0:HID], rows_pc(w_gate)), (gu[:, :, HID:2 * HID], rows_pc(w_up)),
            (down, w_down.rearrange("(f p) n -> p f n", p=P))]


def experts(k, tag, r, layer, blocks, spill, xn_rows, y_rows, w_gate, w_up, w_down, first_loads=None):
    nc = k.nc
    first = EXPERTS if spill else 0
    U = 3
    assert U * EXPERT_WORDS <= RING
    slots = [expert_slots(k, u) for u in range(U)]
    with ExitStack() as ctx:
        def sb(name, shape, dt=F32):
            return ctx.enter_context(nc.sbuf_tensor(tag + "_" + name, shape, dt))

        idx = sb("idx", [P, U, 2], I32)
        xs = sb("xs", [P, U, D])
        xsT = sb("xsT", [P, U, DC, P])
        silu = sb("silu", [P, HID])
        hid = sb("hid", [P, U, HID])
        hidT = sb("hidT", [P, U, 2, P])
        y = sb("y", [P, U, D])
        names = ("cleared wait_kept token_ready row_ready gathered0 gathered1 gathered2 turned xsT_ready gu_done silu_done hid_ready "
                 "hid_turned hidT_ready down_done y_act y_dve scattered0 scattered1 scattered2")
        sem = dict(zip(names.split(), sems(k, ctx, " ".join(tag + "_" + n for n in names.split()))))
        gathered, scattered = [[sem[f"{n}{u}"] for u in range(U)] for n in ("gathered", "scattered")]
        found = first_loads.landed if first_loads else sems(k, ctx, " ".join(
            f"{tag}_{n}_landed{u}" for u in range(U) for n in ("gu", "down")))
        w_landed, down_landed = found[0::2], found[1::2]
        block = ctx.enter_context(nc.Block())

        def before(it, u):
            return (it, u - 1) if u else (it - 1, U - 1)

        def after(it, u):
            return (it, u + 1) if u + 1 < U else (it + 1, 0)

        def first_block(it, u):
            return isinstance(it, int) and it == 0 and u == 0

        def last_block(it, u):
            return isinstance(it, int) and it * U + u == blocks - 1

        @block.sync
        def _(sp):
            def step(it, u):
                if first_loads and isinstance(it, int) and it == 0:
                    return
                n = it * U + u
                e = sp.value_load(r.spill_expert[0:1, bass.ds(n, 1)], min_val=0, max_val=EXPERTS - 1) if spill else n
                gate, up, down = expert_pairs(k, u, w_gate[layer, e], w_up[layer, e], w_down[layer, e])
                wait(sp, sem["gu_done"], it * U + (u - U + 1))
                for dst, src in (gate, up):
                    sp.dma_start(dst, src).then_inc(w_landed[u], 16)
                wait(sp, sem["down_done"], it * U + (u - U + 1))
                sp.dma_start(*down).then_inc(down_landed[u], 16)

            every(sp, blocks, U, step)

        @block.gpsimd
        def _(pool):
            def gather(it, u):
                n = it * U + u
                wait(pool, sem["turned"], it * U + (u - U + 1))
                nc.gpsimd.tensor_copy(idx[:, u, 0:1], r.token[:, bass.ds(n + first, 1)]).then_inc(sem["token_ready"], 1)
                pool.wait_ge(sem["token_ready"], it * U + (u + 1))
                pool.sem_inc(sem["wait_kept"], 1)
                nc.gpsimd.indirect_dma_start(out=xs[:, u, :], out_offset=None, in_=xn_rows[:, :],
                                             in_offset=bass.IndirectOffsetOnAxis(ap=idx[:, u, 0:1], axis=0),
                                             bounds_check=last_token, oob_is_err=False).then_inc(gathered[u], 16)

            def scatter(it, u):
                n = it * U + u
                wait(pool, scattered[u], it * 16)
                nc.gpsimd.tensor_copy(idx[:, u, 1:2], r.row[:, bass.ds(n + first, 1)]).then_inc(sem["row_ready"], 1)
                pool.wait_ge(sem["row_ready"], it * U + (u + 1))
                pool.wait_ge(sem["y_act"], it * U + (u + 1))
                pool.wait_ge(sem["y_dve"], it * U + (u + 1))
                pool.sem_inc(sem["wait_kept"], 1)
                nc.gpsimd.indirect_dma_start(out=y_rows[:, :], in_=y[:, u, :], in_offset=None,
                                             out_offset=bass.IndirectOffsetOnAxis(ap=idx[:, u, 1:2], axis=0),
                                             bounds_check=last_row, oob_is_err=False).then_inc(scattered[u], 16)

            last_token, last_row = pool.to_reg(S - 1), pool.to_reg(2 * S - 1)
            nc.gpsimd.memset(xs[:], 0.0).then_inc(sem["cleared"], 1)
            pool.wait_ge(sem["cleared"], 1)
            for u in range(U):
                gather(0, u)

            def step(it, u):
                if not isinstance(it, int) or (it + 1) * U + u < blocks:
                    gather(it + 1, u)
                scatter(it, u)

            every(pool, blocks, U, step)
            for u in range(U):
                pool.wait_ge(scattered[u], 16 * len(range(u, blocks, U)))

        @block.tensor
        def _(pe):
            def turn(it, u):
                pe.wait_ge(gathered[u], it * 16 + 16)
                wait(pe, sem["xsT_ready"], it * U + u)
                for c in range(DC):
                    last = nc.tensor.transpose(k.ps[:, c // 4, (c % 4) * P:(c % 4 + 1) * P], xs[:, u, c::DC], k.ident[:])
                last.then_inc(sem["turned"], 1)

            def down(it, u):
                pe.wait_ge(down_landed[u], it * 16 + 16)
                pe.wait_ge(sem["hidT_ready"], it * U + (u + 1))
                wait(pe, sem["y_act"], it * U + u)
                wait(pe, sem["y_dve"], it * U + u)
                for half in (0, 1):
                    for f in (0, 1):
                        last = nc.tensor.matmul(k.ps[:, 4 + half, :], hidT[:, u, f, :],
                                                slots[u][1][:, f, half * 512:(half + 1) * 512], start=(f == 0), stop=(f == 1))
                last.then_inc(sem["down_done"], 1)

            def step(it, u):
                pe.wait_ge(w_landed[u], it * 32 + 32)
                pe.wait_ge(sem["xsT_ready"], it * U + (u + 1))
                wait(pe, sem["hid_ready"], it * U + u)
                for c in range(DC):
                    last = nc.tensor.matmul(k.ps[:, 2, :], xsT[:, u, c, :], slots[u][0][:, c, :],
                                            start=(c == 0), stop=(c == DC - 1))
                last.then_inc(sem["gu_done"], 1)
                if not last_block(it, u):
                    turn(*after(it, u))
                if not first_block(it, u):
                    down(*before(it, u))
                pe.wait_ge(sem["hid_ready"], it * U + (u + 1))
                for f in (0, 1):
                    last = nc.tensor.transpose(k.ps[:, 3, f * P:(f + 1) * P], hid[:, u, f * P:(f + 1) * P], k.ident[:])
                last.then_inc(sem["hid_turned"], 1)

            turn(0, 0)
            every(pe, blocks, U, step)
            down(*divmod(blocks - 1, U))

        @block.scalar
        def _(act):
            def y_half(it, u):
                act.wait_ge(sem["down_done"], it * U + (u + 1))
                wait(act, scattered[u], it * 16)
                nc.scalar.activation(y[:, u, 0:512], k.ps[:, 4, :], ACT.Copy).then_inc(sem["y_act"], 1)

            def step(it, u):
                act.wait_ge(sem["gu_done"], it * U + (u + 1))
                nc.scalar.activation(silu[:], k.ps[:, 2, 0:HID], ACT.Silu).then_inc(sem["silu_done"], 1)
                if not first_block(it, u):
                    y_half(*before(it, u))
                act.wait_ge(sem["hid_turned"], it * U + (u + 1))
                nc.scalar.activation(hidT[:, u, :, :].rearrange("p f n -> p (f n)"), k.ps[:, 3, 0:HID],
                                     ACT.Copy).then_inc(sem["hidT_ready"], 1)

            every(act, blocks, U, step)
            y_half(*divmod(blocks - 1, U))

        @block.vector
        def _(dve):
            def gained(it, u):
                dve.wait_ge(sem["turned"], it * U + (u + 1))
                for b in (0, 1):
                    last = nc.vector.tensor_tensor(xsT[:, u, 4 * b:4 * b + 4, :],
                                                   k.ps[:, b, :].rearrange("p (c n) -> p c n", c=4),
                                                   r.gain[:, 4 * b:4 * b + 4].unsqueeze(2).to_broadcast([P, 4, P]), ALU.mult)
                last.then_inc(sem["xsT_ready"], 1)

            def y_half(it, u):
                dve.wait_ge(sem["down_done"], it * U + (u + 1))
                wait(dve, scattered[u], it * 16)
                nc.vector.tensor_copy(y[:, u, 512:D], k.ps[:, 5, :]).then_inc(sem["y_dve"], 1)

            def step(it, u):
                dve.wait_ge(sem["silu_done"], it * U + (u + 1))
                nc.vector.tensor_tensor(hid[:, u, :], silu[:], k.ps[:, 2, HID:2 * HID], ALU.mult).then_inc(sem["hid_ready"], 1)
                if not last_block(it, u):
                    gained(*after(it, u))
                if not first_block(it, u):
                    y_half(*before(it, u))

            gained(0, 0)
            every(dve, blocks, U, step)
            y_half(*divmod(blocks - 1, U))


def combine_experts(k, tag, r, y_rows, ahead):
    nc = k.nc
    rows = y_rows.rearrange("(t p c) d -> p t (c d)", p=P, c=2)
    y = k.ring[:, 0:NT * 2 * D].rearrange("p (t c d) -> p t c d", t=NT, c=2)
    with ExitStack() as ctx:
        (*landed, added) = sems(k, ctx, " ".join(f"{tag}_landed{t}" for t in range(NT)) + f" {tag}_added")
        block = ctx.enter_context(nc.Block())

        @block.sync
        def _(sp):
            for t in range(NT):
                sp.dma_start(y[:, t, :, :].rearrange("p c d -> p (c d)"), rows[:, t, :]).then_inc(landed[t], 16)
            ahead.issue(sp)

        @block.vector
        def _(dve):
            for t in range(NT):
                dve.wait_ge(landed[t], 16)
                for c in (0, 1):
                    nc.vector.scalar_tensor_tensor(out=k.x[:, t, :], in0=y[:, t, c, :], scalar=r.gate[:, c, t:t + 1],
                                                   in1=k.x[:, t, :], op0=ALU.mult, op1=ALU.add).then_inc(added, 1)
                    dve.wait_ge(added, 2 * t + c + 1)


def embed_loads(k, ctx, tag, p_rows, rows, w_ple, w_gate):
    wg, wp = k.slot(RING - 10 * D, DC, D), k.slot(RING - 2 * D, 2, D)
    halves = [(tag + f"_wg{n}", [(wg[:, :, n * 512:(n + 1) * 512], rows_pc(w_gate)[:, :, n * 512:(n + 1) * 512])])
              for n in (0, 1)]
    loads = Loads(k, ctx, (tag + "_p_landed", [(rows[:], p_rows.rearrange("(t p) d -> p t d", p=P))]),
                  (tag + "_wp_landed", [(wp, w_ple.rearrange("(c p) n -> p c n", p=P))]), *halves)
    loads.slots = wg, wp
    return loads


def embed_per_layer(k, tag, rows, first):
    nc = k.nc
    PC = 2
    wg, wp = first.slots
    p_landed, wp_landed, wg0, wg1 = first.landed
    with ExitStack() as ctx:
        def sb(name, shape):
            return ctx.enter_context(nc.sbuf_tensor(tag + "_" + name, shape, F32))

        pT = sb("pT", [P, PC, S])
        sig, part = sb("sig", [P, 3, 512]), sb("part", [P, 3, 512])
        turned, pT_ready, multiplied, sig_done, part_done = sems(
            k, ctx, " ".join(tag + n for n in "_turned _pT_ready _multiplied _sig_done _part_done".split()))
        block = ctx.enter_context(nc.Block())

        @block.tensor
        def _(pe):
            pe.wait_ge(p_landed, 16)
            for c in range(PC):
                for t in range(NT):
                    last = nc.tensor.transpose(k.ps[:, 6 + c, t * P:(t + 1) * P], rows[:, t, c * P:(c + 1) * P], k.ident[:])
            last.then_inc(turned, 1)
            pe.wait_ge(pT_ready, 1)
            pe.wait_ge(wp_landed, 16)
            for n, sem in enumerate((wg0, wg1)):
                pe.wait_ge(sem, 16)
                half = slice(n * 512, (n + 1) * 512)
                for t in range(NT):
                    i = n * NT + t
                    wait(pe, part_done, i - 2)
                    g = 2 * (i % 3)
                    for c in range(PC):
                        nc.tensor.matmul(k.ps[:, g + 1, :], pT[:, c, t * P:(t + 1) * P], wp[:, c, half],
                                         start=(c == 0), stop=(c == PC - 1))
                    for c in range(DC):
                        last = nc.tensor.matmul(k.ps[:, g, :], k.hT[:, c, t * P:(t + 1) * P], wg[:, c, half],
                                                start=(c == 0), stop=(c == DC - 1))
                    last.then_inc(multiplied, 1)

        @block.scalar
        def _(act):
            for i in range(2 * NT):
                act.wait_ge(multiplied, i + 1)
                nc.scalar.activation(sig[:, i % 3, :], k.ps[:, 2 * (i % 3), :], ACT.Sigmoid).then_inc(sig_done, 1)

        @block.vector
        def _(dve):
            dve.wait_ge(turned, 1)
            nc.vector.tensor_copy(pT[:], k.ps[:, 6:8, :]).then_inc(pT_ready, 1)
            for n in (0, 1):
                for t in range(NT):
                    i = n * NT + t
                    dve.wait_ge(sig_done, i + 1)
                    nc.vector.tensor_tensor(part[:, i % 3, :], sig[:, i % 3, :], k.ps[:, 2 * (i % 3) + 1, :],
                                            ALU.mult).then_inc(part_done, 1)
                    dve.wait_ge(part_done, i + 1)
                    xs = k.x[:, t, n * 512:(n + 1) * 512]
                    nc.vector.tensor_tensor(xs, xs, part[:, i % 3, :], ALU.add)



WINDOW_HEADS, WINDOW_GROUPS = 4, ((128, 1), (512, 4), (2048, 16))
BLOCK_HEADS = 8
BIAS_HEADS = WINDOW_HEADS * len(WINDOW_GROUPS) + BLOCK_HEADS
BUCKETS = 32
LINE = S + P


def bias_lines(k, rel_bias, lines, line, stored):
    nc = k.nc
    with ExitStack() as ctx:
        def sb(name, shape):
            return ctx.enter_context(nc.sbuf_tensor("bl_" + name, shape, F32))

        table, hot, hidden = sb("table", [BUCKETS, BIAS_HEADS]), sb("hot", [BUCKETS, LINE]), sb("hidden", [BIAS_HEADS, LINE])
        landed, multiplied, line_ready = sems(k, ctx, "bl_landed bl_multiplied bl_line_ready")
        block = ctx.enter_context(nc.Block())
        half = LINE // 2

        @block.sync
        def _(sp):
            sp.dma_start(table[:], rel_bias).then_inc(landed, 16)
            sp.dma_start(hot[:], k.t["c_bucket_hot"]).then_inc(landed, 16)
            sp.dma_start(hidden[:], k.t["c_hidden"]).then_inc(landed, 16)
            sp.wait_ge(line_ready, 2)
            sp.dma_start(lines, line[:].unsqueeze(1).to_broadcast([BIAS_HEADS, P, LINE])).then_inc(stored, 16)

        @block.tensor
        def _(pe):
            pe.wait_ge(landed, 48)
            for n in (0, 1):
                nc.tensor.matmul(k.ps[0:BIAS_HEADS, n, 0:half], table[:], hot[:, n * half:(n + 1) * half], start=True,
                                 stop=True).then_inc(multiplied, 1)

        @block.vector
        def _(dve):
            for n in (0, 1):
                dve.wait_ge(multiplied, n + 1)
                part = slice(n * half, (n + 1) * half)
                nc.vector.tensor_tensor(line[:, part], k.ps[0:BIAS_HEADS, n, 0:half], hidden[:, part],
                                        ALU.add).then_inc(line_ready, 1)


def bias_rows(lines):
    return bass.AP(lines.tensor, P - 1, [[P * LINE, BIAS_HEADS], [LINE - 1, P], [1, S]])



def biased_attention(k, tag, w_in, groups, banded, pairs, lines, yT, first, ahead):
    nc = k.nc
    ng = len(groups)
    units = 3 * ng
    steps = 8 * pairs
    w = rows_pc(w_in)
    kinds = [(g, kind) for g in range(ng) for kind in (0, 1)] + [(g, 2) for g in range(ng)]
    slots = [first.slots[3 * g + kind] for g, kind in kinds]
    landed = [first.landed[3 * g + kind] for g, kind in kinds]
    rows = bias_rows(lines)

    if ng > 1:
        before = [[(n, c) for c in range(4)] for n in range(7)] + [[(7, c) for c in range(8)]]
        after = [[(n, c) for c in range(4, 8)] for n in range(7)] + [[(8, c) for c in range(8)]]
        opening_bank = (5, 4, 3, 2, 1, 0, 7, 6, 5)
        bank_of = (7,) * units
        s_base, t_base = (0, 0), (3, 3)
    else:
        before, after = spread_eighths()
        opening_bank = bank_of = (2, 5, 7)
        s_base, t_base = (0, 1), (3, 4)
    finished = [[m for m, c in before[n] + after[n] if c == 7] for n in range(8)]

    def span(g, t):
        return max(0, t - 1) if banded and g == 0 else 0

    def width(s):
        return sum((s % 4 + 1 - span(g, s % 4)) * P for g in range(ng))

    widest = width(3)
    with ExitStack() as ctx:
        def sb(name, shape):
            return ctx.enter_context(nc.sbuf_tensor(tag + "_" + name, shape, F32))

        qT, kT, v = sb("qT", [P, 2, ng, S]), sb("kT", [P, 2, ng, S]), sb("v", [P, 2, ng, NT, P])
        bias = sb("bias", [P, 2, ng, S])
        probs, probsT = sb("probs", [P, 2, widest]), sb("probsT", [P, 2, widest])
        maxima, neg_max, sums = sb("maxima", [P, 8, ng]), sb("neg_max", [P, 8]), sb("sums", [P, 8])
        names = ("bias_landed0 bias_landed1 projected qk_ready v_ready s_done biased max_ready exp_done inverted "
                 "normed turned probsT_ready pv_done y_out")
        sem = dict(zip(names.split(), sems(k, ctx, " ".join(tag + "_" + n for n in names.split()))))
        block = ctx.enter_context(nc.Block())

        def wait_ready(eng, pair, m):
            if m < 2 * ng:
                eng.wait_ge(sem["qk_ready"], pair * 2 * ng + m + 1)
            else:
                eng.wait_ge(sem["v_ready"], pair * ng + m - 2 * ng + 1)

        @block.sync
        def _(sp):
            ahead.issue(sp)
            for pair in range(1, pairs):
                for m, (g, kind) in enumerate(kinds):
                    sp.wait_ge(sem["projected"], (pair - 1) * units + m + 1)
                    sp.dma_start(slots[m], w[:, :, groups[g][kind] + pair * P:][:, :, 0:P]).then_inc(landed[m], 16)

        @block.gpsimd
        def _(pool):
            for pair in range(pairs):
                for h in (0, 1):
                    wait(pool, sem["biased"], ((pair - 1) * 8 + 4 * h + 4) * ng)
                    for g in range(ng):
                        nc.gpsimd.dma_start(bias[:, h, g, :], rows[groups[g][3] + 2 * pair + h])\
                            .then_inc(sem[f"bias_landed{h}"], 16)

        @block.tensor
        def _(pe):
            def project(pair, part, bank):
                for m, c in part:
                    if c == 0:
                        pe.wait_ge(landed[m], 16 * (pair + 1))
                        if pair and ng > 1:
                            if m:
                                wait_ready(pe, pair, m - 1)
                        elif m == 8:
                            wait_ready(pe, 0, 0)
                    last = projection(nc, k, bank[m], kinds[m][1], slots[m], c)
                    if c == 7:
                        last.then_inc(sem["projected"], 1)

            def scores(s):
                pair, h, t = s // 8, s % 8 // 4, s % 4
                if t == 0 and h == 0:
                    pe.wait_ge(sem["qk_ready"], 2 * ng * (pair + 1))
                wait(pe, sem["biased"], (s if ng > 1 else s - 1) * ng)
                half = slice(64 * h, 64 * h + 64)
                for g in range(ng):
                    k0 = span(g, t) * P
                    last = nc.tensor.matmul(k.ps[:, s_base[s % 2] + g, 0:(t + 1) * P - k0],
                                            qT[half, pair % 2, g, t * P:(t + 1) * P],
                                            kT[half, pair % 2, g, k0:(t + 1) * P], start=True, stop=True)
                last.then_inc(sem["s_done"], 1)

            for m in range(units):
                project(0, [(m, c) for c in range(8)], opening_bank)
            scores(0)
            for s in range(steps):
                pair, h, t = s // 8, s % 8 // 4, s % 4
                if s + 1 < steps:
                    scores(s + 1)
                if pair + 1 < pairs:
                    project(pair + 1, before[s % 8], bank_of)
                if s == 0:
                    pe.wait_ge(sem["v_ready"], ng)
                pe.wait_ge(sem["normed"], s + 1)
                for b in range(width(s) // P):
                    last = nc.tensor.transpose(k.ps[:, t_base[s % 2] + b // 4, (b % 4) * P:(b % 4 + 1) * P],
                                               probs[:, s % 2, b * P:(b + 1) * P], k.ident[:])
                last.then_inc(sem["turned"], 1)
                if pair + 1 < pairs:
                    project(pair + 1, after[s % 8], bank_of)
                if s % 8 == 0:
                    pe.wait_ge(sem["v_ready"], ng * (pair + 1))
                    wait(pe, sem["y_out"], pair)
                pe.wait_ge(sem["probsT_ready"], s + 1)
                keys = [(g, kt) for g in range(ng) for kt in range(span(g, t), t + 1)]
                for b, (g, kt) in enumerate(keys):
                    last = nc.tensor.matmul(k.ps[64 * h:64 * h + 64, 6, t * P:(t + 1) * P],
                                            v[:, pair % 2, g, kt, 64 * h:64 * h + 64], probsT[:, s % 2, b * P:(b + 1) * P],
                                            start=(b == 0), stop=(b == len(keys) - 1))
                if s % 8 == 7:
                    last.then_inc(sem["pv_done"], 1)

        @block.scalar
        def _(act):
            def take(pair, m, bank):
                g, kind = kinds[m]
                act.wait_ge(sem["projected"], pair * units + m + 1)
                nc.scalar.activation((kT if kind else qT)[:, pair % 2, g, :], k.ps[:, bank[m], :], ACT.Copy,
                                     scale=1.0 if kind else SCALE).then_inc(sem["qk_ready"], 1)

            def exponential(s):
                act.wait_ge(sem["max_ready"], s + 1)
                a = probs[:, s % 2, 0:width(s)]
                nc.scalar.activation(a, a, ACT.Exp, bias=neg_max[:, s % 8:s % 8 + 1],
                                     accum_out=sums[:, s % 8:s % 8 + 1]).then_inc(sem["exp_done"], 1)

            for m in range(2 * ng):
                take(0, m, opening_bank)
            exponential(0)
            for s in range(steps):
                pair = s // 8
                if s + 1 < steps:
                    exponential(s + 1)
                act.wait_ge(sem["turned"], s + 1)
                for b in range(0, width(s), 512):
                    n = min(512, width(s) - b)
                    last = nc.scalar.activation(probsT[:, s % 2, b:b + n], k.ps[:, t_base[s % 2] + b // 512, 0:n], ACT.Copy)
                last.then_inc(sem["probsT_ready"], 1)
                if pair + 1 < pairs:
                    for m in finished[s % 8]:
                        if m < 2 * ng:
                            take(pair + 1, m, bank_of)
                if s % 8 == 7:
                    act.wait_ge(sem["pv_done"], pair + 1)
                    nc.scalar.activation(yT[:, pair, :], k.ps[:, 6, :], ACT.Copy).then_inc(sem["y_out"], 1)

        @block.vector
        def _(dve):
            def take(pair, m, bank):
                g, _ = kinds[m]
                dve.wait_ge(sem["projected"], pair * units + m + 1)
                nc.vector.tensor_copy(v[:, pair % 2, g, :, :], k.ps[:, bank[m], :].rearrange("p (t n) -> p t n", t=NT))\
                    .then_inc(sem["v_ready"], 1)

            def biased(s):
                pair, h, t = s // 8, s % 8 // 4, s % 4
                dve.wait_ge(sem[f"bias_landed{h}"], 16 * ng * (pair + 1))
                dve.wait_ge(sem["s_done"], s + 1)
                at = 0
                for g in range(ng):
                    n = (t + 1 - span(g, t)) * P
                    nc.vector.tensor_tensor_reduce(out=probs[:, s % 2, at:at + n], in0=k.ps[:, s_base[s % 2] + g, 0:n],
                                                   in1=bias[:, h, g, S - n:S], scale=1.0, scalar=NEG,
                                                   op0=ALU.add, op1=ALU.max,
                                                   accum_out=maxima[:, s % 8, g:g + 1]).then_inc(sem["biased"], 1)
                    at += n
                dve.wait_ge(sem["biased"], ng * (s + 1))
                nc.vector.tensor_reduce(out=neg_max[:, s % 8:s % 8 + 1], in_=maxima[:, s % 8, :], axis=AX.X, op=ALU.max,
                                        negate=True).then_inc(sem["max_ready"], 1)

            for m in range(2 * ng, units):
                take(0, m, opening_bank)
            biased(0)
            for s in range(steps):
                pair = s // 8
                if s + 1 < steps:
                    if s >= 1:
                        dve.wait_ge(sem["turned"], s)
                    biased(s + 1)
                dve.wait_ge(sem["exp_done"], s + 1)
                one = sums[:, s % 8:s % 8 + 1]
                nc.vector.reciprocal(one, one).then_inc(sem["inverted"], 1)
                dve.wait_ge(sem["inverted"], s + 1)
                a = probs[:, s % 2, 0:width(s)]
                nc.vector.tensor_scalar(a, a, one, None, ALU.mult).then_inc(sem["normed"], 1)
                if pair + 1 < pairs:
                    for m in finished[s % 8]:
                        if m >= 2 * ng:
                            take(pair + 1, m, bank_of)



TAPS = 4
LRU_C = 8.0


def recurrence_loads(k, ctx, base, w_in, off_x, off_g):
    n = 4 * P
    wx, wg = k.slot(base, DC, n), k.slot(base + DC * n, DC, n)
    loads = Loads(k, ctx, ("rg_wx", [(wx, rows_pc(w_in)[:, :, off_x:off_x + n])]),
                  ("rg_wg", [(wg, rows_pc(w_in)[:, :, off_g:off_g + n])]))
    loads.slots = wx, wg
    return loads


def recurrence(k, conv_w, conv_b, w_a, b_a, w_x, b_x, lam, yT, first, ahead):
    nc = k.nc
    C = 4
    wx, wg = first.slots
    with ExitStack() as ctx:
        def sb(name, shape):
            return ctx.enter_context(nc.sbuf_tensor("rg_" + name, shape, F32))

        diag_a, diag_x = sb("diag_a", [P, C, P]), sb("diag_x", [P, C, P])
        taps, bias = sb("taps", [P, TAPS, C]), sb("bias", [P, 4, C])
        sp_t = sb("sp_t", [P, 6, C])
        xp, xc = sb("xp", [P, C, S + TAPS - 1]), sb("xc", [P, C, S])
        mag, inp, tanh_t, recip, gate = (sb(n, [P, C, S]) for n in ("mag", "inp", "tanh_t", "recip", "gate"))
        names = ("small blocks zeroed x_done g_done xp_ready conv gates_done r_ready i_ready softplus lam_exp link "
                 "mag_ready tanh_done log_done recip_done a_ready ratio_ready root_done gelu_done")
        sem = dict(zip(names.split(), sems(k, ctx, " ".join("rg_" + n for n in names.split()))))
        sem["wx"], sem["wg"] = first.landed
        block = ctx.enter_context(nc.Block())

        @block.sync
        def _(sp):
            with nc.allow_non_contiguous_dma(reason="one word per channel"):
                for tap in range(TAPS):
                    sp.dma_start(taps[:, tap, :], conv_w[tap].rearrange("(c p) -> p c", p=P)).then_inc(sem["small"], 16)
                for n, b in enumerate((conv_b, b_a, b_x, lam)):
                    sp.dma_start(bias[:, n, :], b.rearrange("(c p) -> p c", p=P)).then_inc(sem["small"], 16)
            sp.wait_ge(sem["zeroed"], 1)
            for dst, src in ((diag_a, w_a), (diag_x, w_x)):
                for h in (0, 1):
                    half = slice(64 * h, 64 * h + 64)
                    sp.dma_start(dst[half, :, half], src[h::2].rearrange("n d e -> d n e")).then_inc(sem["blocks"], 16)
            ahead.issue(sp)

        @block.tensor
        def _(pe):
            for name, wt, base, done in (("wx", wx, 0, "x_done"), ("wg", wg, C, "g_done")):
                pe.wait_ge(sem[name], 16)
                for c in range(C):
                    for d in range(DC):
                        last = nc.tensor.matmul(k.ps[:, base + c, :], wt[:, d, c * P:(c + 1) * P], k.hT[:, d, :],
                                                start=(d == 0), stop=(d == DC - 1))
                    last.then_inc(sem[done], 1)
            pe.wait_ge(sem["blocks"], 64)
            pe.wait_ge(sem["conv"], C * TAPS)
            pe.wait_ge(sem["gelu_done"], C)
            for c in range(C):
                nc.tensor.matmul(k.ps[:, c, :], diag_a[:, c, :], xc[:, c, :], start=True, stop=True)
                nc.tensor.matmul(k.ps[:, C + c, :], diag_x[:, c, :], xc[:, c, :], start=True,
                                 stop=True).then_inc(sem["gates_done"], 1)

        @block.scalar
        def _(act):
            A = nc.scalar.activation
            act.wait_ge(sem["small"], 16 * 8)
            act.wait_ge(sem["link"], 1)
            A(sp_t[:, 1, :], sp_t[:, 0, :], ACT.Exp, scale=-1.0).then_inc(sem["lam_exp"], 1)
            for c in range(C):
                act.wait_ge(sem["x_done"], c + 1)
                A(xp[:, c, TAPS - 1:], k.ps[:, c, :], ACT.Copy).then_inc(sem["xp_ready"], 1)
            for c in range(C):
                act.wait_ge(sem["g_done"], c + 1)
                A(gate[:, c, :], k.ps[:, C + c, :], ACT.Gelu_apprx_tanh).then_inc(sem["gelu_done"], 1)
            for c in range(C):
                act.wait_ge(sem["gates_done"], c + 1)
                A(mag[:, c, :], k.ps[:, c, :], ACT.Sigmoid, bias=bias[:, 1, c:c + 1]).then_inc(sem["r_ready"], 1)
                A(inp[:, c, :], k.ps[:, C + c, :], ACT.Sigmoid, bias=bias[:, 2, c:c + 1]).then_inc(sem["i_ready"], 1)
            for c in range(C):
                act.wait_ge(sem["mag_ready"], c + 1)
                A(tanh_t[:, c, :], mag[:, c, :], ACT.Tanh).then_inc(sem["tanh_done"], 1)
            act.preload_act_table_set("natural_log_exp_and_others")
            for c in range(C):
                act.wait_ge(sem["tanh_done"], c + 1)
                A(recip[:, c, :], tanh_t[:, c, :], ACT.Ln, bias=1.0).then_inc(sem["log_done"], 1)
            for c in range(C):
                act.wait_ge(sem["log_done"], c + 1)
                A(recip[:, c, :], recip[:, c, :], ACT.Exp, scale=-1.0).then_inc(sem["recip_done"], 1)
                A(mag[:, c, :], mag[:, c, :], ACT.Exp, scale=-1.0).then_inc(sem["a_ready"], 1)
            for c in range(C):
                act.wait_ge(sem["ratio_ready"], c + 1)
                A(recip[:, c, :], recip[:, c, :], ACT.Sqrt, scale=2.0).then_inc(sem["root_done"], 1)

        @block.vector
        def _(dve):
            V = nc.vector
            done = [0]

            def link(*instructions):
                for ins in instructions:
                    ins.then_inc(sem["link"], 1)
                    done[0] += 1
                dve.wait_ge(sem["link"], done[0])

            dve.wait_ge(sem["small"], 16 * 8)
            link(V.scalar_tensor_tensor(out=sp_t[:, 0, :], in0=bias[:, 3, :], scalar=-1.0, in1=bias[:, 3, :],
                                        op0=ALU.mult, op1=ALU.max))
            dve.wait_ge(sem["lam_exp"], 1)
            link(V.tensor_scalar(sp_t[:, 2, :], sp_t[:, 1, :], 2.0, None, ALU.add))
            link(V.reciprocal(sp_t[:, 2, :], sp_t[:, 2, :]))
            link(V.tensor_tensor(sp_t[:, 2, :], sp_t[:, 2, :], sp_t[:, 1, :], ALU.mult))
            link(V.tensor_tensor(sp_t[:, 3, :], sp_t[:, 2, :], sp_t[:, 2, :], ALU.mult),
                 V.memset(sp_t[:, 4, :], 1.0 / 17))
            for odd in (15, 13, 11, 9, 7, 5, 3, 1):
                link(V.tensor_tensor(sp_t[:, 4, :], sp_t[:, 4, :], sp_t[:, 3, :], ALU.mult))
                link(V.tensor_scalar(sp_t[:, 4, :], sp_t[:, 4, :], 1.0 / odd, None, ALU.add))
            link(V.tensor_tensor(sp_t[:, 4, :], sp_t[:, 4, :], sp_t[:, 2, :], ALU.mult),
                 V.tensor_scalar(sp_t[:, 5, :], bias[:, 3, :], -1.0, 0.0, ALU.mult, ALU.max))
            link(V.scalar_tensor_tensor(out=sp_t[:, 5, :], in0=sp_t[:, 4, :], scalar=2.0, in1=sp_t[:, 5, :],
                                        op0=ALU.mult, op1=ALU.add))
            link(V.tensor_scalar(sp_t[:, 5, :], sp_t[:, 5, :], LRU_C, None, ALU.mult))
            dve.sem_inc(sem["softplus"], 1)
            dve.wait_ge(sem["zeroed"], 1)
            for c in range(C):
                dve.wait_ge(sem["xp_ready"], c + 1)
                V.tensor_scalar(xc[:, c, :], xp[:, c, 0:S], taps[:, 0, c:c + 1], bias[:, 0, c:c + 1], ALU.mult,
                                ALU.add).then_inc(sem["conv"], 1)
                for tap in range(1, TAPS):
                    dve.wait_ge(sem["conv"], TAPS * c + tap)
                    V.scalar_tensor_tensor(out=xc[:, c, :], in0=xp[:, c, tap:tap + S], scalar=taps[:, tap, c:c + 1],
                                           in1=xc[:, c, :], op0=ALU.mult, op1=ALU.add).then_inc(sem["conv"], 1)
            for c in range(C):
                dve.wait_ge(sem["r_ready"], c + 1)
                V.tensor_scalar(mag[:, c, :], mag[:, c, :], sp_t[:, 5, c:c + 1], None, ALU.mult).then_inc(sem["mag_ready"], 1)
                dve.wait_ge(sem["i_ready"], c + 1)
                link(V.tensor_tensor(inp[:, c, :], inp[:, c, :], xc[:, c, :], ALU.mult))
            for c in range(C):
                dve.wait_ge(sem["recip_done"], c + 1)
                V.tensor_tensor(recip[:, c, :], recip[:, c, :], tanh_t[:, c, :], ALU.mult).then_inc(sem["ratio_ready"], 1)
            for c in range(C):
                dve.wait_ge(sem["root_done"], c + 1)
                dve.wait_ge(sem["a_ready"], c + 1)
                link(V.tensor_tensor(inp[:, c, :], inp[:, c, :], recip[:, c, :], ALU.mult))
                link(V.tensor_tensor_scan(xc[:, c, :], mag[:, c, :], inp[:, c, :], 0.0, ALU.mult, ALU.add))
                V.tensor_tensor(yT[:, c, :], xc[:, c, :], gate[:, c, :], ALU.mult)

        @block.gpsimd
        def _(pool):
            nc.gpsimd.memset(xp[:, :, 0:TAPS - 1], 0.0)
            nc.gpsimd.memset(diag_a[:], 0.0)
            nc.gpsimd.memset(diag_x[:], 0.0)
            pool.drain().then_inc(sem["zeroed"], 1)



FFN = -(-8 * D // (3 * 256)) * 256
FC = FFN // P


class FeedForward:

    def __init__(self, k, ctx, w_gu, w_down):
        def sb(name, shape, dt=F32):
            return ctx.enter_context(k.nc.sbuf_tensor("ff_" + name, shape, dt))

        self.w_gu, self.w_down = rows_pc(w_gu), w_down
        self.hiddenT = sb("hiddenT", [P, FC, S])
        self.raw = sb("raw", [P, 2, 2, DC, P])
        self.first = Loads(k, ctx, *((f"ff_landed{u}{part}", [(self.raw[:, u, part], self.columns(u, part))])
                                     for u in (0, 1) for part in (0, 1)))
        self.rows = 4
        self.raw_down = sb("raw_down", [P, self.rows, D])
        self.first_down = Loads(k, ctx, *((f"fd_landed{n}", [(self.raw_down[:, n, :], w_down[n * P:(n + 1) * P, :])])
                                          for n in range(self.rows)))

    def columns(self, chunk, part):
        return self.w_gu[:, :, bass.ds(chunk * P + part * FFN, P)]


def feed_forward(k, ff):
    nc = k.nc
    with ExitStack() as ctx:
        def sb(name, shape, dt=F32):
            return ctx.enter_context(nc.sbuf_tensor("ff_" + name, shape, dt))

        hT_masked = sb("hT_masked", [P, 2, S])
        hT_high, hT_low = sb("hT_high", [P, DC, S], F32R), sb("hT_low", [P, DC, S], F32R)
        masked_w = sb("masked_w", [P, 2, DC, P])
        high_w, low_w = sb("high_w", [P, 2, 2, DC, P], F32R), sb("low_w", [P, 2, 2, DC, P], F32R)
        silu = sb("silu", [P, 2, S])
        hT_mask_done, hT_high_ready, hT_low_ready, masked, high_ready, low_ready, multiplied, silu_done, hidden_ready = sems(
            k, ctx, "ff_hT_mask_done ff_hT_high_ready ff_hT_low_ready ff_masked ff_high_ready ff_low_ready ff_multiplied "
            "ff_silu_done ff_hidden_ready")
        landed = ff.first.landed
        block = ctx.enter_context(nc.Block())

        @block.sync
        def _(sp):
            ff.first_down.issue(sp)

            def step(it, u):
                if isinstance(it, int) and it == 0 and u < 2:
                    return
                for part in (0, 1):
                    wait(sp, low_ready, it * 8 + (2 * u - 3 + part))
                    sp.dma_start(ff.raw[:, u % 2, part], ff.columns(it * 4 + u, part)).then_inc(landed[u % 2 * 2 + part], 16)

            every(sp, FC, 4, step)

        @block.tensor
        def _(pe):
            def step(it, u):
                opening = isinstance(it, int) and it == 0 and u == 0
                wait(pe, hidden_ready, it * 4 + (u - 3))
                for part in (0, 1):
                    pe.wait_ge(high_ready, it * 8 + (2 * u + part + 1))
                    pe.wait_ge(low_ready, it * 8 + (2 * u + part + 1))
                    for c in range(DC):
                        if opening and part == 0:
                            pe.wait_ge(hT_high_ready, c + 1)
                            pe.wait_ge(hT_low_ready, c + 1)
                        last = split_product(nc, k.ps[:, 2 * u + part, :],
                                             (high_w[:, u % 2, part, c, :], low_w[:, u % 2, part, c, :]),
                                             (hT_high[:, c, :], hT_low[:, c, :]), c == 0, c == DC - 1)
                last.then_inc(multiplied, 1)

            every(pe, FC, 4, step)

        @block.scalar
        def _(act):
            def split_weights(it, u):
                for part in (0, 1):
                    act.wait_ge(masked, it * 8 + (2 * u + part + 1))
                    nc.scalar.activation(high_w[:, u % 2, part], masked_w[:, part], ACT.Copy).then_inc(high_ready, 1)

            def gate(it, u):
                act.wait_ge(multiplied, it * 4 + (u + 1))
                wait(act, hidden_ready, it * 4 + (u - 1))
                nc.scalar.activation(silu[:, u % 2, :], k.ps[:, 2 * u, :], ACT.Silu).then_inc(silu_done, 1)

            def step(it, u):
                split_weights(it, u)
                if isinstance(it, int) and it == 0 and u == 0:
                    for c in range(DC):
                        act.wait_ge(hT_mask_done, c + 1)
                        nc.scalar.activation(hT_high[:, c, :], hT_masked[:, c % 2, :], ACT.Copy).then_inc(hT_high_ready, 1)
                else:
                    gate(*((it, u - 1) if u else (it - 1, 3)))

            every(act, FC, 4, step)
            gate(*divmod(FC - 1, 4))

        @block.vector
        def _(dve):
            def split_weights(it, u):
                for part in (0, 1):
                    dve.wait_ge(landed[u % 2 * 2 + part], it * 32 + 16 * (u // 2 + 1))
                    wait(dve, high_ready, it * 8 + (2 * u - 1 + part))
                    wait(dve, multiplied, it * 4 + (u - 1))
                    mask_low_bits(nc, masked_w[:, part], ff.raw[:, u % 2, part]).then_inc(masked, 1)
                    dve.wait_ge(masked, it * 8 + (2 * u + part + 1))
                    nc.vector.tensor_tensor(low_w[:, u % 2, part], ff.raw[:, u % 2, part], masked_w[:, part],
                                            ALU.subtract).then_inc(low_ready, 1)

            def hidden(it, u):
                dve.wait_ge(silu_done, it * 4 + (u + 1))
                nc.vector.tensor_tensor(ff.hiddenT[:, bass.ds(it * 4 + u, 1), :].rearrange("p a n -> p (a n)"),
                                        silu[:, u % 2, :], k.ps[:, 2 * u + 1, :], ALU.mult).then_inc(hidden_ready, 1)

            def step(it, u):
                split_weights(it, u)
                if isinstance(it, int) and it == 0 and u == 0:
                    for c in range(DC):
                        wait(dve, hT_high_ready, c - 1)
                        mask_low_bits(nc, hT_masked[:, c % 2, :], k.hT[:, c, :]).then_inc(hT_mask_done, 1)
                        dve.wait_ge(hT_mask_done, c + 1)
                        nc.vector.tensor_tensor(hT_low[:, c, :], k.hT[:, c, :], hT_masked[:, c % 2, :],
                                                ALU.subtract).then_inc(hT_low_ready, 1)
                else:
                    hidden(*((it, u - 1) if u else (it - 1, 3)))

            every(dve, FC, 4, step)
            hidden(*divmod(FC - 1, 4))

    with ExitStack() as ctx:
        def sb(name, shape, dt=F32):
            return ctx.enter_context(nc.sbuf_tensor("fd_" + name, shape, dt))

        R = ff.rows
        masked_h, masked_w = sb("masked_h", [P, 2, S]), sb("masked_w", [P, 2, D])
        high_h, low_h = sb("high_h", [P, 2, S], F32R), sb("low_h", [P, 2, S], F32R)
        high_w, low_w = sb("high_w", [P, 2, D], F32R), sb("low_w", [P, 2, D], F32R)
        masked, high_ready, low_ready, used, added = sems(k, ctx, "fd_masked fd_high_ready fd_low_ready fd_used fd_added")
        landed = ff.first_down.landed
        block = ctx.enter_context(nc.Block())

        @block.sync
        def _(sp):
            def step(it, u):
                if isinstance(it, int) and it == 0:
                    return
                wait(sp, low_ready, it * 2 * R + (2 * u + 2 - 2 * R))
                row = (it * R + u) * P
                sp.dma_start(ff.raw_down[:, u, :], ff.w_down[bass.ds(row, P), :]).then_inc(landed[u], 16)

            every(sp, FC, R, step)

        @block.tensor
        def _(pe):
            def step(it, u):
                first = isinstance(it, int) and it == 0 and u == 0
                final = isinstance(it, int) and it * R + u == FC - 1
                pe.wait_ge(high_ready, it * 2 * R + (2 * u + 2))
                pe.wait_ge(low_ready, it * 2 * R + (2 * u + 2))
                for t in range(NT):
                    tokens = slice(t * P, (t + 1) * P)
                    for n in (0, 1):
                        cols = slice(n * 512, (n + 1) * 512)
                        last = split_product(nc, k.ps[:, 2 * t + n, :], (high_h[:, u % 2, tokens], low_h[:, u % 2, tokens]),
                                             (high_w[:, u % 2, cols], low_w[:, u % 2, cols]), first, final)
                last.then_inc(used, 1)

            every(pe, FC, R, step)

        @block.scalar
        def _(act):
            def step(it, u):
                act.wait_ge(masked, it * 2 * R + (2 * u + 1))
                nc.scalar.activation(high_h[:, u % 2, :], masked_h[:, u % 2, :], ACT.Copy).then_inc(high_ready, 1)
                act.wait_ge(masked, it * 2 * R + (2 * u + 2))
                nc.scalar.activation(high_w[:, u % 2, :], masked_w[:, u % 2, :], ACT.Copy).then_inc(high_ready, 1)

            every(act, FC, R, step)

        @block.vector
        def _(dve):
            def step(it, u):
                wait(dve, used, it * R + (u - 1))
                hidden = ff.hiddenT[:, bass.ds(it * R + u, 1), :].rearrange("p a n -> p (a n)")
                mask_low_bits(nc, masked_h[:, u % 2, :], hidden).then_inc(masked, 1)
                dve.wait_ge(masked, it * 2 * R + (2 * u + 1))
                nc.vector.tensor_tensor(low_h[:, u % 2, :], hidden, masked_h[:, u % 2, :], ALU.subtract).then_inc(low_ready, 1)
                dve.wait_ge(landed[u], it * 16 + 16)
                mask_low_bits(nc, masked_w[:, u % 2, :], ff.raw_down[:, u, :]).then_inc(masked, 1)
                dve.wait_ge(masked, it * 2 * R + (2 * u + 2))
                nc.vector.tensor_tensor(low_w[:, u % 2, :], ff.raw_down[:, u, :], masked_w[:, u % 2, :],
                                        ALU.subtract).then_inc(low_ready, 1)

            every(dve, FC, R, step)
            dve.wait_ge(used, FC)
            for t in range(NT):
                nc.vector.tensor_tensor(k.x[:, t, :], k.x[:, t, :], k.ps[:, 2 * t:2 * t + 2, :].rearrange("p a n -> p (a n)"),
                                        ALU.add).then_inc(added, 1)


def final_norm(k, tag, gain, out=None, wait_for=None):
    nc = k.nc
    with ExitStack() as ctx:
        g = ctx.enter_context(nc.sbuf_tensor(tag + "_g", [P, D], F32))
        ss = ctx.enter_context(nc.sbuf_tensor(tag + "_ss", [P, NT], F32))
        landed, squares, mean_ready, root_ready, rstd_ready, normed, stored = sems(
            k, ctx, " ".join(tag + n for n in "_landed _squares _mean _root _rstd _normed _stored".split()))
        block = ctx.enter_context(nc.Block())

        @block.sync
        def _(sp):
            sp.dma_start(g[:], gain.partition_broadcast(P)).then_inc(landed, 16)
            if wait_for is not None:
                sp.wait_ge(wait_for, 16)
            if out is not None:
                for t in range(NT):
                    sp.wait_ge(normed, t + 1)
                    sp.dma_start(out[0, t * P:(t + 1) * P, :], k.x[:, t, :]).then_inc(stored, 16)
                sp.wait_ge(stored, 16 * NT)

        @block.scalar
        def _(act):
            for t in range(NT):
                nc.scalar.activation(k.ps[:, 2 * t:2 * t + 2, :], k.x[:, t, :].rearrange("p (a n) -> p a n", a=2),
                                     ACT.Square, accum_out=ss[:, t:t + 1]).then_inc(squares, 1)
            act.wait_ge(mean_ready, 1)
            nc.scalar.activation(ss[:], ss[:], ACT.Sqrt).then_inc(root_ready, 1)

        @block.vector
        def _(dve):
            dve.wait_ge(squares, NT)
            nc.vector.tensor_scalar(ss[:], ss[:], 1.0 / D, EPS, ALU.mult, ALU.add).then_inc(mean_ready, 1)
            dve.wait_ge(root_ready, 1)
            nc.vector.reciprocal(ss[:], ss[:]).then_inc(rstd_ready, 1)
            dve.wait_ge(rstd_ready, 1)
            dve.wait_ge(landed, 16)
            for t in range(NT):
                nc.vector.scalar_tensor_tensor(out=k.x[:, t, :], in0=k.x[:, t, :], scalar=ss[:, t:t + 1], in1=g[:],
                                               op0=ALU.mult, op1=ALU.mult).then_inc(normed, 1)


def second_layer(k, t, lines):
    nc = k.nc
    w_in = t["w_in_2"][0]
    width = WINDOW_HEADS * HD
    window = len(WINDOW_GROUPS) * width
    lru, block = 3 * window, 3 * window + 1024
    gates = block + 1536
    groups = tuple((g * width, window + g * width, 2 * window + g * width, g * WINDOW_HEADS)
                   for g in range(len(WINDOW_GROUPS)))
    with ExitStack() as mix:
        yaT = mix.enter_context(nc.sbuf_tensor("ya2_transposed", [P, 2, S], F32))
        ybT = mix.enter_context(nc.sbuf_tensor("yb2_transposed", [P, 4, S], F32))
        ycT = mix.enter_context(nc.sbuf_tensor("yc2_transposed", [P, 4, S], F32))
        branches = ((t["p_a_2"][0], yaT, 2), (t["p_b_2"][0], ybT, 4), (t["p_c_2"][0], ycT, 4))
        window_loads = qkv_loads(k, mix, "wa", 0, w_in, [off for g in groups for off in g[:3]])
        lru_loads = recurrence_loads(k, mix, 9 * DC * P, w_in, lru, lru + 512)
        block_loads = qkv_loads(k, mix, "ba", 0, w_in, (block, block + 512, block + 1024))
        gate_cols = (gates, gates + D, gates + 2 * D)
        words = MergePlan.words(gate_cols, branches)
        plan = MergePlan(k, mix, "mg2", w_in, gate_cols, branches, (RING - words, RING - 2 * words), 1)
        assert RING - words >= 3 * DC * P
        out_loads = output_loads(k, mix, "op2", RING - words, t["w_out_2"][0])

        norm_transpose(k, "mix2", t["g_mix_2"][0], (window_loads,))
        biased_attention(k, "wa", w_in, groups, True, WINDOW_HEADS // 2, lines, yaT, window_loads, lru_loads)
        recurrence(k, t["conv_w_2"][0], t["conv_b_2"][0], t["lru_wa_2"][0], t["lru_ba_2"][0],
                   t["lru_wx_2"][0], t["lru_bx_2"][0], t["lru_lam_2"][0], ybT, lru_loads, block_loads)
        assert S // 256 - 1 <= 3
        biased_attention(k, "ba", w_in, ((block, block + 512, block + 1024, BIAS_HEADS - BLOCK_HEADS),), False,
                         BLOCK_HEADS // 2, lines, ycT, block_loads, plan.first)
        mergedT = mix.enter_context(nc.sbuf_tensor("merged2_transposed", [P, DC, S], F32))
        merge(k, "mg2", plan, mergedT, out_loads)
        project_and_add(k, "op2", t["w_out_2"][0], mergedT, out_loads)
    k.ring_scope.close()
    with ExitStack() as ctx:
        ff = FeedForward(k, ctx, t["w_gu_2"][0], t["w_down_2"][0])
        norm_transpose(k, "ffn2", t["g_ffn_2"][0], (ff.first,))
        feed_forward(k, ff)



IN = {}


def first_layer(k, t, i, scratch):
    nc = k.nc
    xn_rows, y_rows = scratch
    w_in = t["w_in"][i]
    with ExitStack() as ctx:
        r = Routing(nc, ctx)
        route_loads = r.loads(k, ctx, t["w_router_group"][i], t["b_router_group"][i], t["w_router_expert"][i],
                              t["b_router_expert"][i], t["g_ffn"][i])
        with ExitStack() as mix:
            mergedT = mix.enter_context(nc.sbuf_tensor("merged_transposed", [P, DC, S], F32))
            yaT = mix.enter_context(nc.sbuf_tensor("ya_transposed", [P, 4, S], F32))
            ybT = mix.enter_context(nc.sbuf_tensor("yb_transposed", [P, 4, S], F32))
            gates, branches = (3072, 4096), ((t["w_br_a"][i], yaT, 4), (t["w_br_b"][i], ybT, 4))
            stick_loads = qkv_loads(k, mix, "sb", 0, w_in, (0, 512, 1024))
            diff_loads = qkv_loads(k, mix, "da", 3 * DC * P, w_in, (1536, 2048, 2560))
            words = MergePlan.words(gates, branches)
            plan = MergePlan(k, mix, "mg", w_in, gates, branches, (6 * DC * P, 6 * DC * P + words), 2)
            out_loads = output_loads(k, mix, "op", 6 * DC * P, t["w_o"][i])
            norm_transpose(k, "mix", t["g_mix"][i], (stick_loads,))
            stick_breaking(k, w_in, 0, 512, 1024, yaT, stick_loads, diff_loads)
            differential(k, w_in, 1536, 2048, 2560, [t[n][i] for n in ("lam_q1", "lam_k1", "lam_q2", "lam_k2")],
                         t["g_subln"][i], t["c_lam_init"][i], t["c_keep"][i], k.cosT, k.sinT, ybT, diff_loads, plan.first)
            merge(k, "mg", plan, mergedT, out_loads)
            project_and_add(k, "op", t["w_o"][i], mergedT, out_loads, (route_loads,))
        p_rows = ctx.enter_context(nc.sbuf_tensor("ple_rows", [P, NT, 2 * P], F32))
        ple_loads = embed_loads(k, ctx, "pe", t["p"][i, 0], p_rows, t["w_ple"][i], t["w_ple_gate"][i])
        with ExitStack() as moe:
            weights = (t["w_exp_gate"], t["w_exp_up"], t["w_exp_down"])
            expert_loads = Loads(k, moe, *((f"ex_{n}_landed{u}", expert_pairs(k, u, *(w[i, u] for w in weights))[part])
                                           for u in range(3) for n, part in (("gu", slice(0, 2)), ("down", slice(2, 3)))))
            norm_transpose(k, "ffn", t["g_ffn"][i], (expert_loads,), xn_rows)
            route(k, "rt", r, route_loads)
            experts(k, "ex", r, i, EXPERTS, False, xn_rows, y_rows, *weights, expert_loads)
            spilled = nc.values_load(r.spill_expert[0:1, SPILL:SPILL + 1], min_val=0, max_val=SPILL)
            with nc.If(spilled > 0):
                experts(k, "sp", r, i, SPILL, True, xn_rows, y_rows, *weights)
            combine_experts(k, "cb", r, y_rows, ple_loads)
        norm_transpose(k, "ple", t["g_ple"][i])
        embed_per_layer(k, "pe", p_rows, ple_loads)


def program(nc, t, out, stop=None):
    with ExitStack() as ctx:
        k = Core(nc, ctx)
        k.t = t
        lines = nc.dram_tensor("bias_lines", [BIAS_HEADS, P, LINE], F32).ap()
        k.bias_stored = ctx.enter_context(nc.semaphore("bias_lines_stored"))
        first_stack = ctx.enter_context(ExitStack())
        line = first_stack.enter_context(nc.sbuf_tensor("bias_line", [BIAS_HEADS, LINE], F32))
        load_start(k, t)
        k.cosT = first_stack.enter_context(nc.sbuf_tensor("cos_t", [P, S], F32))
        k.sinT = first_stack.enter_context(nc.sbuf_tensor("sin_t", [P, S], F32))
        rotary_tables(k, t, k.cosT, k.sinT)
        bias_lines(k, t["rel_bias_2"], lines, line, k.bias_stored)
        xn_rows = nc.dram_tensor("xn_rows", [S, D], F32)
        y_rows = nc.dram_tensor("y_rows", [2 * S, D], F32)
        clear_sems(k)
        with nc.Fori(0, DEPTH) as i:
            first_layer(k, t, i, (xn_rows.ap(), y_rows.ap()))
            clear_sems(k)
        if stop == 1:
            return
        first_stack.close()
        final_norm(k, "fn", t["g_final"], wait_for=k.bias_stored)
        second_layer(k, t, lines)
        final_norm(k, "fn2", t["g_final_2"], out)


def constants():
    f = np.float32
    r = np.arange(P)
    half = 8
    swap = np.zeros((P, P), f)
    freq = np.zeros((P, 1), f)
    inv = (f(500000.0) ** (-np.arange(0, 16, 2, dtype=f) / f(16))).astype(f)
    for head in (0, 64):
        for i in range(half):
            swap[head + half + i, head + i] = -1
            swap[head + i, head + half + i] = 1
            freq[head + i] = freq[head + half + i] = inv[i]
    lam_init = np.array([[0.8 - 0.6 * math.exp(-0.3 * i)] for i in range(DEPTH)], f)
    dist = S - 1 - np.arange(LINE)
    far = np.maximum(dist, 1).astype(f)
    exact = BUCKETS // 2
    large = exact + (np.log(far / exact).astype(f) / f(math.log(2048 / exact)) * f(BUCKETS - exact)).astype(np.int32)
    bucket = np.where(dist < exact, np.maximum(dist, 0), np.minimum(large, BUCKETS - 1))
    hot = (np.arange(BUCKETS)[:, None] == bucket[None, :]).astype(f)
    hidden = np.zeros((BIAS_HEADS, LINE), f)
    for g, (window, dilation) in enumerate(WINDOW_GROUPS):
        seen = (dist >= 0) & (dist <= window) & (dist % dilation == 0)
        hidden[g * WINDOW_HEADS:(g + 1) * WINDOW_HEADS] = np.where(seen, f(0), f(NEG))
    hidden[BIAS_HEADS - BLOCK_HEADS:] = np.where(dist >= 0, f(0), f(NEG))
    token = np.arange(S).reshape(NT, P)
    values = np.zeros((P, 8, 2), f)
    for tile in range(NT):
        for c in (0, 1):
            values[:, 2 * tile + c, 0] = token[tile] + 1
            values[:, 2 * tile + c, 1] = 2 * token[tile] + c + 1
    return {
        "c_iota": r.astype(f),
        "c_bucket_hot": hot,
        "c_hidden": hidden,
        "c_before": (r[:, None] < r[None, :]).astype(f),
        "c_slot_values": values,
        "c_ident": np.eye(P, dtype=f),
        "c_neg_tri": -(r[:, None] >= r[None, :]).astype(f),
        "c_chunk_bias": np.where((r[:, None] < 64) & (r[None, :] >= 64), f(NEG), f(0)),
        "c_rope_swap": swap,
        "c_rope_freq": freq,
        "c_lam_init": lam_init,
        "c_keep": (1.0 - lam_init.astype(np.float64)).astype(f),
        "c_strict_bias": np.where(r[:, None] < r[None, :], f(0), f(NEG)),
    }



_INPUTS = (
    "x p positions g_mix w_in lam_q1 lam_k1 lam_q2 lam_k2 g_subln w_br_a w_br_b w_o g_ffn w_router_group b_router_group "
    "w_router_expert b_router_expert w_exp_gate w_exp_up w_exp_down g_ple w_ple w_ple_gate g_final rel_bias_2 g_mix_2 "
    "w_in_2 conv_w_2 conv_b_2 lru_wa_2 lru_ba_2 lru_wx_2 lru_bx_2 lru_lam_2 p_a_2 p_b_2 p_c_2 w_out_2 g_ffn_2 w_gu_2 "
    "w_down_2 g_final_2").split()


def kernel(**inputs):
    import concourse.bacc as bacc
    from concourse.bass_utils import run_bass_kernel_spmd

    nc = bacc.Bacc("TRN2", target_bir_lowering=False, num_devices=1)
    arrays, t = {}, {}
    given = {name: np.ascontiguousarray(inputs[name]) for name in _INPUTS}
    for name, a in {**given, **constants()}.items():
        arrays["in_" + name] = a
        t[name] = nc.dram_tensor("in_" + name, a.shape, mybir.dt.from_np(a.dtype), kind="ExternalInput").ap()
    out = nc.dram_tensor("out_0", (1, S, D), F32, kind="ExternalOutput").ap()
    program(nc, t, out)
    r = run_bass_kernel_spmd(nc, [arrays], core_ids=[0])
    return r.results[0]["out_0"]
```

```python
from contextlib import ExitStack
import math

import numpy as np
import concourse.bass as bass
from concourse import mybir

F32 = mybir.dt.float32
I32 = mybir.dt.int32
U32 = mybir.dt.uint32
ALU = mybir.AluOpType
F32R = mybir.dt.float32r
ACT = mybir.ActivationFunctionType
AX = mybir.AxisListType

P = 128
D = 1024
S = 512
NT = S // P
DC = D // P
DEPTH = 2
EPS = 1e-6
NEG = -1e30
HD = 64
SCALE = HD ** -0.5
RING = 13312
EXTRA = 6144


class Core:

    def __init__(self, nc, ctx):
        def sb(name, shape, dt=F32):
            return ctx.enter_context(nc.sbuf_tensor(name, shape, dt))

        self.nc = nc
        self.used_sems = set()
        self.ps = ctx.enter_context(nc.psum_tensor("banks", [P, 8, 512], F32))
        self.x = sb("x_tokens", [P, NT, D])
        self.hT = sb("h_transposed", [P, DC, S])
        self.ident = sb("identity", [P, P])
        self.neg_tri = sb("neg_tri", [P, P])
        self.neg_ones = sb("neg_ones", [P, P])
        self.strict_bias = sb("strict_bias", [P, P])
        self.chunk_bias = sb("chunk_bias", [P, P])
        self.rope_swap = sb("rope_swap", [P, P])
        self.ring_scope = ctx.enter_context(ExitStack())
        self.ring = self.ring_scope.enter_context(nc.sbuf_tensor("weight_ring", [P, RING], F32))

    def extend(self, ctx, tag):
        self.extra = ctx.enter_context(self.nc.sbuf_tensor(tag + "_ring_extension", [P, EXTRA], F32))

    def slot(self, offset, chunks, cols):
        words = chunks * cols
        if offset >= RING:
            return self.extra[:, offset - RING:offset - RING + words].rearrange("p (c n) -> p c n", c=chunks)
        assert offset + words <= RING
        return self.ring[:, offset:offset + words].rearrange("p (c n) -> p c n", c=chunks)


def sems(k, ctx, names):
    found = [ctx.enter_context(k.nc.semaphore(n)) for n in names.split()]
    assert not k.used_sems & {x.num for x in found}
    k.used_sems |= {x.num for x in found}
    return found


def clear_sems(k, keep=()):
    k.nc.gpsimd.dma_reset()
    kept = {x.num for x in keep}
    done = k.used_sems - kept
    starts = [num for num in sorted(done) if num - 1 not in done]
    ends = [num for num in sorted(done) if num + 1 not in done]
    for start, end in zip(starts, ends):
        k.nc.gpsimd.sem_clear(range(start, end + 1))
    k.used_sems = kept
    k.nc.all_engine_barrier()


class Loads:

    def __init__(self, k, ctx, *groups):
        self.landed = sems(k, ctx, " ".join(name for name, _ in groups))
        self.groups = [pairs for _, pairs in groups]

    def issue(self, sp):
        for landed, pairs in zip(self.landed, self.groups):
            for dst, src in pairs:
                sp.dma_start(dst, src).then_inc(landed, 16)


def rows_pc(w):
    return w.rearrange("(p c) n -> p c n", c=DC)



def mask_low_bits(nc, dst, src):
    return nc.vector.tensor_scalar(dst.bitcast(I32), src.bitcast(I32), -4096, None, ALU.bitwise_and)


def split_product(nc, out, a, b, start, stop):
    for n, (left, right) in enumerate(((a[0], b[0]), (a[0], b[1]), (a[1], b[0]))):
        last = nc.tensor.matmul(out, left, right, start=(start and n == 0), stop=(stop and n == 2))
    return last



def load_start(k, t, ctx):
    return Loads(k, ctx, ("start_landed", [
        (k.x[:], t["x"].rearrange("b (t p) d -> p (b t) d", p=P)), (k.ident[:], t["c_ident"]),
        (k.neg_tri[:], t["c_neg_tri"]), (k.strict_bias[:], t["c_strict_bias"]), (k.chunk_bias[:], t["c_chunk_bias"]),
        (k.rope_swap[:], t["c_rope_swap"])]))



def inverse_rms(nc, k, ss, squares, squares_done, mean_ready, root_ready, rstd_ready):
    def on_scalar(act):
        for t in (0, 1):
            nc.scalar.activation(k.ps[:, 2 * t:2 * t + 2, :], k.x[:, t, :].rearrange("p (a n) -> p a n", a=2),
                                 ACT.Square, accum_out=ss[:, t:t + 1]).then_inc(squares_done, 1)
        act.wait_ge(mean_ready, 1)
        nc.scalar.activation(ss[:], ss[:], ACT.Sqrt).then_inc(root_ready, 1)

    def on_vector(dve):
        for n, t in enumerate((2, 3)):
            nc.vector.tensor_tensor_reduce(out=squares[:, n, :], in0=k.x[:, t, :], in1=k.x[:, t, :], scale=1.0, scalar=0.0,
                                           op0=ALU.mult, op1=ALU.add, accum_out=ss[:, t:t + 1]).then_inc(squares_done, 1)
        dve.wait_ge(squares_done, NT)
        nc.vector.tensor_scalar(ss[:], ss[:], 1.0 / D, EPS, ALU.mult, ALU.add).then_inc(mean_ready, 1)
        dve.wait_ge(root_ready, 1)
        nc.vector.reciprocal(ss[:], ss[:]).then_inc(rstd_ready, 1)
        dve.wait_ge(rstd_ready, 1)

    return on_scalar, on_vector


def norm_transpose(k, tag, gain, ahead=(), rows=None):
    nc = k.nc
    with ExitStack() as ctx:
        xn = ctx.enter_context(nc.sbuf_tensor(tag + "_xn", [P, NT, D], F32))
        ss = ctx.enter_context(nc.sbuf_tensor(tag + "_ss", [P, NT], F32))
        g = ctx.enter_context(nc.sbuf_tensor(tag + "_g", [P, DC], F32))
        gain_landed, squares_done, mean_ready, root_ready, rstd_ready, xn_act, xn_dve, turned, stored = sems(
            k, ctx, " ".join(tag + n for n in "_gain _squares _mean _root _rstd _xn_act _xn_dve _turned _stored".split()))
        rms_on_scalar, rms_on_vector = inverse_rms(nc, k, ss, xn[:, 2:4, :], squares_done, mean_ready, root_ready, rstd_ready)
        block = ctx.enter_context(nc.Block())

        @block.sync
        def _(sp):
            if rows is not None:
                sp.wait_ge(xn_act, 2)
                sp.wait_ge(xn_dve, 2)
                sp.dma_start(rows.rearrange("(t p) d -> p t d", p=P), xn[:]).then_inc(stored, 16)
            for loads in ahead:
                loads.issue(sp)
            if rows is not None:
                sp.wait_ge(stored, 16)

        @block.scalar
        def _(act):
            nc.scalar.dma_start(g[:], gain.rearrange("(p c) -> p c", c=DC)).then_inc(gain_landed, 16)
            rms_on_scalar(act)
            act.wait_ge(rstd_ready, 1)
            for t in (0, 1):
                nc.scalar.activation(xn[:, t, :], k.x[:, t, :], ACT.Copy, scale=ss[:, t:t + 1]).then_inc(xn_act, 1)
            act.wait_ge(gain_landed, 16)
            for c in range(1, DC, 2):
                act.wait_ge(turned, c + 1)
                nc.scalar.activation(k.hT[:, c, :], k.ps[:, c, :], ACT.Copy, scale=g[:, c:c + 1])

        @block.vector
        def _(dve):
            rms_on_vector(dve)
            for t in (2, 3):
                nc.vector.tensor_scalar(xn[:, t, :], k.x[:, t, :], ss[:, t:t + 1], None, ALU.mult).then_inc(xn_dve, 1)
            dve.wait_ge(gain_landed, 16)
            for c in range(0, DC, 2):
                dve.wait_ge(turned, c + 1)
                nc.vector.tensor_scalar(k.hT[:, c, :], k.ps[:, c, :], g[:, c:c + 1], None, ALU.mult)

        @block.tensor
        def _(pe):
            for n, t in enumerate((0, 2, 1, 3)):
                pe.wait_ge(xn_dve if t >= 2 else xn_act, n // 2 + 1)
                for c in range(DC):
                    last = nc.tensor.transpose(k.ps[:, c, t * P:(t + 1) * P], xn[:, t, c::DC], k.ident[:])
                    if n == NT - 1:
                        last.then_inc(turned, 1)



def projection(nc, k, bank, kind, w, quantum):
    if kind < 2:
        last = nc.tensor.matmul(k.ps[:, bank, :], w[:, quantum, :], k.hT[:, quantum, :], start=(quantum == 0),
                                stop=(quantum == DC - 1))
    else:
        t, half = divmod(quantum, 2)
        for c in range(half * 4, half * 4 + 4):
            last = nc.tensor.matmul(k.ps[:, bank, t * P:(t + 1) * P], k.hT[:, c, t * P:(t + 1) * P], w[:, c, :],
                                    start=(c == 0), stop=(c == DC - 1))
    return last


def qkv_loads(k, ctx, tag, base, w_in, offs):
    slots = [k.slot(base + n * DC * P, DC, P) for n in range(len(offs))]
    loads = Loads(k, ctx, *((f"{tag}_landed{n}", [(dst, rows_pc(w_in)[:, :, off:off + P])])
                            for n, (dst, off) in enumerate(zip(slots, offs))))
    loads.slots = slots
    return loads


def spread_eighths():
    eighths = [(m, c) for m in range(3) for c in range(8)]
    return [eighths[3 * n:3 * n + 2] for n in range(8)], [eighths[3 * n + 2:3 * n + 3] for n in range(8)]


def stick_breaking(k, w_in, off_q, off_k, off_v, yT, first, following, opened):
    nc = k.nc
    pairs = 4
    steps = 8 * pairs
    w = rows_pc(w_in)
    before, after = spread_eighths()
    banks = (4, 5, 6)
    with ExitStack() as ctx:
        def sb(name, shape):
            return ctx.enter_context(nc.sbuf_tensor("sb_" + name, shape, F32))

        qT, kT, v = sb("qT", [P, 2, S]), sb("kT", [P, 2, S]), sb("v", [P, 2, NT, P])
        mag = sb("mag", [P, 2, S])
        stay = sb("stay", [P, 8, S])
        prob = sb("prob", [P, 8, S])
        projected, q_ready, k_ready, v_ready, z_done, act_step, stay_done, logit_done, exp_done, \
            pv_done, y_out = sems(k, ctx, " ".join("sb_" + n for n in (
                "projected q_ready k_ready v_ready z_done act_step stay_done logit_done exp_done "
                "pv_done y_out").split()))
        block = ctx.enter_context(nc.Block())

        def place(s):
            j = 3 - s % 4
            return s % 8 // 4, j, S - P * j

        @block.sync
        def _(sp):
            following.issue(sp)
            with sp.Fori(1, pairs) as it:
                for n, off in enumerate((off_q, off_k, off_v)):
                    sp.wait_ge(projected, 3 * it + (n - 2))
                    sp.dma_start(first.slots[n], w[:, :, bass.ds(off + it * P, P)]).then_inc(first.landed[n], 16)

        @block.tensor
        def _(pe):
            def project(pair, part):
                loads, count, done = (first, pair + 1, projected) if pair < pairs else (following, 1, opened)
                for m, c in part:
                    if c == 0:
                        pe.wait_ge(loads.landed[m], 16 * count)
                        wait(pe, (q_ready, k_ready, v_ready)[m], pair)
                    last = projection(nc, k, banks[m], m, loads.slots[m], c)
                    if c == 7:
                        last.then_inc(done, 1)

            def scores(s):
                h, j, cols = place(s)
                pair = s // 8
                if s % 8 == 0:
                    pe.wait_ge(q_ready, pair + 1)
                    pe.wait_ge(k_ready, pair + 1)
                wait(pe, exp_done, s - 3)
                nc.tensor.matmul(k.ps[:, s % 4, 0:cols], kT[64 * h:64 * h + 64, pair % 2, j * P:(j + 1) * P],
                                 qT[64 * h:64 * h + 64, pair % 2, j * P:S], start=True, stop=False,
                                 skip_group_check=True)
                nc.tensor.matmul(k.ps[:, s % 4, 0:P], k.ident[:], k.strict_bias[:], start=False, stop=False,
                                 skip_group_check=True).then_inc(z_done, 1)

            def cumulate(s):
                h, j, cols = place(s)
                pe.wait_ge(stay_done, s + 1)
                for jj in range(j, NT):
                    tri = k.neg_tri if jj == j else k.neg_ones
                    last = nc.tensor.matmul(k.ps[:, s % 4, (jj - j) * P:cols], tri[:],
                                            stay[:, 4 * h + 3 - jj, jj * P:S], start=False, stop=(jj == NT - 1),
                                            skip_group_check=True)
                last.then_inc(logit_done, 1)

            def weigh(head):
                pair, h = divmod(head, 2)
                if h == 0:
                    wait(pe, y_out, pair)
                    pe.wait_ge(v_ready, pair + 1)
                pe.wait_ge(exp_done, 4 * head + 4)
                for j in range(NT):
                    last = nc.tensor.matmul(k.ps[64 * h:64 * h + 64, 7, j * P:S], v[:, pair % 2, j, 64 * h:64 * h + 64],
                                            prob[:, 4 * h + 3 - j, j * P:S], start=(j == 0), stop=(j == NT - 1),
                                            skip_group_check=True)
                last.then_inc(pv_done, 1)

            for m in range(3):
                project(0, [(m, c) for c in range(8)])
            scores(0)
            scores(1)
            for s in range(steps):
                if s + 2 < steps:
                    scores(s + 2)
                project(s // 8 + 1, before[s % 8])
                cumulate(s)
                project(s // 8 + 1, after[s % 8])
                if s and s % 4 == 0:
                    weigh(s // 4 - 1)
            weigh(2 * pairs - 1)

        @block.scalar
        def _(act):
            def take_q(pair):
                act.wait_ge(projected, 3 * pair + 1)
                nc.scalar.activation(qT[:, pair % 2, :], k.ps[:, banks[0], :], ACT.Copy, scale=SCALE).then_inc(q_ready, 1)

            def take_result(pair):
                act.wait_ge(pv_done, 2 * pair + 2)
                nc.scalar.activation(yT[:, pair, :], k.ps[:, 7, :], ACT.Copy).then_inc(y_out, 1)

            def final(s):
                _, j, cols = place(s)
                act.wait_ge(logit_done, s + 1)
                nc.scalar.activation(prob[:, s % 8, j * P:S], k.ps[:, s % 4, 0:cols], ACT.Exp).then_inc(exp_done, 1)

            act.preload_act_table_set("natural_log_exp_and_others")
            take_q(0)
            for s in range(steps):
                _, j, cols = place(s)
                a = mag[:, s % 2, 0:cols]
                act.wait_ge(z_done, s + 1)
                wait(act, stay_done, s - 1)
                nc.scalar.activation(a, k.ps[:, s % 4, 0:cols], ACT.Abs).then_inc(act_step, 1)
                act.wait_ge(act_step, 3 * s + 1)
                nc.scalar.activation(a, a, ACT.Exp, scale=-1.0).then_inc(act_step, 1)
                act.wait_ge(act_step, 3 * s + 2)
                nc.scalar.activation(a, a, ACT.Ln, bias=1.0).then_inc(act_step, 1)
                if s:
                    final(s - 1)
                if s % 8 == 2 and s // 8 + 1 < pairs:
                    take_q(s // 8 + 1)
                if s % 8 == 1 and s > 8:
                    take_result(s // 8 - 1)
            final(steps - 1)
            take_result(pairs - 1)

        @block.vector
        def _(dve):
            def take(pair, m):
                dve.wait_ge(projected, 3 * pair + m + 1)
                if m == 1:
                    nc.vector.tensor_copy(kT[:, pair % 2, :], k.ps[:, banks[1], :]).then_inc(k_ready, 1)
                else:
                    nc.vector.tensor_copy(v[:, pair % 2, :, :], k.ps[:, banks[2], :].rearrange("p (t n) -> p t n", t=NT))\
                        .then_inc(v_ready, 1)

            take(0, 1)
            take(0, 2)
            for s in range(steps):
                _, j, cols = place(s)
                dve.wait_ge(act_step, 3 * s + 3)
                nc.vector.scalar_tensor_tensor(out=stay[:, s % 8, j * P:S], in0=k.ps[:, s % 4, 0:cols],
                                               scalar=0.0, in1=mag[:, s % 2, 0:cols],
                                               op0=ALU.max, op1=ALU.add).then_inc(stay_done, 1)
                if s // 8 + 1 < pairs and s % 8 in (5, 7):
                    take(s // 8 + 1, 1 if s % 8 == 5 else 2)



def rotary_tables(k, t, cosT, sinT, start):
    nc = k.nc
    two_pi = (6.28125, 0.0019353071693331003, 1.0253131677018246e-11)
    magic = 12582912.0
    lim = 3.1415925
    with ExitStack() as ctx:
        def sb(name, shape, dt=F32):
            return ctx.enter_context(nc.sbuf_tensor("rot_" + name, shape, dt))

        pos_i, freq = sb("pos_i", [P, S], I32), sb("freq", [P, 1])
        ang, turn = sb("ang", [P, S]), sb("turn", [P, 2, S])
        landed, step, reduced = sems(k, ctx, "rot_landed rot_step rot_reduced")
        block = ctx.enter_context(nc.Block())

        @block.sync
        def _(sp):
            sp.dma_start(pos_i[:], t["positions"][0, :].partition_broadcast(P)).then_inc(landed, 16)
            sp.dma_start(freq[:], t["c_rope_freq"]).then_inc(landed, 16)
            start.issue(sp)
            sp.wait_ge(start.landed[0], 16 * 6)

        @block.vector
        def _(dve):
            done = [0]

            def link(ins):
                ins.then_inc(step, 1)
                done[0] += 1
                dve.wait_ge(step, done[0])

            nc.vector.memset(k.neg_ones[:], -1.0)
            dve.wait_ge(landed, 32)
            link(nc.vector.tensor_copy(ang[:], pos_i[:]))
            link(nc.vector.tensor_scalar(ang[:], ang[:], freq[:], None, ALU.mult))
            for n, (quarter, dst) in enumerate(((0.0, sinT), (0.25, cosT))):
                u = turn[:, n, :]
                link(nc.vector.tensor_scalar(u, ang[:], 1.0 / (2 * math.pi), quarter, ALU.mult, ALU.add))
                link(nc.vector.tensor_scalar(u, u, magic, None, ALU.add))
                link(nc.vector.tensor_scalar(u, u, -magic, None, ALU.add))
                src = ang
                for part in two_pi:
                    link(nc.vector.scalar_tensor_tensor(out=dst[:], in0=u, scalar=-part, in1=src[:],
                                                        op0=ALU.mult, op1=ALU.add))
                    src = dst
                link(nc.vector.tensor_scalar(dst[:], dst[:], quarter * 2 * math.pi, None, ALU.add))
                nc.vector.tensor_scalar(dst[:], dst[:], lim, -lim, ALU.min, ALU.max).then_inc(reduced, 1)

        @block.scalar
        def _(act):
            for n, dst in enumerate((sinT, cosT)):
                act.wait_ge(reduced, n + 1)
                nc.scalar.activation(dst[:], dst[:], ACT.Sin)



def differential(k, w_in, off_q, off_k, off_v, lams, gain, lam_init, keep, cosT, sinT, yT, first, opened, ahead):
    nc = k.nc
    heads = 4
    steps = heads * NT
    w = rows_pc(w_in)
    matrices = first.slots
    before = [[(0, c) for c in range(5)], [(1, c) for c in range(4)], [], [(2, c) for c in range(4, 8)]]
    after = [[(0, c) for c in range(5, 8)], [(1, c) for c in range(4, 8)], [(2, c) for c in range(4)], []]
    with ExitStack() as ctx:
        def sb(name, shape):
            return ctx.enter_context(nc.sbuf_tensor("da_" + name, shape, F32))

        raw = sb("raw", [P, 2, S])
        turned_part = sb("turned_part", [P, 2, S])
        qT, kT, v = sb("qT", [P, 2, S]), sb("kT", [P, 2, S]), sb("v", [P, 2, NT, P])
        probs = sb("probs", [P, 2, 2, S])
        diff = sb("diff", [P, 2, S])
        diffT = sb("diffT", [P, 2, S])
        neg_max, sums, coef = sb("neg_max", [P, 2 * NT]), sb("sums", [P, 2 * NT]), sb("coef", [P, NT])
        y, squares = sb("y", [P, 2, NT, P]), sb("squares", [P, P])
        ss = sb("ss", [P, 2, NT])
        lam_in, lam_dot, neg_lam = sb("lam_in", [P, 4, HD]), sb("lam_dot", [P, 4]), sb("neg_lam", [P, 1])
        lam_prod, scale_col, lam_const = sb("lam_prod", [P, HD]), sb("scale_col", [P, 1]), sb("lam_const", [P, 2])
        names = ("lam_landed lam_step lam_exp raw_ready v_ready swapped rope_step "
                 "qk_ready s_done max_done exp_done diff_step diff_done turned diffT_ready pv_done y_scaled "
                 "squared mean_ready log_ready rstd_ready normed yT_done y_out")
        sem = dict(zip(names.split(), sems(k, ctx, " ".join("da_" + n for n in names.split()))))
        sem["projected"] = opened
        block = ctx.enter_context(nc.Block())

        @block.sync
        def _(sp):
            def load(it):
                for n, off in enumerate((off_q, off_k, off_v)):
                    sp.wait_ge(sem["projected"], 3 * it + (n - 2))
                    sp.dma_start(matrices[n], w[:, :, bass.ds(off + it * P, P)]).then_inc(first.landed[n], 16)

            for n, lam in enumerate(lams):
                sp.dma_start(lam_in[:, n, :], lam.partition_broadcast(P)).then_inc(sem["lam_landed"], 16)
            sp.dma_start(scale_col[:], gain.rearrange("(p a) -> p a", a=1)).then_inc(sem["lam_landed"], 16)
            sp.dma_start(lam_const[:, 0:1], lam_init.partition_broadcast(P)).then_inc(sem["lam_landed"], 16)
            sp.dma_start(lam_const[:, 1:2], keep.partition_broadcast(P)).then_inc(sem["lam_landed"], 16)
            load(1)
            ahead.issue(sp)
            with sp.Fori(2, heads) as it:
                load(it)

        @block.tensor
        def _(pe):
            def project(head, part, bank):
                for n, c in part:
                    if c == 0:
                        pe.wait_ge(first.landed[n], 16 * (head + 1))
                        if head and n == 0:
                            pe.wait_ge(sem["v_ready"], head)
                        if head and n == 2:
                            pe.wait_ge(sem["rope_step"], 4 * head + 3)
                    last = projection(nc, k, bank, n, matrices[n], c)
                    if c == 7:
                        last.then_inc(sem["projected"], 1)

            def swap(head, n, bank):
                pe.wait_ge(sem["raw_ready"], 2 * head + n + 1)
                nc.tensor.matmul(k.ps[:, bank, :], k.rope_swap[:], raw[:, n, :], start=True,
                                 stop=True).then_inc(sem["swapped"], 1)

            def scores(s):
                head, t = divmod(s, NT)
                n = (t + 1) * P
                if t == 0:
                    pe.wait_ge(sem["qk_ready"], 2 * head + 2)
                wait(pe, sem["exp_done"], 2 * (s - 1))
                for m in (0, 1):
                    half = slice(64 * m, 64 * m + 64)
                    bank = 2 * (s % 2) + m
                    nc.tensor.matmul(k.ps[:, bank, 0:n], qT[half, head % 2, t * P:n], kT[half, head % 2, 0:n],
                                     start=True, stop=False)
                    last = nc.tensor.matmul(k.ps[:, bank, t * P:n], k.ident[:], k.chunk_bias[:], start=False, stop=True)
                last.then_inc(sem["s_done"], 1)

            def turn_result(head):
                pe.wait_ge(sem["normed"], NT * (head + 1))
                for t in range(NT):
                    last = nc.tensor.transpose(k.ps[:, 5, t * P:(t + 1) * P], y[:, head % 2, t, :], k.ident[:])
                last.then_inc(sem["yT_done"], 1)

            swap(0, 0, 0)
            swap(0, 1, 1)
            scores(0)
            for s in range(steps):
                head, t = divmod(s, NT)
                more = head + 1 < heads
                if s + 1 < steps:
                    scores(s + 1)
                if t == 1 and head:
                    if more:
                        pe.wait_ge(sem["raw_ready"], 2 * head + 3)
                    turn_result(head - 1)
                if more:
                    project(head + 1, before[t], (5, 7, 5, 5)[t])
                    if t == 2:
                        wait(pe, sem["y_out"], head)
                        swap(head + 1, 0, 5)
                        swap(head + 1, 1, 7)
                if t == 0:
                    pe.wait_ge(sem["v_ready"], head + 1)
                pe.wait_ge(sem["diff_done"], s + 1)
                for b in range(t + 1):
                    last = nc.tensor.transpose(k.ps[:, 4, b * P:(b + 1) * P], diff[:, s % 2, b * P:(b + 1) * P], k.ident[:])
                last.then_inc(sem["turned"], 1)
                if more:
                    project(head + 1, after[t], (5, 7, 5, 5)[t])
                pe.wait_ge(sem["diffT_ready"], s + 1)
                wait(pe, sem["y_scaled"], s - 1)
                for b in range(t + 1):
                    last = nc.tensor.matmul(k.ps[:, 6, s % 2 * P:(s % 2 + 1) * P], diffT[:, s % 2, b * P:(b + 1) * P],
                                            v[:, head % 2, b, :], start=(b == 0), stop=(b == t))
                last.then_inc(sem["pv_done"], 1)
            turn_result(heads - 1)

        @block.scalar
        def _(act):
            def take_raw(head, n, bank):
                act.wait_ge(sem["projected"], 3 * head + n + 1)
                nc.scalar.activation(raw[:, n, :], k.ps[:, bank, :], ACT.Copy,
                                     scale=1.0 if n else SCALE).then_inc(sem["raw_ready"], 1)

            def exps(s):
                t = s % NT
                n = (t + 1) * P
                act.wait_ge(sem["max_done"], s + 1)
                wait(act, sem["diff_done"], s - 1)
                for m in (0, 1):
                    nc.scalar.activation(probs[:, s % 2, m, 0:n], k.ps[:, 2 * (s % 2) + m, 0:n], ACT.Exp,
                                         bias=neg_max[:, 2 * t + m:2 * t + m + 1],
                                         accum_out=sums[:, 2 * t + m:2 * t + m + 1]).then_inc(sem["exp_done"], 1)

            def scale_result(s):
                head, t = divmod(s, NT)
                act.wait_ge(sem["pv_done"], s + 1)
                nc.scalar.activation(y[:, head % 2, t, :], k.ps[:, 6, s % 2 * P:(s % 2 + 1) * P], ACT.Copy,
                                     scale=sums[:, 2 * t:2 * t + 1]).then_inc(sem["y_scaled"], 1)
                act.wait_ge(sem["y_scaled"], s + 1)
                nc.scalar.activation(squares[:], y[:, head % 2, t, :], ACT.Square,
                                     accum_out=ss[:, head % 2, t:t + 1]).then_inc(sem["squared"], 1)

            def inverse_root(head):
                one = ss[:, head % 2, :]
                act.wait_ge(sem["mean_ready"], head + 1)
                nc.scalar.activation(one, one, ACT.Ln).then_inc(sem["log_ready"], 1)
                act.wait_ge(sem["log_ready"], head + 1)
                nc.scalar.activation(one, one, ACT.Exp, scale=-0.5).then_inc(sem["rstd_ready"], 1)

            def take_result(head):
                act.wait_ge(sem["yT_done"], head + 1)
                nc.scalar.activation(yT[:, head, :], k.ps[:, 5, :], ACT.Copy, scale=scale_col[:]).then_inc(sem["y_out"], 1)

            act.preload_act_table_set("natural_log_exp_and_others")
            take_raw(0, 0, 4)
            take_raw(0, 1, 5)
            act.wait_ge(sem["lam_step"], 2)
            nc.scalar.activation(lam_dot[:, 2:4], lam_dot[:, 0:2], ACT.Exp).then_inc(sem["lam_exp"], 1)
            exps(0)
            for s in range(steps):
                head, t = divmod(s, NT)
                if s + 1 < steps:
                    exps(s + 1)
                if s:
                    scale_result(s - 1)
                act.wait_ge(sem["turned"], s + 1)
                nc.scalar.activation(diffT[:, s % 2, 0:(t + 1) * P], k.ps[:, 4, 0:(t + 1) * P],
                                     ACT.Copy).then_inc(sem["diffT_ready"], 1)
                if t == 0:
                    if head + 1 < heads:
                        take_raw(head + 1, 0, 5)
                    if head:
                        inverse_root(head - 1)
                if t == 1:
                    if head:
                        take_result(head - 1)
                    if head + 1 < heads:
                        take_raw(head + 1, 1, 7)
            scale_result(steps - 1)
            inverse_root(heads - 1)
            take_result(heads - 1)

        @block.vector
        def _(dve):
            def cos_part(head, n):
                dve.wait_ge(sem["raw_ready"], 2 * head + n + 1)
                nc.vector.tensor_tensor(turned_part[:, n, :], raw[:, n, :], cosT[:], ALU.mult)\
                    .then_inc(sem["rope_step"], 1)

            def sin_part(head, n, bank):
                dst = (qT, kT)[n][:, head % 2, :]
                dve.wait_ge(sem["swapped"], 2 * head + n + 1)
                nc.vector.tensor_tensor(dst, k.ps[:, bank, :], sinT[:], ALU.mult).then_inc(sem["rope_step"], 1)
                dve.wait_ge(sem["rope_step"], 4 * head + 3 + n)
                nc.vector.tensor_tensor(dst, dst, turned_part[:, n, :], ALU.add).then_inc(sem["qk_ready"], 1)

            def take_v(head, bank):
                dve.wait_ge(sem["projected"], 3 * head + 3)
                nc.vector.tensor_copy(v[:, head % 2, :, :], k.ps[:, bank, :].rearrange("p (t n) -> p t n", t=NT))\
                    .then_inc(sem["v_ready"], 1)

            def maxima(s):
                t, b = s % NT, 2 * (s % 2)
                dve.wait_ge(sem["s_done"], s + 1)
                nc.vector.tensor_reduce(out=neg_max[:, 2 * t:2 * t + 2], in_=k.ps[:, b:b + 2, 0:(t + 1) * P],
                                        axis=AX.X, op=ALU.max, negate=True).then_inc(sem["max_done"], 1)

            def difference(s):
                t = s % NT
                n = (t + 1) * P
                dve.wait_ge(sem["exp_done"], 2 * s + 2)
                nc.vector.reciprocal(coef[:, t:t + 1], sums[:, 2 * t + 1:2 * t + 2]).then_inc(sem["diff_step"], 1)
                dve.wait_ge(sem["diff_step"], 3 * s + 1)
                nc.vector.scalar_tensor_tensor(out=coef[:, t:t + 1], in0=coef[:, t:t + 1], scalar=neg_lam[:],
                                               in1=sums[:, 2 * t:2 * t + 1], op0=ALU.mult,
                                               op1=ALU.mult).then_inc(sem["diff_step"], 1)
                dve.wait_ge(sem["diff_step"], 3 * s + 2)
                nc.vector.reciprocal(sums[:, 2 * t:2 * t + 1], sums[:, 2 * t:2 * t + 1]).then_inc(sem["diff_step"], 1)
                nc.vector.scalar_tensor_tensor(out=diff[:, s % 2, 0:n], in0=probs[:, s % 2, 1, 0:n],
                                               scalar=coef[:, t:t + 1], in1=probs[:, s % 2, 0, 0:n],
                                               op0=ALU.mult, op1=ALU.add).then_inc(sem["diff_done"], 1)

            def norm(head):
                one = ss[:, head % 2, :]
                dve.wait_ge(sem["squared"], NT * (head + 1))
                nc.vector.tensor_scalar(one, one, 1.0 / P, EPS, ALU.mult, ALU.add).then_inc(sem["mean_ready"], 1)
                dve.wait_ge(sem["rstd_ready"], head + 1)
                for t in range(NT):
                    nc.vector.tensor_scalar(y[:, head % 2, t, :], y[:, head % 2, t, :], ss[:, head % 2, t:t + 1], None,
                                            ALU.mult).then_inc(sem["normed"], 1)

            def negated_lambda():
                dve.wait_ge(sem["lam_landed"], 16 * 7)
                for n in (0, 1):
                    nc.vector.tensor_tensor_reduce(out=lam_prod[:], in0=lam_in[:, 2 * n, :], in1=lam_in[:, 2 * n + 1, :],
                                                   scale=1.0, scalar=0.0, op0=ALU.mult, op1=ALU.add,
                                                   accum_out=lam_dot[:, n:n + 1]).then_inc(sem["lam_step"], 1)
                    dve.wait_ge(sem["lam_step"], n + 1)
                dve.wait_ge(sem["lam_exp"], 1)
                nc.vector.tensor_tensor(neg_lam[:], lam_dot[:, 3:4], lam_dot[:, 2:3], ALU.subtract).then_inc(sem["lam_step"], 1)
                dve.wait_ge(sem["lam_step"], 3)
                nc.vector.tensor_tensor(neg_lam[:], neg_lam[:], lam_const[:, 0:1], ALU.subtract).then_inc(sem["lam_step"], 1)
                nc.vector.tensor_tensor(scale_col[:], scale_col[:], lam_const[:, 1:2], ALU.mult).then_inc(sem["lam_step"], 1)
                dve.wait_ge(sem["lam_step"], 5)

            for n in (0, 1):
                cos_part(0, n)
            for n in (0, 1):
                sin_part(0, n, n)
            take_v(0, 6)
            maxima(0)
            negated_lambda()
            for s in range(steps):
                head, t = divmod(s, NT)
                if s + 1 < steps:
                    maxima(s + 1)
                difference(s)
                if t == 0 and head:
                    norm(head - 1)
                if head + 1 < heads:
                    if t == 2:
                        cos_part(head + 1, 0)
                        cos_part(head + 1, 1)
                        sin_part(head + 1, 0, 5)
                        sin_part(head + 1, 1, 7)
                    if t == 3:
                        take_v(head + 1, 5)
            norm(heads - 1)



def every(eng, blocks, per_round, step):
    rounds = -(-blocks // per_round)
    for u in range(min(per_round, blocks)):
        step(0, u)
    if rounds > 3:
        with eng.Fori(1, rounds - 2) as it:
            for u in range(per_round):
                step(it, u)
    for it in range(max(1, rounds - 2), rounds):
        for u in range(min(per_round, blocks - it * per_round)):
            step(it, u)


def wait(eng, sem, value):
    if not isinstance(value, int) or value > 0:
        eng.wait_ge(sem, value)


class MergePlan:

    SLOTS = 4
    WORDS = (DC + 4) * P

    def __init__(self, k, ctx, tag, base, w_in, gates, branches):
        self.w, self.gates, self.branches = rows_pc(w_in), gates, branches
        self.slots = [(k.slot(base + n * self.WORDS, DC, P), k.slot(base + n * self.WORDS + DC * P, 4, P))
                      for n in range(self.SLOTS)]
        self.first = Loads(k, ctx, *((f"{tag}_landed{i}", self.pairs(i)) for i in range(self.SLOTS)))

    def pairs(self, i):
        chunk, b = divmod(i, len(self.gates))
        gate_at, branch_at = self.slots[i % self.SLOTS]
        w_branch, _, n = self.branches[b]
        return [(gate_at, self.w[:, :, self.gates[b] + chunk * P:][:, :, 0:P]),
                (branch_at[:, 0:n, :], w_branch.rearrange("(c p) n -> p c n", p=P)[:, :, chunk * P:(chunk + 1) * P])]


def merge(k, tag, plan, mergedT, ahead):
    nc = k.nc
    nb, slots = len(plan.gates), plan.SLOTS
    units = DC * nb
    landed = plan.first.landed
    with ExitStack() as ctx:
        def sb(name, shape, dt=F32):
            return ctx.enter_context(nc.sbuf_tensor(tag + "_" + name, shape, dt))

        hT_high, hT_low = sb("hT_high", [P, DC, S], F32R), sb("hT_low", [P, DC, S], F32R)
        masked_w = sb("masked_w", [P, DC * P])
        high_w, low_w = sb("high_w", [P, 2, DC * P], F32R), sb("low_w", [P, 2, DC * P], F32R)
        sig, part = sb("sig", [P, 2, S]), sb("part", [P, 2, S])
        hT_mask_done, hT_high_ready, hT_low_ready, masked, high_ready, low_ready, multiplied, sig_done, weighed, summed = sems(
            k, ctx, " ".join(tag + n for n in ("_hT_mask_done _hT_high_ready _hT_low_ready _masked _high_ready _low_ready "
                                               "_multiplied _sig_done _weighed _summed").split()))
        block = ctx.enter_context(nc.Block())

        def hT_masked(c):
            return masked_w[:, c % 2 * S:(c % 2 + 1) * S]

        @block.sync
        def _(sp):
            ahead.issue(sp)
            for i in range(slots, units):
                sp.wait_ge(multiplied, i - slots + 1)
                for dst, src in plan.pairs(i):
                    sp.dma_start(dst, src).then_inc(landed[i % slots], 16)

        @block.tensor
        def _(pe):
            for i in range(units):
                _, yT, n = plan.branches[i % nb]
                gate, value = 2 * (i % 4), 2 * (i % 4) + 1
                wait(pe, weighed, i - 3)
                pe.wait_ge(landed[i % slots], 32 * (i // slots + 1))
                for c in range(n):
                    nc.tensor.matmul(k.ps[:, value, :], plan.slots[i % slots][1][:, c, :], yT[:, c, :],
                                     start=(c == 0), stop=(c == n - 1))
                pe.wait_ge(high_ready, i + 1)
                pe.wait_ge(low_ready, i + 1)
                for c in range(DC):
                    if i == 0:
                        pe.wait_ge(hT_high_ready, c + 1)
                        pe.wait_ge(hT_low_ready, c + 1)
                    cols = slice(c * P, (c + 1) * P)
                    last = split_product(nc, k.ps[:, gate, :], (high_w[:, i % 2, cols], low_w[:, i % 2, cols]),
                                         (hT_high[:, c, :], hT_low[:, c, :]), c == 0, c == DC - 1)
                last.then_inc(multiplied, 1)

        @block.scalar
        def _(act):
            def gate(i):
                act.wait_ge(multiplied, i + 1)
                wait(act, weighed, i - 1)
                nc.scalar.activation(sig[:, i % 2, :], k.ps[:, 2 * (i % 4), :], ACT.Sigmoid).then_inc(sig_done, 1)

            for i in range(units):
                act.wait_ge(masked, i + 1)
                nc.scalar.activation(high_w[:, i % 2, :], masked_w[:], ACT.Copy).then_inc(high_ready, 1)
                if i == 0:
                    for c in range(DC):
                        act.wait_ge(hT_mask_done, c + 1)
                        nc.scalar.activation(hT_high[:, c, :], hT_masked(c), ACT.Copy).then_inc(hT_high_ready, 1)
                else:
                    gate(i - 1)
            gate(units - 1)

        @block.vector
        def _(dve):
            def weigh(i):
                chunk, b = divmod(i, nb)
                out = mergedT[:, chunk, :]
                dve.wait_ge(sig_done, i + 1)
                nc.vector.tensor_tensor(part[:, i % 2, :] if b else out, sig[:, i % 2, :], k.ps[:, 2 * (i % 4) + 1, :],
                                        ALU.mult).then_inc(weighed, 1)
                if b:
                    dve.wait_ge(weighed, i + 1)
                    if b > 1:
                        dve.wait_ge(summed, chunk * (nb - 1) + b - 1)
                    nc.vector.tensor_tensor(out, out, part[:, i % 2, :], ALU.add).then_inc(summed, 1)

            for i in range(units):
                raw = plan.slots[i % slots][0].rearrange("p c n -> p (c n)")
                dve.wait_ge(landed[i % slots], 32 * (i // slots + 1))
                if i == 1:
                    dve.wait_ge(hT_high_ready, DC)
                    dve.wait_ge(hT_low_ready, DC)
                wait(dve, high_ready, i)
                wait(dve, low_ready, i)
                wait(dve, multiplied, i - 1)
                mask_low_bits(nc, masked_w[:], raw).then_inc(masked, 1)
                dve.wait_ge(masked, i + 1)
                nc.vector.tensor_tensor(low_w[:, i % 2, :], raw, masked_w[:], ALU.subtract).then_inc(low_ready, 1)
                if i == 0:
                    dve.wait_ge(high_ready, 1)
                    dve.wait_ge(low_ready, 1)
                    for c in range(DC):
                        wait(dve, hT_high_ready, c - 1)
                        wait(dve, hT_low_ready, c - 1)
                        mask_low_bits(nc, hT_masked(c), k.hT[:, c, :]).then_inc(hT_mask_done, 1)
                        dve.wait_ge(hT_mask_done, c + 1)
                        nc.vector.tensor_tensor(hT_low[:, c, :], k.hT[:, c, :], hT_masked(c),
                                                ALU.subtract).then_inc(hT_low_ready, 1)
                else:
                    weigh(i - 1)
            weigh(units - 1)


class RowBlocks:

    R = 4

    def __init__(self, k, ctx, tag, raw, w):
        self.raw, self.w = raw, w
        self.first = Loads(k, ctx, *((f"{tag}_landed{n}", [(raw[:, n, :], self.block(n))]) for n in range(self.R)))

    def block(self, n):
        return self.w[bass.ds(n * P, P), :]


def add_product(k, tag, srcT, count, rows, ahead=()):
    nc = k.nc
    R = rows.R
    with ExitStack() as ctx:
        def sb(name, shape, dt=F32):
            return ctx.enter_context(nc.sbuf_tensor(f"{tag}_{name}", shape, dt))

        masked_s, masked_w = sb("masked_s", [P, S]), sb("masked_w", [P, D])
        high_s, low_s = sb("high_s", [P, 2, S], F32R), sb("low_s", [P, 2, S], F32R)
        high_w, low_w = sb("high_w", [P, 2, D], F32R), sb("low_w", [P, 2, D], F32R)
        masked, high_ready, low_ready, used, tile_done, added = sems(
            k, ctx, " ".join(tag + n for n in "_masked _high_ready _low_ready _used _tile_done _added".split()))
        landed = rows.first.landed
        block = ctx.enter_context(nc.Block())

        @block.sync
        def _(sp):
            def step(it, u):
                if isinstance(it, int) and it == 0:
                    return
                wait(sp, low_ready, it * 2 * R + (2 * u + 2 - 2 * R))
                sp.dma_start(rows.raw[:, u, :], rows.block(it * R + u)).then_inc(landed[u], 16)

            every(sp, count, R, step)
            for loads in ahead:
                loads.issue(sp)

        @block.tensor
        def _(pe):
            def step(it, u):
                first = isinstance(it, int) and it == 0 and u == 0
                final = isinstance(it, int) and it * R + u == count - 1
                pe.wait_ge(high_ready, it * 2 * R + (2 * u + 2))
                pe.wait_ge(low_ready, it * 2 * R + (2 * u + 2))
                for t in range(NT):
                    tokens = slice(t * P, (t + 1) * P)
                    for n in (0, 1):
                        cols = slice(n * 512, (n + 1) * 512)
                        last = split_product(nc, k.ps[:, 2 * t + n, :], (high_s[:, u % 2, tokens], low_s[:, u % 2, tokens]),
                                             (high_w[:, u % 2, cols], low_w[:, u % 2, cols]), first, final)
                    if final:
                        last.then_inc(tile_done, 1)
                if not final:
                    last.then_inc(used, 1)

            every(pe, count, R, step)

        @block.scalar
        def _(act):
            def step(it, u):
                for n, (high, source) in enumerate(((high_s, masked_s), (high_w, masked_w))):
                    act.wait_ge(masked, it * 2 * R + (2 * u + n + 1))
                    nc.scalar.activation(high[:, u % 2, :], source[:], ACT.Copy).then_inc(high_ready, 1)

            every(act, count, R, step)

        @block.vector
        def _(dve):
            def step(it, u):
                wait(dve, used, it * R + (u - 1))
                chunk = srcT[:, bass.ds(it * R + u, 1), :].rearrange("p a n -> p (a n)")
                operands = ((chunk, masked_s, low_s), (rows.raw[:, u, :], masked_w, low_w))
                for n, (source, masked_part, _) in enumerate(operands):
                    if n:
                        dve.wait_ge(landed[u], it * 16 + 16)
                    wait(dve, high_ready, it * 2 * R + (2 * u + n - 1))
                    wait(dve, low_ready, it * 2 * R + (2 * u + n - 1))
                    mask_low_bits(nc, masked_part[:], source).then_inc(masked, 1)
                for n, (source, masked_part, low) in enumerate(operands):
                    dve.wait_ge(masked, it * 2 * R + (2 * u + n + 1))
                    nc.vector.tensor_tensor(low[:, u % 2, :], source, masked_part[:], ALU.subtract).then_inc(low_ready, 1)

            every(dve, count, R, step)
            for t in range(NT):
                dve.wait_ge(tile_done, t + 1)
                nc.vector.tensor_tensor(k.x[:, t, :], k.x[:, t, :], k.ps[:, 2 * t:2 * t + 2, :].rearrange("p a n -> p (a n)"),
                                        ALU.add).then_inc(added, 1)



GROUPS, PER_GROUP = 4, 8
EXPERTS = GROUPS * PER_GROUP
HID = 256
SPILL = 2 * S // P
BLOCKS = EXPERTS + SPILL
SKIP = 65536.0


class Routing:

    def __init__(self, nc, ctx):
        def sb(name, shape, dt=F32):
            return ctx.enter_context(nc.sbuf_tensor("route_" + name, shape, dt))

        self.gate = sb("gate", [P, 2, NT])
        self.token = sb("token", [P, BLOCKS], I32)
        self.row = sb("row", [P, BLOCKS], I32)
        self.spill_expert = sb("spill_expert", [1, SPILL + 1], I32)
        self.gain = sb("gain", [P, DC])
        self.w = sb("w", [P, DC, GROUPS + EXPERTS])
        self.bias = sb("bias", [P, GROUPS + EXPERTS])
        self.iota = sb("iota", [P, P])
        self.before = sb("before", [P, P])
        self.values = sb("values", [P, 8, 2])

    def loads(self, k, ctx, w_group, b_group, w_expert, b_expert, gain):
        return Loads(k, ctx, ("rt_landed", [
            (self.w[:, :, 0:GROUPS], rows_pc(w_group)), (self.w[:, :, GROUPS:], rows_pc(w_expert)),
            (self.bias[:, 0:GROUPS], b_group.partition_broadcast(P)),
            (self.bias[:, GROUPS:], b_expert.partition_broadcast(P)),
            (self.gain[:], gain.rearrange("(p c) -> p c", c=DC)), (self.iota[:], k.t["c_iota"].partition_broadcast(P)),
            (self.before[:], k.t["c_before"]), (self.values[:], k.t["c_slot_values"])]))


def route(k, tag, r, first):
    nc = k.nc
    NE, NL = EXPERTS, GROUPS + EXPERTS
    magic = 12582912.0
    with ExitStack() as ctx:
        def sb(name, shape, dt=F32):
            return ctx.enter_context(nc.sbuf_tensor(tag + "_" + name, shape, dt))

        w, bias, iota, before, values = r.w, r.bias, r.iota, r.before, r.values
        block_base = sb("block_base", [P, NE])
        lg = sb("lg", [P, NT, NL])
        gpad = sb("gpad", [P, NT, 8])
        gtop, gidx = sb("gtop", [P, NT, 8]), sb("gidx", [P, NT, 8], U32)
        gsel, gneg, gsum = sb("gsel", [P, NT]), sb("gneg", [P, NT]), sb("gsum", [P, NT])
        gexp = sb("gexp", [P, NT, GROUPS])
        chosen = sb("chosen", [P, NT, GROUPS])
        em = sb("em", [P, NT, NE])
        pen = sb("pen", [P, NT, GROUPS])
        etop, eidx = sb("etop", [P, NT, 8]), sb("eidx", [P, NT, 8], U32)
        esel = sb("esel", [P, 2, NT])
        gap, den = sb("gap", [P, NT]), sb("den", [P, NT])
        onehot = sb("onehot", [P, 2, NT, NE])
        member = sb("member", [P, NT, NE])
        counts, spills, ends, delta = sb("counts", [P, NE]), sb("spills", [P, NE]), sb("ends", [P, NE]), sb("delta", [P, NE])
        ones_row = sb("ones_row", [P, NE])
        over = sb("over", [P, NT, NE])
        slotv = sb("slotv", [P, NT, NE])
        junk = sb("junk", [P, 8, NE])
        dest, blk, lane = sb("dest", [P, 8]), sb("blk", [P, 8]), sb("lane", [P, 8])
        lane_hot = sb("lane_hot", [P, 8, P])
        block_hot = sb("block_hot", [P, 8, 2, BLOCKS])
        table = sb("table", [P, 2, BLOCKS])
        spill_f = sb("spill_f", [P, SPILL + 1])
        ones = sb("ones", [P, P])
        (landed,) = first.landed
        link_sem, logits_done, gneg_ready, gexp_done, gap_ready, ratio_done, member_ready, ranked, hot_ready, tabled = sems(
            k, ctx, " ".join(f"{tag}_{n}" for n in (
                "link logits_done gneg_ready gexp_done gap_ready ratio_done member_ready ranked hot_ready tabled").split()))
        block = ctx.enter_context(nc.Block())

        @block.tensor
        def _(pe):
            pe.wait_ge(landed, 16 * 8)
            for t in range(NT):
                for c in range(DC):
                    last = nc.tensor.matmul(k.ps[:, 0, t * NL:(t + 1) * NL], k.hT[:, c, t * P:(t + 1) * P], w[:, c, :],
                                            start=(c == 0), stop=(c == DC - 1))
            last.then_inc(logits_done, 1)
            pe.wait_ge(member_ready, 1)
            for t in range(NT):
                for b in range(t + 1):
                    nc.tensor.matmul(k.ps[:, 1, t * NE:(t + 1) * NE], (before if b == t else ones)[:], member[:, b, :],
                                     start=(b == 0), stop=(b == t))
            for b in range(NT):
                last = nc.tensor.matmul(k.ps[:, 2, 0:NE], ones[:], member[:, b, :], start=(b == 0), stop=(b == NT - 1))
            last.then_inc(ranked, 1)
            pe.wait_ge(hot_ready, 8)
            for i in range(8):
                last = nc.tensor.matmul(k.ps[:, 3, 0:2 * BLOCKS], lane_hot[:, i, :],
                                        block_hot[:, i, :, :].rearrange("p a b -> p (a b)"), start=(i == 0), stop=(i == 7))
            last.then_inc(tabled, 1)

        @block.scalar
        def _(act):
            act.wait_ge(gneg_ready, 1)
            for t in range(NT):
                nc.scalar.activation(gexp[:, t, :], lg[:, t, 0:GROUPS], ACT.Exp, bias=gneg[:, t:t + 1],
                                     accum_out=gsum[:, t:t + 1]).then_inc(gexp_done, 1)
            act.wait_ge(gap_ready, 1)
            nc.scalar.activation(gap[:], gap[:], ACT.Exp).then_inc(ratio_done, 1)

        @block.vector
        def _(dve):
            V = nc.vector
            done = [0]

            def link(*instructions):
                for ins in instructions:
                    ins.then_inc(link_sem, 1)
                    done[0] += 1
                dve.wait_ge(link_sem, done[0])

            link(V.memset(gpad[:], NEG), V.memset(ones[:], 1.0), V.memset(ones_row[:], 1.0))
            dve.wait_ge(landed, 16 * 8)
            dve.wait_ge(logits_done, 1)
            link(*[V.tensor_tensor(lg[:, t, :], k.ps[:, 0, t * NL:(t + 1) * NL], bias[:], ALU.add) for t in range(NT)])
            link(V.tensor_copy(gpad[:, :, 0:GROUPS], lg[:, :, 0:GROUPS]),
                 V.tensor_scalar(block_base[:], iota[:, 0:NE], float(P), None, ALU.mult))
            link(*[V.max(gtop[:, t, :], gpad[:, t, :]) for t in range(NT)])
            link(V.tensor_scalar(gneg[:], gtop[:, :, 0], -1.0, None, ALU.mult))
            dve.sem_inc(gneg_ready, 1)
            link(*[V.max_index(gidx[:, t, :], gtop[:, t, :], gpad[:, t, :]) for t in range(NT)])
            link(V.tensor_copy(gsel[:], gidx[:, :, 0]))
            link(*[V.tensor_scalar(chosen[:, t, :], iota[:, 0:GROUPS], gsel[:, t:t + 1], None, ALU.is_equal)
                   for t in range(NT)])
            link(V.tensor_scalar(pen[:], chosen[:], -NEG, NEG, ALU.mult, ALU.add))

            def per_group(a):
                return a.rearrange("p (g e) -> p g e", g=GROUPS)

            def spread(a):
                return a.unsqueeze(2).to_broadcast([P, GROUPS, PER_GROUP])

            link(*[V.tensor_tensor(per_group(em[:, t, :]), per_group(lg[:, t, GROUPS:NL]), spread(chosen[:, t, :]), ALU.mult)
                   for t in range(NT)])
            link(*[V.tensor_tensor(per_group(em[:, t, :]), per_group(em[:, t, :]), spread(pen[:, t, :]), ALU.add)
                   for t in range(NT)])
            link(*[V.max(etop[:, t, :], em[:, t, :]) for t in range(NT)])
            link(*[V.max_index(eidx[:, t, :], etop[:, t, :], em[:, t, :]) for t in range(NT)])
            link(V.tensor_copy(esel[:, 0, :], eidx[:, :, 0]), V.tensor_copy(esel[:, 1, :], eidx[:, :, 1]),
                 V.tensor_tensor(gap[:], etop[:, :, 1], etop[:, :, 0], ALU.subtract))
            dve.sem_inc(gap_ready, 1)
            link(*[V.tensor_scalar(onehot[:, c, t, :], iota[:, 0:NE], esel[:, c, t:t + 1], None, ALU.is_equal)
                   for t in range(NT) for c in (0, 1)])
            link(V.tensor_tensor(member[:], onehot[:, 0, :, :], onehot[:, 1, :, :], ALU.add))
            dve.sem_inc(member_ready, 1)
            dve.wait_ge(gexp_done, NT)
            dve.wait_ge(ratio_done, 1)
            link(V.tensor_scalar(den[:], gap[:], 1.0, None, ALU.add))
            link(V.tensor_tensor(den[:], den[:], gsum[:], ALU.mult))
            link(V.reciprocal(r.gate[:, 0, :], den[:]))
            link(V.tensor_tensor(r.gate[:, 1, :], r.gate[:, 0, :], gap[:], ALU.mult))
            dve.wait_ge(ranked, 1)
            link(V.tensor_copy(counts[:], k.ps[:, 2, 0:NE]))
            link(V.tensor_scalar(spills[:], counts[:], 1.0 * P, None, ALU.is_gt))
            for full in (2, 3):
                link(V.scalar_tensor_tensor(out=spills[:], in0=counts[:], scalar=full * P + 0.0, in1=spills[:],
                                            op0=ALU.is_gt, op1=ALU.add))
            link(V.tensor_tensor_scan(ends[:], ones_row[:], spills[:], 0.0, ALU.mult, ALU.add))
            link(V.tensor_tensor(delta[:], ends[:], spills[:], ALU.subtract))
            link(V.tensor_scalar(delta[:], delta[:], float(P), float((NE - 1) * P), ALU.mult, ALU.add))
            link(V.tensor_tensor(delta[:], delta[:], block_base[:], ALU.subtract))
            tiles = range(NT)
            rank = [k.ps[:, 1, t * NE:(t + 1) * NE] for t in tiles]
            link(*[V.tensor_scalar(over[:, t, :], rank[t], P - 0.5, None, ALU.is_gt) for t in tiles],
                 *[V.tensor_tensor(slotv[:, t, :], rank[t], block_base[:], ALU.add) for t in tiles])
            link(*[V.tensor_tensor(over[:, t, :], over[:, t, :], delta[:], ALU.mult) for t in tiles])
            link(*[V.tensor_tensor(slotv[:, t, :], slotv[:, t, :], over[:, t, :], ALU.add) for t in tiles])
            link(*[V.tensor_tensor_reduce(out=junk[:, 2 * t + c, :], in0=onehot[:, c, t, :], in1=slotv[:, t, :], scale=1.0,
                                          scalar=0.0, op0=ALU.mult, op1=ALU.add,
                                          accum_out=dest[:, 2 * t + c:2 * t + c + 1]) for t in tiles for c in (0, 1)])
            link(V.tensor_scalar(blk[:], dest[:], -(P / 2 - 0.5), 1.0 / P, ALU.add, ALU.mult))
            link(V.tensor_scalar(blk[:], blk[:], magic, None, ALU.add))
            link(V.tensor_scalar(blk[:], blk[:], -magic, None, ALU.add))
            link(V.scalar_tensor_tensor(out=lane[:], in0=blk[:], scalar=-float(P), in1=dest[:], op0=ALU.mult, op1=ALU.add))
            for i in range(8):
                V.tensor_scalar(lane_hot[:, i, :], iota[:], lane[:, i:i + 1], None, ALU.is_equal)
                for a in (0, 1):
                    last = V.tensor_scalar(block_hot[:, i, a, :], iota[:, 0:BLOCKS], blk[:, i:i + 1], values[:, i, a:a + 1],
                                           ALU.is_equal, ALU.mult)
                last.then_inc(hot_ready, 1)
            link(*[V.tensor_scalar(junk[:, b, :], ends[:], b + 0.5, None, ALU.is_lt, ALU.add, accum_out=spill_f[:, b:b + 1])
                   for b in range(SPILL)])
            link(V.tensor_scalar(spill_f[:, 0:SPILL], spill_f[:, 0:SPILL], float(NE - 1), None, ALU.min),
                 V.tensor_copy(spill_f[:, SPILL:SPILL + 1], ends[:, NE - 1:NE]))
            link(V.tensor_copy(r.spill_expert[:], spill_f[0:1, :]))
            dve.wait_ge(tabled, 1)
            link(V.tensor_scalar(table[:].rearrange("p a b -> p (a b)"), k.ps[:, 3, 0:2 * BLOCKS], 0.0, SKIP,
                                 ALU.is_equal, ALU.mult))
            link(V.tensor_tensor(table[:].rearrange("p a b -> p (a b)"), table[:].rearrange("p a b -> p (a b)"),
                                 k.ps[:, 3, 0:2 * BLOCKS], ALU.add))
            link(V.tensor_scalar(r.token[:], table[:, 0, :], -1.0, None, ALU.add),
                 V.tensor_scalar(r.row[:], table[:, 1, :], -1.0, None, ALU.add))


EXPERT_WORDS = DC * 2 * HID + 2 * D


def expert_slots(k, u):
    at = u * EXPERT_WORDS if u < 2 else RING
    return k.slot(at, DC, 2 * HID), k.slot(at + DC * 2 * HID, 2, D)


def expert_pairs(k, u, w_gate, w_up, w_down):
    gu, down = expert_slots(k, u)
    return [(gu[:, :, 0:HID], rows_pc(w_gate)), (gu[:, :, HID:2 * HID], rows_pc(w_up)),
            (down, w_down.rearrange("(f p) n -> p f n", p=P))]


def experts(k, tag, r, layer, blocks, spill, xn_rows, y_rows, w_gate, w_up, w_down, first_loads=None):
    nc = k.nc
    first = EXPERTS if spill else 0
    U = 3
    assert 2 * EXPERT_WORDS <= RING and EXPERT_WORDS <= EXTRA
    slots = [expert_slots(k, u) for u in range(U)]
    with ExitStack() as ctx:
        def sb(name, shape, dt=F32):
            return ctx.enter_context(nc.sbuf_tensor(tag + "_" + name, shape, dt))

        idx = sb("idx", [P, U, 2], I32)
        xs = sb("xs", [P, U, D])
        xsT = sb("xsT", [P, U, DC, P])
        silu = sb("silu", [P, HID])
        hid = sb("hid", [P, U, HID])
        hidT = sb("hidT", [P, U, 2, P])
        y = sb("y", [P, U, D])
        names = ("cleared wait_kept token_ready row_ready gathered0 gathered1 gathered2 turned xsT_ready gu_done silu_done hid_ready "
                 "hid_turned hidT_ready down_done y_act y_dve scattered0 scattered1 scattered2")
        sem = dict(zip(names.split(), sems(k, ctx, " ".join(tag + "_" + n for n in names.split()))))
        gathered, scattered = [[sem[f"{n}{u}"] for u in range(U)] for n in ("gathered", "scattered")]
        found = first_loads.landed if first_loads else sems(k, ctx, " ".join(
            f"{tag}_{n}_landed{u}" for u in range(U) for n in ("gu", "down")))
        w_landed, down_landed = found[0::2], found[1::2]
        block = ctx.enter_context(nc.Block())

        def before(it, u):
            return (it, u - 1) if u else (it - 1, U - 1)

        def after(it, u):
            return (it, u + 1) if u + 1 < U else (it + 1, 0)

        def first_block(it, u):
            return isinstance(it, int) and it == 0 and u == 0

        def last_block(it, u):
            return isinstance(it, int) and it * U + u == blocks - 1

        @block.sync
        def _(sp):
            def step(it, u):
                if first_loads and isinstance(it, int) and it == 0:
                    return
                n = it * U + u
                e = sp.value_load(r.spill_expert[0:1, bass.ds(n, 1)], min_val=0, max_val=EXPERTS - 1) if spill else n
                gate, up, down = expert_pairs(k, u, w_gate[layer, e], w_up[layer, e], w_down[layer, e])
                wait(sp, sem["gu_done"], it * U + (u - U + 1))
                for dst, src in (gate, up):
                    sp.dma_start(dst, src).then_inc(w_landed[u], 16)
                wait(sp, sem["down_done"], it * U + (u - U + 1))
                sp.dma_start(*down).then_inc(down_landed[u], 16)

            every(sp, blocks, U, step)

        @block.gpsimd
        def _(pool):
            def gather(it, u):
                n = it * U + u
                wait(pool, sem["turned"], it * U + (u - U + 1))
                nc.gpsimd.tensor_copy(idx[:, u, 0:1], r.token[:, bass.ds(n + first, 1)]).then_inc(sem["token_ready"], 1)
                pool.wait_ge(sem["token_ready"], it * U + (u + 1))
                pool.sem_inc(sem["wait_kept"], 1)
                nc.gpsimd.indirect_dma_start(out=xs[:, u, :], out_offset=None, in_=xn_rows[:, :],
                                             in_offset=bass.IndirectOffsetOnAxis(ap=idx[:, u, 0:1], axis=0),
                                             bounds_check=last_token, oob_is_err=False).then_inc(gathered[u], 16)

            def scatter(it, u):
                n = it * U + u
                wait(pool, scattered[u], it * 16)
                nc.gpsimd.tensor_copy(idx[:, u, 1:2], r.row[:, bass.ds(n + first, 1)]).then_inc(sem["row_ready"], 1)
                pool.wait_ge(sem["row_ready"], it * U + (u + 1))
                pool.wait_ge(sem["y_act"], it * U + (u + 1))
                pool.wait_ge(sem["y_dve"], it * U + (u + 1))
                pool.sem_inc(sem["wait_kept"], 1)
                nc.gpsimd.indirect_dma_start(out=y_rows[:, :], in_=y[:, u, :], in_offset=None,
                                             out_offset=bass.IndirectOffsetOnAxis(ap=idx[:, u, 1:2], axis=0),
                                             bounds_check=last_row, oob_is_err=False).then_inc(scattered[u], 16)

            last_token, last_row = pool.to_reg(S - 1), pool.to_reg(2 * S - 1)
            for u in range(U):
                nc.gpsimd.memset(xs[:, u, :], 0.0).then_inc(sem["cleared"], 1)
                pool.wait_ge(sem["cleared"], u + 1)
                gather(0, u)

            def step(it, u):
                if not isinstance(it, int) or (it + 1) * U + u < blocks:
                    gather(it + 1, u)
                scatter(it, u)

            every(pool, blocks, U, step)
            for u in range(U):
                pool.wait_ge(scattered[u], 16 * len(range(u, blocks, U)))

        @block.tensor
        def _(pe):
            def turn(it, u):
                pe.wait_ge(gathered[u], it * 16 + 16)
                wait(pe, sem["xsT_ready"], it * U + u)
                for c in range(DC):
                    last = nc.tensor.transpose(k.ps[:, c // 4, (c % 4) * P:(c % 4 + 1) * P], xs[:, u, c::DC], k.ident[:])
                last.then_inc(sem["turned"], 1)

            def down(it, u):
                pe.wait_ge(down_landed[u], it * 16 + 16)
                pe.wait_ge(sem["hidT_ready"], it * U + (u + 1))
                wait(pe, sem["y_act"], it * U + u)
                wait(pe, sem["y_dve"], it * U + u)
                for half in (0, 1):
                    for f in (0, 1):
                        last = nc.tensor.matmul(k.ps[:, 4 + half, :], hidT[:, u, f, :],
                                                slots[u][1][:, f, half * 512:(half + 1) * 512], start=(f == 0), stop=(f == 1))
                last.then_inc(sem["down_done"], 1)

            def step(it, u):
                pe.wait_ge(w_landed[u], it * 32 + 32)
                pe.wait_ge(sem["xsT_ready"], it * U + (u + 1))
                wait(pe, sem["hid_ready"], it * U + u)
                for c in range(DC):
                    last = nc.tensor.matmul(k.ps[:, 2, :], xsT[:, u, c, :], slots[u][0][:, c, :],
                                            start=(c == 0), stop=(c == DC - 1))
                last.then_inc(sem["gu_done"], 1)
                if not last_block(it, u):
                    turn(*after(it, u))
                if not first_block(it, u):
                    down(*before(it, u))
                pe.wait_ge(sem["hid_ready"], it * U + (u + 1))
                for f in (0, 1):
                    last = nc.tensor.transpose(k.ps[:, 3, f * P:(f + 1) * P], hid[:, u, f * P:(f + 1) * P], k.ident[:])
                last.then_inc(sem["hid_turned"], 1)

            turn(0, 0)
            every(pe, blocks, U, step)
            down(*divmod(blocks - 1, U))

        @block.scalar
        def _(act):
            def y_half(it, u):
                act.wait_ge(sem["down_done"], it * U + (u + 1))
                wait(act, scattered[u], it * 16)
                nc.scalar.activation(y[:, u, 0:512], k.ps[:, 4, :], ACT.Copy).then_inc(sem["y_act"], 1)

            def step(it, u):
                act.wait_ge(sem["gu_done"], it * U + (u + 1))
                nc.scalar.activation(silu[:], k.ps[:, 2, 0:HID], ACT.Silu).then_inc(sem["silu_done"], 1)
                if not first_block(it, u):
                    y_half(*before(it, u))
                act.wait_ge(sem["hid_turned"], it * U + (u + 1))
                nc.scalar.activation(hidT[:, u, :, :].rearrange("p f n -> p (f n)"), k.ps[:, 3, 0:HID],
                                     ACT.Copy).then_inc(sem["hidT_ready"], 1)

            every(act, blocks, U, step)
            y_half(*divmod(blocks - 1, U))

        @block.vector
        def _(dve):
            def gained(it, u):
                dve.wait_ge(sem["turned"], it * U + (u + 1))
                for b in (0, 1):
                    last = nc.vector.tensor_tensor(xsT[:, u, 4 * b:4 * b + 4, :],
                                                   k.ps[:, b, :].rearrange("p (c n) -> p c n", c=4),
                                                   r.gain[:, 4 * b:4 * b + 4].unsqueeze(2).to_broadcast([P, 4, P]), ALU.mult)
                last.then_inc(sem["xsT_ready"], 1)

            def y_half(it, u):
                dve.wait_ge(sem["down_done"], it * U + (u + 1))
                wait(dve, scattered[u], it * 16)
                nc.vector.tensor_copy(y[:, u, 512:D], k.ps[:, 5, :]).then_inc(sem["y_dve"], 1)

            def step(it, u):
                dve.wait_ge(sem["silu_done"], it * U + (u + 1))
                nc.vector.tensor_tensor(hid[:, u, :], silu[:], k.ps[:, 2, HID:2 * HID], ALU.mult).then_inc(sem["hid_ready"], 1)
                if not last_block(it, u):
                    gained(*after(it, u))
                if not first_block(it, u):
                    y_half(*before(it, u))

            gained(0, 0)
            every(dve, blocks, U, step)
            y_half(*divmod(blocks - 1, U))


class Embedding:

    PC = 2

    def __init__(self, k, ctx, tag, p_rows, w_ple, w_gate):
        def sb(name, shape):
            return ctx.enter_context(k.nc.sbuf_tensor(f"{tag}_{name}", shape, F32))

        self.rows, self.w = sb("rows", [P, NT, self.PC * P]), sb("w", [P, self.PC, D])
        self.gate = [k.slot(RING, DC, 512), k.slot(NT * 2 * D, DC, 512)]
        self.loads = Loads(k, ctx, (tag + "_p_landed", [(self.rows[:], p_rows.rearrange("(t p) d -> p t d", p=P))]),
                           (tag + "_w_landed", [(self.w[:], w_ple.rearrange("(c p) n -> p c n", p=P))]))
        self.gate_loads = Loads(k, ctx, *((f"{tag}_gate_landed{n}", [
            (self.gate[n], rows_pc(w_gate)[:, :, n * 512:(n + 1) * 512])]) for n in (0, 1)))


def combine_experts(k, tag, r, y_rows, pe_layer, embedded, ahead):
    nc = k.nc
    PC = pe_layer.PC
    rows = y_rows.rearrange("(t p c) d -> p t (c d)", p=P, c=2)
    y = k.ring[:, 0:NT * 2 * D].rearrange("p (t c d) -> p t c d", t=NT, c=2)
    with ExitStack() as ctx:
        pT = ctx.enter_context(nc.sbuf_tensor(tag + "_pT", [P, PC, S], F32))
        (*landed, added, turned, pT_ready, multiplied, embedded_ready) = sems(
            k, ctx, " ".join(f"{tag}_landed{t}" for t in range(NT))
            + "".join(f" {tag}_{n}" for n in "added turned pT_ready multiplied embedded_ready".split()))
        block = ctx.enter_context(nc.Block())

        @block.sync
        def _(sp):
            for t in range(NT):
                sp.dma_start(y[:, t, :, :].rearrange("p c d -> p (c d)"), rows[:, t, :]).then_inc(landed[t], 16)
            ahead.issue(sp)

        @block.tensor
        def _(pe):
            p_landed, w_landed = pe_layer.loads.landed
            pe.wait_ge(p_landed, 16)
            for c in range(PC):
                for t in range(NT):
                    last = nc.tensor.transpose(k.ps[:, 6 + c, t * P:(t + 1) * P], pe_layer.rows[:, t, c * P:(c + 1) * P],
                                               k.ident[:])
            last.then_inc(turned, 1)
            pe.wait_ge(pT_ready, 1)
            pe.wait_ge(w_landed, 16)
            for i in range(2 * NT):
                t, n = divmod(i, 2)
                wait(pe, embedded_ready, i - 3)
                for c in range(PC):
                    last = nc.tensor.matmul(k.ps[:, i % 4, :], pT[:, c, t * P:(t + 1) * P],
                                            pe_layer.w[:, c, n * 512:(n + 1) * 512], start=(c == 0), stop=(c == PC - 1))
                last.then_inc(multiplied, 1)

        @block.scalar
        def _(act):
            act.wait_ge(turned, 1)
            nc.scalar.activation(pT[:], k.ps[:, 6:8, :], ACT.Copy).then_inc(pT_ready, 1)
            for i in range(2 * NT):
                t, n = divmod(i, 2)
                act.wait_ge(multiplied, i + 1)
                nc.scalar.activation(embedded[:, t, n * 512:(n + 1) * 512], k.ps[:, i % 4, :],
                                     ACT.Copy).then_inc(embedded_ready, 1)

        @block.vector
        def _(dve):
            for t in range(NT):
                dve.wait_ge(landed[t], 16)
                for c in (0, 1):
                    nc.vector.scalar_tensor_tensor(out=k.x[:, t, :], in0=y[:, t, c, :], scalar=r.gate[:, c, t:t + 1],
                                                   in1=k.x[:, t, :], op0=ALU.mult, op1=ALU.add).then_inc(added, 1)
                    dve.wait_ge(added, 2 * t + c + 1)


def embed_per_layer(k, tag, pe_layer, embedded):
    nc = k.nc
    with ExitStack() as ctx:
        def sb(name, shape):
            return ctx.enter_context(nc.sbuf_tensor(tag + "_" + name, shape, F32))

        sig = sb("sig", [P, 4, 512])
        multiplied, sig_done, part_done = sems(k, ctx, " ".join(tag + n for n in "_multiplied _sig_done _part_done".split()))
        block = ctx.enter_context(nc.Block())

        @block.tensor
        def _(pe):
            for n, landed in enumerate(pe_layer.gate_loads.landed):
                pe.wait_ge(landed, 16)
                for t in range(NT):
                    for c in range(DC):
                        last = nc.tensor.matmul(k.ps[:, n * NT + t, :], k.hT[:, c, t * P:(t + 1) * P],
                                                pe_layer.gate[n][:, c, :], start=(c == 0), stop=(c == DC - 1))
                    last.then_inc(multiplied, 1)

        @block.scalar
        def _(act):
            for i in range(2 * NT):
                act.wait_ge(multiplied, i + 1)
                wait(act, part_done, i - 3)
                nc.scalar.activation(sig[:, i % 4, :], k.ps[:, i, :], ACT.Sigmoid).then_inc(sig_done, 1)

        @block.vector
        def _(dve):
            for n in (0, 1):
                for t in range(NT):
                    i = n * NT + t
                    half = slice(n * 512, (n + 1) * 512)
                    dve.wait_ge(sig_done, i + 1)
                    nc.vector.tensor_tensor(embedded[:, t, half], sig[:, i % 4, :], embedded[:, t, half],
                                            ALU.mult).then_inc(part_done, 1)
                    dve.wait_ge(part_done, i + 1)
                    nc.vector.tensor_tensor(k.x[:, t, half], k.x[:, t, half], embedded[:, t, half], ALU.add)



WINDOW_HEADS, WINDOW_GROUPS = 4, ((128, 1), (512, 4), (2048, 16))
BLOCK_HEADS = 8
BIAS_HEADS = WINDOW_HEADS * len(WINDOW_GROUPS) + BLOCK_HEADS
BUCKETS = 32
LINE = S + P


def bias_lines(k, rel_bias, lines, line, stored):
    nc = k.nc
    with ExitStack() as ctx:
        def sb(name, shape):
            return ctx.enter_context(nc.sbuf_tensor("bl_" + name, shape, F32))

        table, hot, hidden = sb("table", [BUCKETS, BIAS_HEADS]), sb("hot", [BUCKETS, LINE]), sb("hidden", [BIAS_HEADS, LINE])
        landed, multiplied, line_ready = sems(k, ctx, "bl_landed bl_multiplied bl_line_ready")
        block = ctx.enter_context(nc.Block())
        half = LINE // 2

        @block.sync
        def _(sp):
            sp.dma_start(table[:], rel_bias).then_inc(landed, 16)
            sp.dma_start(hot[:], k.t["c_bucket_hot"]).then_inc(landed, 16)
            sp.dma_start(hidden[:], k.t["c_hidden"]).then_inc(landed, 16)
            sp.wait_ge(line_ready, 2)
            sp.dma_start(lines, line[:].unsqueeze(1).to_broadcast([BIAS_HEADS, P, LINE])).then_inc(stored, 16)

        @block.tensor
        def _(pe):
            pe.wait_ge(landed, 48)
            for n in (0, 1):
                nc.tensor.matmul(k.ps[0:BIAS_HEADS, n, 0:half], table[:], hot[:, n * half:(n + 1) * half], start=True,
                                 stop=True).then_inc(multiplied, 1)

        @block.vector
        def _(dve):
            for n in (0, 1):
                dve.wait_ge(multiplied, n + 1)
                part = slice(n * half, (n + 1) * half)
                nc.vector.tensor_tensor(line[:, part], k.ps[0:BIAS_HEADS, n, 0:half], hidden[:, part],
                                        ALU.add).then_inc(line_ready, 1)


def bias_rows(lines):
    return bass.AP(lines.tensor, P - 1, [[P * LINE, BIAS_HEADS], [LINE - 1, P], [1, S]])



def bias_loads(k, ctx, tag, bias, heads, lines):
    rows = bias_rows(lines)
    return Loads(k, ctx, *((f"{tag}_first_bias{h}", [(bias[:, h, g, :], rows[head + h]) for g, head in enumerate(heads)])
                           for h in (0, 1)))


def biased_attention(k, tag, w_in, groups, banded, pairs, lines, bias, yT, first, first_bias, ahead, opened=None):
    nc = k.nc
    ng = len(groups)
    units = 3 * ng
    steps = 8 * pairs
    w = rows_pc(w_in)
    kinds = [(g, kind) for g in range(ng) for kind in (0, 1)] + [(g, 2) for g in range(ng)]
    slots = [first.slots[3 * g + kind] for g, kind in kinds]
    landed = [first.landed[3 * g + kind] for g, kind in kinds]
    rows = bias_rows(lines)

    if ng > 1:
        before = [[(n, c) for c in range(4)] for n in range(7)] + [[(7, c) for c in range(8)]]
        after = [[(n, c) for c in range(4, 8)] for n in range(7)] + [[(8, c) for c in range(8)]]
        opening_bank = (5, 4, 3, 2, 1, 0, 7, 6, 5)
        bank_of = (7,) * units
        s_base, t_base = (0, 0), (3, 3)
    else:
        before, after = spread_eighths()
        opening_bank = bank_of = (2, 5, 7)
        s_base, t_base = (0, 1), (3, 4)
    finished = [[m for m, c in before[n] + after[n] if c == 7] for n in range(8)]

    def span(g, t):
        return max(0, t - 1) if banded and g == 0 else 0

    def width(s):
        return sum((s % 4 + 1 - span(g, s % 4)) * P for g in range(ng))

    widest = width(3)
    with ExitStack() as ctx:
        def sb(name, shape):
            return ctx.enter_context(nc.sbuf_tensor(tag + "_" + name, shape, F32))

        qT, kT, v = sb("qT", [P, 2, ng, S]), sb("kT", [P, 2, ng, S]), sb("v", [P, 2, ng, NT, P])
        probs, probsT = sb("probs", [P, 3, widest]), sb("probsT", [P, 2, widest])
        maxima, neg_max, sums = sb("maxima", [P, 8, ng]), sb("neg_max", [P, 8]), sb("sums", [P, 8])
        names = ("bias_landed0 bias_landed1 qk_ready v_ready s_done biased max_ready exp_done inverted "
                 "normed turned probsT_ready pv_done y_out")
        sem = dict(zip(names.split(), sems(k, ctx, " ".join(tag + "_" + n for n in names.split()))))
        sem["projected"] = opened if opened is not None else sems(k, ctx, tag + "_projected")[0]
        block = ctx.enter_context(nc.Block())

        def wait_ready(eng, pair, m):
            if m < 2 * ng:
                eng.wait_ge(sem["qk_ready"], pair * 2 * ng + m + 1)
            else:
                eng.wait_ge(sem["v_ready"], pair * ng + m - 2 * ng + 1)

        @block.sync
        def _(sp):
            for pair in range(1, pairs):
                if pair == 2 or pairs == 2:
                    ahead.issue(sp)
                for m, (g, kind) in enumerate(kinds):
                    sp.wait_ge(sem["projected"], (pair - 1) * units + m + 1)
                    sp.dma_start(slots[m], w[:, :, groups[g][kind] + pair * P:][:, :, 0:P]).then_inc(landed[m], 16)

        @block.gpsimd
        def _(pool):
            for pair in range(1, pairs):
                for h in (0, 1):
                    pool.wait_ge(sem["biased"], ((pair - 1) * 8 + 4 * h + 4) * ng)
                    for g in range(ng):
                        nc.gpsimd.dma_start(bias[:, h, g, :], rows[groups[g][3] + 2 * pair + h])\
                            .then_inc(sem[f"bias_landed{h}"], 16)

        @block.tensor
        def _(pe):
            def project(pair, part, bank):
                for m, c in part:
                    if c == 0:
                        pe.wait_ge(landed[m], 16 * (pair + 1))
                        if pair and ng > 1:
                            if m:
                                wait_ready(pe, pair, m - 1)
                        elif m == 8:
                            wait_ready(pe, 0, 0)
                    last = projection(nc, k, bank[m], kinds[m][1], slots[m], c)
                    if c == 7:
                        last.then_inc(sem["projected"], 1)

            def scores(s):
                pair, h, t = s // 8, s % 8 // 4, s % 4
                if t == 0 and h == 0:
                    pe.wait_ge(sem["qk_ready"], 2 * ng * (pair + 1))
                wait(pe, sem["biased"], (s if ng > 1 else s - 1) * ng)
                half = slice(64 * h, 64 * h + 64)
                for g in range(ng):
                    k0 = span(g, t) * P
                    last = nc.tensor.matmul(k.ps[:, s_base[s % 2] + g, 0:(t + 1) * P - k0],
                                            qT[half, pair % 2, g, t * P:(t + 1) * P],
                                            kT[half, pair % 2, g, k0:(t + 1) * P], start=True, stop=True)
                last.then_inc(sem["s_done"], 1)

            for m in range(units if opened is None else 0):
                project(0, [(m, c) for c in range(8)], opening_bank)
            scores(0)
            scores(1)
            for s in range(steps):
                pair, h, t = s // 8, s % 8 // 4, s % 4
                if s + 2 < steps:
                    scores(s + 2)
                if pair + 1 < pairs:
                    project(pair + 1, before[s % 8], bank_of)
                if s == 0:
                    pe.wait_ge(sem["v_ready"], ng)
                pe.wait_ge(sem["normed"], s + 1)
                for b in range(width(s) // P):
                    last = nc.tensor.transpose(k.ps[:, t_base[s % 2] + b // 4, (b % 4) * P:(b % 4 + 1) * P],
                                               probs[:, s % 3, b * P:(b + 1) * P], k.ident[:])
                last.then_inc(sem["turned"], 1)
                if pair + 1 < pairs:
                    project(pair + 1, after[s % 8], bank_of)
                if s % 8 == 0:
                    pe.wait_ge(sem["v_ready"], ng * (pair + 1))
                    wait(pe, sem["y_out"], pair)
                pe.wait_ge(sem["probsT_ready"], s + 1)
                keys = [(g, kt) for g in range(ng) for kt in range(span(g, t), t + 1)]
                for b, (g, kt) in enumerate(keys):
                    last = nc.tensor.matmul(k.ps[64 * h:64 * h + 64, 6, t * P:(t + 1) * P],
                                            v[:, pair % 2, g, kt, 64 * h:64 * h + 64], probsT[:, s % 2, b * P:(b + 1) * P],
                                            start=(b == 0), stop=(b == len(keys) - 1))
                if s % 8 == 7:
                    last.then_inc(sem["pv_done"], 1)

        @block.scalar
        def _(act):
            def take(pair, m, bank):
                g, kind = kinds[m]
                act.wait_ge(sem["projected"], pair * units + m + 1)
                nc.scalar.activation((kT if kind else qT)[:, pair % 2, g, :], k.ps[:, bank[m], :], ACT.Copy,
                                     scale=1.0 if kind else SCALE).then_inc(sem["qk_ready"], 1)

            def exponential(s):
                act.wait_ge(sem["max_ready"], s + 1)
                a = probs[:, s % 3, 0:width(s)]
                nc.scalar.activation(a, a, ACT.Exp, bias=neg_max[:, s % 8:s % 8 + 1],
                                     accum_out=sums[:, s % 8:s % 8 + 1]).then_inc(sem["exp_done"], 1)

            for m in range(2 * ng):
                take(0, m, opening_bank)
            exponential(0)
            exponential(1)
            for s in range(steps):
                pair = s // 8
                if s + 2 < steps:
                    exponential(s + 2)
                act.wait_ge(sem["turned"], s + 1)
                for b in range(0, width(s), 512):
                    n = min(512, width(s) - b)
                    last = nc.scalar.activation(probsT[:, s % 2, b:b + n], k.ps[:, t_base[s % 2] + b // 512, 0:n], ACT.Copy)
                last.then_inc(sem["probsT_ready"], 1)
                if pair + 1 < pairs:
                    for m in finished[s % 8]:
                        if m < 2 * ng:
                            take(pair + 1, m, bank_of)
                if s % 8 == 7:
                    act.wait_ge(sem["pv_done"], pair + 1)
                    nc.scalar.activation(yT[:, pair, :], k.ps[:, 6, :], ACT.Copy).then_inc(sem["y_out"], 1)

        @block.vector
        def _(dve):
            def take(pair, m, bank):
                g, _ = kinds[m]
                dve.wait_ge(sem["projected"], pair * units + m + 1)
                nc.vector.tensor_copy(v[:, pair % 2, g, :, :], k.ps[:, bank[m], :].rearrange("p (t n) -> p t n", t=NT))\
                    .then_inc(sem["v_ready"], 1)

            def biased(s):
                pair, h, t = s // 8, s % 8 // 4, s % 4
                if pair:
                    dve.wait_ge(sem[f"bias_landed{h}"], 16 * ng * pair)
                else:
                    dve.wait_ge(first_bias.landed[h], 16 * ng)
                dve.wait_ge(sem["s_done"], s + 1)
                at = 0
                for g in range(ng):
                    n = (t + 1 - span(g, t)) * P
                    nc.vector.tensor_tensor_reduce(out=probs[:, s % 3, at:at + n], in0=k.ps[:, s_base[s % 2] + g, 0:n],
                                                   in1=bias[:, h, g, S - n:S], scale=1.0, scalar=NEG,
                                                   op0=ALU.add, op1=ALU.max,
                                                   accum_out=maxima[:, s % 8, g:g + 1]).then_inc(sem["biased"], 1)
                    at += n
                dve.wait_ge(sem["biased"], ng * (s + 1))
                nc.vector.tensor_reduce(out=neg_max[:, s % 8:s % 8 + 1], in_=maxima[:, s % 8, :], axis=AX.X, op=ALU.max,
                                        negate=True).then_inc(sem["max_ready"], 1)

            for m in range(2 * ng, units):
                take(0, m, opening_bank)
            def normalized(s):
                dve.wait_ge(sem["exp_done"], s + 1)
                one = sums[:, s % 8:s % 8 + 1]
                nc.vector.reciprocal(one, one).then_inc(sem["inverted"], 1)
                dve.wait_ge(sem["inverted"], s + 1)
                a = probs[:, s % 3, 0:width(s)]
                nc.vector.tensor_scalar(a, a, one, None, ALU.mult).then_inc(sem["normed"], 1)

            biased(0)
            biased(1)
            normalized(0)
            for s in range(steps):
                pair = s // 8
                if s + 2 < steps:
                    wait(dve, sem["turned"], s)
                    biased(s + 2)
                if s + 1 < steps:
                    normalized(s + 1)
                if pair + 1 < pairs:
                    for m in finished[s % 8]:
                        if m >= 2 * ng:
                            take(pair + 1, m, bank_of)



TAPS = 4
LRU_C = 8.0


def recurrence_loads(k, ctx, base_x, base_g, w_in, off_x, off_g):
    n = 4 * P
    wx, wg = k.slot(base_x, DC, n), k.slot(base_g, DC, n)
    loads = Loads(k, ctx, ("rg_wx", [(wx, rows_pc(w_in)[:, :, off_x:off_x + n])]),
                  ("rg_wg", [(wg, rows_pc(w_in)[:, :, off_g:off_g + n])]))
    loads.slots = wx, wg
    return loads


def recurrence(k, conv_w, conv_b, w_a, b_a, w_x, b_x, lam, yT, first, following, following_bias, opened):
    nc = k.nc
    C = 4
    wx, wg = first.slots
    with ExitStack() as ctx:
        def sb(name, shape):
            return ctx.enter_context(nc.sbuf_tensor("rg_" + name, shape, F32))

        diag_a, diag_x = sb("diag_a", [P, C, P]), sb("diag_x", [P, C, P])
        taps, bias = sb("taps", [P, TAPS, C]), sb("bias", [P, 4, C])
        sp_t = sb("sp_t", [P, 6, C])
        xp, xc = sb("xp", [P, C, S + TAPS - 1]), sb("xc", [P, C, S])
        mag, inp, tanh_t, recip, gate = (sb(n, [P, C, S]) for n in ("mag", "inp", "tanh_t", "recip", "gate"))
        names = ("small blocks zeroed x_done g_done xp_ready conv gates_done r_ready i_ready softplus lam_exp link "
                 "mag_ready tanh_done log_done recip_done a_ready ratio_ready root_done gelu_done")
        sem = dict(zip(names.split(), sems(k, ctx, " ".join("rg_" + n for n in names.split()))))
        sem["wx"], sem["wg"] = first.landed
        block = ctx.enter_context(nc.Block())

        @block.sync
        def _(sp):
            with nc.allow_non_contiguous_dma(reason="one word per channel"):
                for tap in range(TAPS):
                    sp.dma_start(taps[:, tap, :], conv_w[tap].rearrange("(c p) -> p c", p=P)).then_inc(sem["small"], 16)
                for n, b in enumerate((conv_b, b_a, b_x, lam)):
                    sp.dma_start(bias[:, n, :], b.rearrange("(c p) -> p c", p=P)).then_inc(sem["small"], 16)
            following_bias.issue(sp)
            following.issue(sp)
            sp.wait_ge(sem["zeroed"], 1)
            for dst, src in ((diag_a, w_a), (diag_x, w_x)):
                for h in (0, 1):
                    half = slice(64 * h, 64 * h + 64)
                    sp.dma_start(dst[half, :, half], src[h::2].rearrange("n d e -> d n e")).then_inc(sem["blocks"], 16)

        @block.tensor
        def _(pe):
            for name, wt, base, done in (("wx", wx, 0, "x_done"), ("wg", wg, C, "g_done")):
                pe.wait_ge(sem[name], 16)
                for c in range(C):
                    for d in range(DC):
                        last = nc.tensor.matmul(k.ps[:, base + c, :], wt[:, d, c * P:(c + 1) * P], k.hT[:, d, :],
                                                start=(d == 0), stop=(d == DC - 1))
                    last.then_inc(sem[done], 1)
            pe.wait_ge(sem["blocks"], 64)
            pe.wait_ge(sem["conv"], C * TAPS)
            pe.wait_ge(sem["gelu_done"], C)
            for c in range(C):
                nc.tensor.matmul(k.ps[:, c, :], diag_a[:, c, :], xc[:, c, :], start=True, stop=True)
                nc.tensor.matmul(k.ps[:, C + c, :], diag_x[:, c, :], xc[:, c, :], start=True,
                                 stop=True).then_inc(sem["gates_done"], 1)
            for m, (bank, ready, count) in enumerate(((2, "r_ready", 3), (5, "i_ready", 2), (7, "i_ready", 4))):
                pe.wait_ge(following.landed[m], 16)
                pe.wait_ge(sem[ready], count)
                for c in range(8):
                    last = projection(nc, k, bank, m, following.slots[m], c)
                last.then_inc(opened, 1)

        @block.scalar
        def _(act):
            A = nc.scalar.activation
            act.wait_ge(sem["small"], 16 * 8)
            act.wait_ge(sem["link"], 1)
            A(sp_t[:, 1, :], sp_t[:, 0, :], ACT.Exp, scale=-1.0).then_inc(sem["lam_exp"], 1)
            for c in range(C):
                act.wait_ge(sem["x_done"], c + 1)
                A(xp[:, c, TAPS - 1:], k.ps[:, c, :], ACT.Copy).then_inc(sem["xp_ready"], 1)
            for c in range(C):
                act.wait_ge(sem["g_done"], c + 1)
                A(gate[:, c, :], k.ps[:, C + c, :], ACT.Gelu_apprx_tanh).then_inc(sem["gelu_done"], 1)
            for c in range(C):
                act.wait_ge(sem["gates_done"], c + 1)
                A(mag[:, c, :], k.ps[:, c, :], ACT.Sigmoid, bias=bias[:, 1, c:c + 1]).then_inc(sem["r_ready"], 1)
                A(inp[:, c, :], k.ps[:, C + c, :], ACT.Sigmoid, bias=bias[:, 2, c:c + 1]).then_inc(sem["i_ready"], 1)
            for c in range(C):
                act.wait_ge(sem["mag_ready"], c + 1)
                A(tanh_t[:, c, :], mag[:, c, :], ACT.Tanh).then_inc(sem["tanh_done"], 1)
            act.preload_act_table_set("natural_log_exp_and_others")
            for c in range(C):
                act.wait_ge(sem["tanh_done"], c + 1)
                A(recip[:, c, :], tanh_t[:, c, :], ACT.Ln, bias=1.0).then_inc(sem["log_done"], 1)
            for c in range(C):
                act.wait_ge(sem["log_done"], c + 1)
                A(recip[:, c, :], recip[:, c, :], ACT.Exp, scale=-1.0).then_inc(sem["recip_done"], 1)
                A(mag[:, c, :], mag[:, c, :], ACT.Exp, scale=-1.0).then_inc(sem["a_ready"], 1)
            for c in range(C):
                act.wait_ge(sem["ratio_ready"], c + 1)
                A(recip[:, c, :], recip[:, c, :], ACT.Sqrt, scale=2.0).then_inc(sem["root_done"], 1)

        @block.vector
        def _(dve):
            V = nc.vector
            done = [0]

            def link(*instructions):
                for ins in instructions:
                    ins.then_inc(sem["link"], 1)
                    done[0] += 1
                dve.wait_ge(sem["link"], done[0])

            dve.wait_ge(sem["small"], 16 * 8)
            link(V.scalar_tensor_tensor(out=sp_t[:, 0, :], in0=bias[:, 3, :], scalar=-1.0, in1=bias[:, 3, :],
                                        op0=ALU.mult, op1=ALU.max))
            dve.wait_ge(sem["lam_exp"], 1)
            link(V.tensor_scalar(sp_t[:, 2, :], sp_t[:, 1, :], 2.0, None, ALU.add))
            link(V.reciprocal(sp_t[:, 2, :], sp_t[:, 2, :]))
            link(V.tensor_tensor(sp_t[:, 2, :], sp_t[:, 2, :], sp_t[:, 1, :], ALU.mult))
            link(V.tensor_tensor(sp_t[:, 3, :], sp_t[:, 2, :], sp_t[:, 2, :], ALU.mult),
                 V.memset(sp_t[:, 4, :], 1.0 / 17))
            for odd in (15, 13, 11, 9, 7, 5, 3, 1):
                link(V.tensor_tensor(sp_t[:, 4, :], sp_t[:, 4, :], sp_t[:, 3, :], ALU.mult))
                link(V.tensor_scalar(sp_t[:, 4, :], sp_t[:, 4, :], 1.0 / odd, None, ALU.add))
            link(V.tensor_tensor(sp_t[:, 4, :], sp_t[:, 4, :], sp_t[:, 2, :], ALU.mult),
                 V.tensor_scalar(sp_t[:, 5, :], bias[:, 3, :], -1.0, 0.0, ALU.mult, ALU.max))
            link(V.scalar_tensor_tensor(out=sp_t[:, 5, :], in0=sp_t[:, 4, :], scalar=2.0, in1=sp_t[:, 5, :],
                                        op0=ALU.mult, op1=ALU.add))
            link(V.tensor_scalar(sp_t[:, 5, :], sp_t[:, 5, :], LRU_C, None, ALU.mult))
            dve.sem_inc(sem["softplus"], 1)
            dve.wait_ge(sem["zeroed"], 1)
            for c in range(C):
                dve.wait_ge(sem["xp_ready"], c + 1)
                V.tensor_scalar(xc[:, c, :], xp[:, c, 0:S], taps[:, 0, c:c + 1], bias[:, 0, c:c + 1], ALU.mult,
                                ALU.add).then_inc(sem["conv"], 1)
                for tap in range(1, TAPS):
                    dve.wait_ge(sem["conv"], TAPS * c + tap)
                    V.scalar_tensor_tensor(out=xc[:, c, :], in0=xp[:, c, tap:tap + S], scalar=taps[:, tap, c:c + 1],
                                           in1=xc[:, c, :], op0=ALU.mult, op1=ALU.add).then_inc(sem["conv"], 1)
            for c in range(C):
                dve.wait_ge(sem["r_ready"], c + 1)
                V.tensor_scalar(mag[:, c, :], mag[:, c, :], sp_t[:, 5, c:c + 1], None, ALU.mult).then_inc(sem["mag_ready"], 1)
                dve.wait_ge(sem["i_ready"], c + 1)
                link(V.tensor_tensor(inp[:, c, :], inp[:, c, :], xc[:, c, :], ALU.mult))
            for c in range(C):
                dve.wait_ge(sem["recip_done"], c + 1)
                V.tensor_tensor(recip[:, c, :], recip[:, c, :], tanh_t[:, c, :], ALU.mult).then_inc(sem["ratio_ready"], 1)
            for c in range(C):
                dve.wait_ge(sem["root_done"], c + 1)
                dve.wait_ge(sem["a_ready"], c + 1)
                link(V.tensor_tensor(inp[:, c, :], inp[:, c, :], recip[:, c, :], ALU.mult))
                link(V.tensor_tensor_scan(xc[:, c, :], mag[:, c, :], inp[:, c, :], 0.0, ALU.mult, ALU.add))
                V.tensor_tensor(yT[:, c, :], xc[:, c, :], gate[:, c, :], ALU.mult)

        @block.gpsimd
        def _(pool):
            nc.gpsimd.memset(xp[:, :, 0:TAPS - 1], 0.0)
            nc.gpsimd.memset(diag_a[:], 0.0)
            nc.gpsimd.memset(diag_x[:], 0.0)
            pool.drain().then_inc(sem["zeroed"], 1)



FFN = -(-8 * D // (3 * 256)) * 256
FC = FFN // P


class FeedForward:

    def __init__(self, k, ctx, w_gu, w_down):
        def sb(name, shape, dt=F32):
            return ctx.enter_context(k.nc.sbuf_tensor("ff_" + name, shape, dt))

        self.w_gu = rows_pc(w_gu)
        self.hiddenT = sb("hiddenT", [P, FC, S])
        self.raw = sb("raw", [P, 2, 2, DC, P])
        self.first = Loads(k, ctx, *((f"ff_landed{u}{part}", [(self.raw[:, u, part], self.columns(u, part))])
                                     for u in (0, 1) for part in (0, 1)))
        self.down = RowBlocks(k, ctx, "fd", sb("raw_down", [P, RowBlocks.R, D]), w_down)

    def columns(self, chunk, part):
        return self.w_gu[:, :, bass.ds(chunk * P + part * FFN, P)]


def feed_forward(k, ff):
    nc = k.nc
    with ExitStack() as ctx:
        def sb(name, shape, dt=F32):
            return ctx.enter_context(nc.sbuf_tensor("ff_" + name, shape, dt))

        hT_masked = sb("hT_masked", [P, 2, S])
        hT_high, hT_low = sb("hT_high", [P, DC, S], F32R), sb("hT_low", [P, DC, S], F32R)
        masked_w = sb("masked_w", [P, 2, DC, P])
        high_w, low_w = sb("high_w", [P, 2, 2, DC, P], F32R), sb("low_w", [P, 2, 2, DC, P], F32R)
        silu = sb("silu", [P, 2, S])
        hT_mask_done, hT_high_ready, hT_low_ready, masked, high_ready, low_ready, multiplied, silu_done, hidden_ready = sems(
            k, ctx, "ff_hT_mask_done ff_hT_high_ready ff_hT_low_ready ff_masked ff_high_ready ff_low_ready ff_multiplied "
            "ff_silu_done ff_hidden_ready")
        landed = ff.first.landed
        block = ctx.enter_context(nc.Block())

        @block.sync
        def _(sp):
            ff.down.first.issue(sp)

            def step(it, u):
                if isinstance(it, int) and it == 0 and u < 2:
                    return
                for part in (0, 1):
                    wait(sp, low_ready, it * 8 + (2 * u - 3 + part))
                    sp.dma_start(ff.raw[:, u % 2, part], ff.columns(it * 4 + u, part)).then_inc(landed[u % 2 * 2 + part], 16)

            every(sp, FC, 4, step)

        @block.tensor
        def _(pe):
            def step(it, u):
                opening = isinstance(it, int) and it == 0 and u == 0
                wait(pe, hidden_ready, it * 4 + (u - 3))
                for part in (0, 1):
                    pe.wait_ge(high_ready, it * 8 + (2 * u + part + 1))
                    pe.wait_ge(low_ready, it * 8 + (2 * u + part + 1))
                    for c in range(DC):
                        if opening and part == 0:
                            pe.wait_ge(hT_high_ready, c + 1)
                            pe.wait_ge(hT_low_ready, c + 1)
                        last = split_product(nc, k.ps[:, 2 * u + part, :],
                                             (high_w[:, u % 2, part, c, :], low_w[:, u % 2, part, c, :]),
                                             (hT_high[:, c, :], hT_low[:, c, :]), c == 0, c == DC - 1)
                last.then_inc(multiplied, 1)

            every(pe, FC, 4, step)

        @block.scalar
        def _(act):
            def split_weights(it, u):
                for part in (0, 1):
                    act.wait_ge(masked, it * 8 + (2 * u + part + 1))
                    nc.scalar.activation(high_w[:, u % 2, part], masked_w[:, part], ACT.Copy).then_inc(high_ready, 1)

            def gate(it, u):
                act.wait_ge(multiplied, it * 4 + (u + 1))
                wait(act, hidden_ready, it * 4 + (u - 1))
                nc.scalar.activation(silu[:, u % 2, :], k.ps[:, 2 * u, :], ACT.Silu).then_inc(silu_done, 1)

            def step(it, u):
                split_weights(it, u)
                if isinstance(it, int) and it == 0 and u == 0:
                    for c in range(DC):
                        act.wait_ge(hT_mask_done, c + 1)
                        nc.scalar.activation(hT_high[:, c, :], hT_masked[:, c % 2, :], ACT.Copy).then_inc(hT_high_ready, 1)
                else:
                    gate(*((it, u - 1) if u else (it - 1, 3)))

            every(act, FC, 4, step)
            gate(*divmod(FC - 1, 4))

        @block.vector
        def _(dve):
            def split_weights(it, u):
                for part in (0, 1):
                    dve.wait_ge(landed[u % 2 * 2 + part], it * 32 + 16 * (u // 2 + 1))
                    wait(dve, high_ready, it * 8 + (2 * u - 1 + part))
                    wait(dve, multiplied, it * 4 + (u - 1))
                    mask_low_bits(nc, masked_w[:, part], ff.raw[:, u % 2, part]).then_inc(masked, 1)
                    dve.wait_ge(masked, it * 8 + (2 * u + part + 1))
                    nc.vector.tensor_tensor(low_w[:, u % 2, part], ff.raw[:, u % 2, part], masked_w[:, part],
                                            ALU.subtract).then_inc(low_ready, 1)

            def hidden(it, u):
                dve.wait_ge(silu_done, it * 4 + (u + 1))
                nc.vector.tensor_tensor(ff.hiddenT[:, bass.ds(it * 4 + u, 1), :].rearrange("p a n -> p (a n)"),
                                        silu[:, u % 2, :], k.ps[:, 2 * u + 1, :], ALU.mult).then_inc(hidden_ready, 1)

            def step(it, u):
                split_weights(it, u)
                if isinstance(it, int) and it == 0 and u == 0:
                    for c in range(DC):
                        wait(dve, hT_high_ready, c - 1)
                        mask_low_bits(nc, hT_masked[:, c % 2, :], k.hT[:, c, :]).then_inc(hT_mask_done, 1)
                        dve.wait_ge(hT_mask_done, c + 1)
                        nc.vector.tensor_tensor(hT_low[:, c, :], k.hT[:, c, :], hT_masked[:, c % 2, :],
                                                ALU.subtract).then_inc(hT_low_ready, 1)
                else:
                    hidden(*((it, u - 1) if u else (it - 1, 3)))

            every(dve, FC, 4, step)
            hidden(*divmod(FC - 1, 4))

    add_product(k, "fd", ff.hiddenT, FC, ff.down)


def final_norm(k, tag, gain, out=None, wait_for=None):
    nc = k.nc
    with ExitStack() as ctx:
        g = ctx.enter_context(nc.sbuf_tensor(tag + "_g", [P, D], F32))
        ss = ctx.enter_context(nc.sbuf_tensor(tag + "_ss", [P, NT], F32))
        landed, squares, mean_ready, root_ready, rstd_ready, normed, stored = sems(
            k, ctx, " ".join(tag + n for n in "_landed _squares _mean _root _rstd _normed _stored".split()))
        block = ctx.enter_context(nc.Block())

        @block.sync
        def _(sp):
            sp.dma_start(g[:], gain.partition_broadcast(P)).then_inc(landed, 16)
            if wait_for is not None:
                sp.wait_ge(wait_for, 16)
            if out is not None:
                for t in range(NT):
                    sp.wait_ge(normed, t + 1)
                    sp.dma_start(out[0, t * P:(t + 1) * P, :], k.x[:, t, :]).then_inc(stored, 16)
                sp.wait_ge(stored, 16 * NT)

        @block.scalar
        def _(act):
            for t in range(NT):
                nc.scalar.activation(k.ps[:, 2 * t:2 * t + 2, :], k.x[:, t, :].rearrange("p (a n) -> p a n", a=2),
                                     ACT.Square, accum_out=ss[:, t:t + 1]).then_inc(squares, 1)
            act.wait_ge(mean_ready, 1)
            nc.scalar.activation(ss[:], ss[:], ACT.Sqrt).then_inc(root_ready, 1)

        @block.vector
        def _(dve):
            dve.wait_ge(squares, NT)
            nc.vector.tensor_scalar(ss[:], ss[:], 1.0 / D, EPS, ALU.mult, ALU.add).then_inc(mean_ready, 1)
            dve.wait_ge(root_ready, 1)
            nc.vector.reciprocal(ss[:], ss[:]).then_inc(rstd_ready, 1)
            dve.wait_ge(rstd_ready, 1)
            dve.wait_ge(landed, 16)
            for t in range(NT):
                nc.vector.scalar_tensor_tensor(out=k.x[:, t, :], in0=k.x[:, t, :], scalar=ss[:, t:t + 1], in1=g[:],
                                               op0=ALU.mult, op1=ALU.mult).then_inc(normed, 1)


def second_layer(k, t, lines):
    nc = k.nc
    w_in = t["w_in_2"][0]
    width = WINDOW_HEADS * HD
    window = len(WINDOW_GROUPS) * width
    lru, block = 3 * window, 3 * window + 1024
    gates = block + 1536
    groups = tuple((g * width, window + g * width, 2 * window + g * width, g * WINDOW_HEADS)
                   for g in range(len(WINDOW_GROUPS)))
    with ExitStack() as mix:
        yaT = mix.enter_context(nc.sbuf_tensor("ya2_transposed", [P, 2, S], F32))
        ybT = mix.enter_context(nc.sbuf_tensor("yb2_transposed", [P, 4, S], F32))
        ycT = mix.enter_context(nc.sbuf_tensor("yc2_transposed", [P, 4, S], F32))
        branches = ((t["p_a_2"][0], yaT, 2), (t["p_b_2"][0], ybT, 4), (t["p_c_2"][0], ycT, 4))
        window_loads = qkv_loads(k, mix, "wa", 0, w_in, [off for g in groups for off in g[:3]])
        bias = mix.enter_context(nc.sbuf_tensor("biases", [P, 2, len(groups), S], F32))
        window_bias_loads = bias_loads(k, mix, "wa", bias, [g[3] for g in groups], lines)
        block_bias_loads = bias_loads(k, mix, "ba", bias, [BIAS_HEADS - BLOCK_HEADS], lines)
        extension = mix.enter_context(ExitStack())
        k.extend(extension, "lru")
        lru_loads = recurrence_loads(k, mix, 9 * DC * P, RING, w_in, lru, lru + 512)
        block_loads = qkv_loads(k, mix, "ba", 0, w_in, (block, block + 512, block + 1024))
        gate_cols = (gates, gates + D, gates + 2 * D)
        plan = MergePlan(k, mix, "mg2", 3 * DC * P, w_in, gate_cols, branches)
        out_rows = RowBlocks(k, mix, "op2", k.slot(9 * DC * P, RowBlocks.R, D), t["w_out_2"][0])

        norm_transpose(k, "mix2", t["g_mix_2"][0], (window_bias_loads, window_loads))
        biased_attention(k, "wa", w_in, groups, True, WINDOW_HEADS // 2, lines, bias, yaT, window_loads, window_bias_loads,
                         lru_loads)
        (opened,) = sems(k, mix, "ba_projected")
        recurrence(k, t["conv_w_2"][0], t["conv_b_2"][0], t["lru_wa_2"][0], t["lru_ba_2"][0],
                   t["lru_wx_2"][0], t["lru_bx_2"][0], t["lru_lam_2"][0], ybT, lru_loads,
                   block_loads, block_bias_loads, opened)
        extension.close()
        assert S // 256 - 1 <= 3
        biased_attention(k, "ba", w_in, ((block, block + 512, block + 1024, BIAS_HEADS - BLOCK_HEADS),), False,
                         BLOCK_HEADS // 2, lines, bias[:, :, 0:1, :], ycT, block_loads, block_bias_loads, plan.first, opened)
        mergedT = mix.enter_context(nc.sbuf_tensor("merged2_transposed", [P, DC, S], F32))
        merge(k, "mg2", plan, mergedT, out_rows.first)
        add_product(k, "op2", mergedT, DC, out_rows)
    k.ring_scope.close()
    with ExitStack() as ctx:
        ff = FeedForward(k, ctx, t["w_gu_2"][0], t["w_down_2"][0])
        norm_transpose(k, "ffn2", t["g_ffn_2"][0], (ff.first,))
        feed_forward(k, ff)



def first_layer(k, t, i, scratch):
    nc = k.nc
    xn_rows, y_rows = scratch
    w_in = t["w_in"][i]
    with ExitStack() as ctx:
        r = Routing(nc, ctx)
        route_loads = r.loads(k, ctx, t["w_router_group"][i], t["b_router_group"][i], t["w_router_expert"][i],
                              t["b_router_expert"][i], t["g_ffn"][i])
        with ExitStack() as mix:
            mergedT = mix.enter_context(nc.sbuf_tensor("merged_transposed", [P, DC, S], F32))
            yaT = mix.enter_context(nc.sbuf_tensor("ya_transposed", [P, 4, S], F32))
            ybT = mix.enter_context(nc.sbuf_tensor("yb_transposed", [P, 4, S], F32))
            gates, branches = (3072, 4096), ((t["w_br_a"][i], yaT, 4), (t["w_br_b"][i], ybT, 4))
            stick_loads = qkv_loads(k, mix, "sb", 0, w_in, (0, 512, 1024))
            diff_loads = qkv_loads(k, mix, "da", 3 * DC * P, w_in, (1536, 2048, 2560))
            plan = MergePlan(k, mix, "mg", 6 * DC * P, w_in, gates, branches)
            out_rows = RowBlocks(k, mix, "op", k.slot(0, RowBlocks.R, D), t["w_o"][i])
            norm_transpose(k, "mix", t["g_mix"][i], (stick_loads,))
            (opened,) = sems(k, mix, "da_projected")
            stick_breaking(k, w_in, 0, 512, 1024, yaT, stick_loads, diff_loads, opened)
            differential(k, w_in, 1536, 2048, 2560, [t[n][i] for n in ("lam_q1", "lam_k1", "lam_q2", "lam_k2")],
                         t["g_subln"][i], t["c_lam_init"][i], t["c_keep"][i], k.cosT, k.sinT, ybT, diff_loads, opened,
                         plan.first)
            merge(k, "mg", plan, mergedT, out_rows.first)
            add_product(k, "op", mergedT, DC, out_rows, (route_loads,))
        k.extend(ctx, "experts")
        embedding = Embedding(k, ctx, "pe", t["p"][i, 0], t["w_ple"][i], t["w_ple_gate"][i])
        with ExitStack() as moe:
            weights = (t["w_exp_gate"], t["w_exp_up"], t["w_exp_down"])
            expert_loads = Loads(k, moe, *((f"ex_{n}_landed{u}", expert_pairs(k, u, *(w[i, u] for w in weights))[part])
                                           for u in range(3) for n, part in (("gu", slice(0, 2)), ("down", slice(2, 3)))))
            norm_transpose(k, "ffn", t["g_ffn"][i], (expert_loads, embedding.loads), xn_rows)
            route(k, "rt", r, route_loads)
            experts(k, "ex", r, i, EXPERTS, False, xn_rows, y_rows, *weights, expert_loads)
            spilled = nc.values_load(r.spill_expert[0:1, SPILL:SPILL + 1], min_val=0, max_val=SPILL)
            with nc.If(spilled > 0):
                experts(k, "sp", r, i, SPILL, True, xn_rows, y_rows, *weights)
        clear_sems(k, keep=embedding.loads.landed + embedding.gate_loads.landed)
        embedded = ctx.enter_context(nc.sbuf_tensor("embedded", [P, NT, D], F32))
        combine_experts(k, "cb", r, y_rows, embedding, embedded, embedding.gate_loads)
        norm_transpose(k, "ple", t["g_ple"][i])
        embed_per_layer(k, "pe", embedding, embedded)


def program(nc, t, out):
    with ExitStack() as ctx:
        k = Core(nc, ctx)
        k.t = t
        lines = nc.dram_tensor("bias_lines", [BIAS_HEADS, P, LINE], F32).ap()
        k.bias_stored = ctx.enter_context(nc.semaphore("bias_lines_stored"))
        first_stack = ctx.enter_context(ExitStack())
        line = first_stack.enter_context(nc.sbuf_tensor("bias_line", [BIAS_HEADS, LINE], F32))
        start = load_start(k, t, ctx)
        k.cosT = first_stack.enter_context(nc.sbuf_tensor("cos_t", [P, S], F32))
        k.sinT = first_stack.enter_context(nc.sbuf_tensor("sin_t", [P, S], F32))
        rotary_tables(k, t, k.cosT, k.sinT, start)
        bias_lines(k, t["rel_bias_2"], lines, line, k.bias_stored)
        xn_rows = nc.dram_tensor("xn_rows", [S, D], F32)
        y_rows = nc.dram_tensor("y_rows", [2 * S, D], F32)
        clear_sems(k)
        with nc.Fori(0, DEPTH) as i:
            first_layer(k, t, i, (xn_rows.ap(), y_rows.ap()))
            clear_sems(k)
        first_stack.close()
        final_norm(k, "fn", t["g_final"], wait_for=k.bias_stored)
        second_layer(k, t, lines)
        final_norm(k, "fn2", t["g_final_2"], out)


def constants():
    f = np.float32
    r = np.arange(P)
    half = 8
    swap = np.zeros((P, P), f)
    freq = np.zeros((P, 1), f)
    inv = (f(500000.0) ** (-np.arange(0, 16, 2, dtype=f) / f(16))).astype(f)
    for head in (0, 64):
        for i in range(half):
            swap[head + half + i, head + i] = -1
            swap[head + i, head + half + i] = 1
            freq[head + i] = freq[head + half + i] = inv[i]
    lam_init = np.array([[0.8 - 0.6 * math.exp(-0.3 * i)] for i in range(DEPTH)], f)
    dist = S - 1 - np.arange(LINE)
    far = np.maximum(dist, 1).astype(f)
    exact = BUCKETS // 2
    large = exact + (np.log(far / exact).astype(f) / f(math.log(2048 / exact)) * f(BUCKETS - exact)).astype(np.int32)
    bucket = np.where(dist < exact, np.maximum(dist, 0), np.minimum(large, BUCKETS - 1))
    hot = (np.arange(BUCKETS)[:, None] == bucket[None, :]).astype(f)
    hidden = np.zeros((BIAS_HEADS, LINE), f)
    for g, (window, dilation) in enumerate(WINDOW_GROUPS):
        seen = (dist >= 0) & (dist <= window) & (dist % dilation == 0)
        hidden[g * WINDOW_HEADS:(g + 1) * WINDOW_HEADS] = np.where(seen, f(0), f(NEG))
    hidden[BIAS_HEADS - BLOCK_HEADS:] = np.where(dist >= 0, f(0), f(NEG))
    token = np.arange(S).reshape(NT, P)
    values = np.zeros((P, 8, 2), f)
    for tile in range(NT):
        for c in (0, 1):
            values[:, 2 * tile + c, 0] = token[tile] + 1
            values[:, 2 * tile + c, 1] = 2 * token[tile] + c + 1
    return {
        "c_iota": r.astype(f),
        "c_bucket_hot": hot,
        "c_hidden": hidden,
        "c_before": (r[:, None] < r[None, :]).astype(f),
        "c_slot_values": values,
        "c_ident": np.eye(P, dtype=f),
        "c_neg_tri": -(r[:, None] >= r[None, :]).astype(f),
        "c_chunk_bias": np.where((r[:, None] < 64) & (r[None, :] >= 64), f(NEG), f(0)),
        "c_rope_swap": swap,
        "c_rope_freq": freq,
        "c_lam_init": lam_init,
        "c_keep": (1.0 - lam_init.astype(np.float64)).astype(f),
        "c_strict_bias": np.where(r[:, None] < r[None, :], f(0), f(NEG)),
    }



_INPUTS = (
    "x p positions g_mix w_in lam_q1 lam_k1 lam_q2 lam_k2 g_subln w_br_a w_br_b w_o g_ffn w_router_group b_router_group "
    "w_router_expert b_router_expert w_exp_gate w_exp_up w_exp_down g_ple w_ple w_ple_gate g_final rel_bias_2 g_mix_2 "
    "w_in_2 conv_w_2 conv_b_2 lru_wa_2 lru_ba_2 lru_wx_2 lru_bx_2 lru_lam_2 p_a_2 p_b_2 p_c_2 w_out_2 g_ffn_2 w_gu_2 "
    "w_down_2 g_final_2").split()


def kernel(**inputs):
    import concourse.bacc as bacc
    from concourse.bass_utils import run_bass_kernel_spmd

    nc = bacc.Bacc("TRN2", target_bir_lowering=False, num_devices=1)
    arrays, t = {}, {}
    given = {name: np.ascontiguousarray(inputs[name]) for name in _INPUTS}
    for name, a in {**given, **constants()}.items():
        arrays["in_" + name] = a
        t[name] = nc.dram_tensor("in_" + name, a.shape, mybir.dt.from_np(a.dtype), kind="ExternalInput").ap()
    out = nc.dram_tensor("out_0", (1, S, D), F32, kind="ExternalOutput").ap()
    program(nc, t, out)
    r = run_bass_kernel_spmd(nc, [arrays], core_ids=[0])
    return r.results[0]["out_0"]
```
